# Optimizing a Trainium2 kernel written in Bass

```python
import math
import jax, jax.numpy as jnp
from jax import lax
import numpy as np

D_MODEL = 1024
BATCH = 1
SEQ = 256
DEPTH = 1

HEAD_DIM = 64
N_HEADS = D_MODEL // HEAD_DIM
N_HEADS_SB = N_HEADS // 2
N_HEADS_DIL = N_HEADS - N_HEADS_SB
D_SB = N_HEADS_SB * HEAD_DIM
D_DIL = N_HEADS_DIL * HEAD_DIM
DIL_PATTERNS = ((128, 1), (512, 4), (2048, 16))
BLOCK = 128
N_BUCKETS = 32
MAX_DISTANCE = 2048
N_EXPERTS = 16
N_GROUPS = 4
EXPERTS_PER_GROUP = N_EXPERTS // N_GROUPS
TOP_K = 2
D_FF_EXPERT = 1024
ALPHA = (2.0 * DEPTH) ** 0.25
BETA = (8.0 * DEPTH) ** -0.25
LN_EPS = 1e-5
NEG_INF = -1e30


def layer_norm(x, g, b):
    xf = x.astype(jnp.float32)
    mu = xf.mean(-1, keepdims=True)
    var = jnp.square(xf - mu).mean(-1, keepdims=True)
    return ((xf - mu) * lax.rsqrt(var + LN_EPS) * g.astype(jnp.float32) + b.astype(jnp.float32)).astype(x.dtype)

def head_rms_merge(o, g):
    b, h, s, dh = o.shape
    of = o.astype(jnp.float32)
    of = of * lax.rsqrt(jnp.mean(jnp.square(of), -1, keepdims=True) + 1e-6)
    of = of.transpose(0, 2, 1, 3).reshape(b, s, h * dh)
    return (of * g.astype(jnp.float32)).astype(o.dtype)

def t5_bucket(dist):
    max_exact = N_BUCKETS // 2
    d = jnp.maximum(dist, 0)
    large = max_exact + (jnp.log(jnp.maximum(d, 1).astype(jnp.float32) / max_exact)
                         / math.log(MAX_DISTANCE / max_exact) * (N_BUCKETS - max_exact)).astype(jnp.int32)
    large = jnp.minimum(large, N_BUCKETS - 1)
    return jnp.where(d < max_exact, d, large)

def stick_breaking_attention(q, k, v):
    b, h, s, dh = q.shape
    nb = s // BLOCK
    scale = dh ** -0.5
    qb = q.reshape(b, h, nb, BLOCK, dh).transpose(2, 0, 1, 3, 4)
    kpos = jnp.arange(s)

    def one_block(args):
        qblk, n = args
        z = jnp.einsum('bhqd,bhkd->bhqk', qblk, k).astype(jnp.float32) * scale
        qpos = n * BLOCK + jnp.arange(BLOCK)
        causal = kpos[None, :] < qpos[:, None]
        log_beta = jax.nn.log_sigmoid(z)
        log_1m = jnp.where(causal, jax.nn.log_sigmoid(-z), 0.0)
        between = lax.cumsum(log_1m, axis=3, reverse=True) - log_1m
        a = jnp.where(causal, jnp.exp(log_beta + between), 0.0)
        return jnp.einsum('bhqk,bhkd->bhqd', a.astype(v.dtype), v)

    out = lax.map(one_block, (qb, jnp.arange(nb)))
    return out.transpose(1, 2, 0, 3, 4).reshape(b, h, s, dh)

def dilated_branch(q, k, v, rel_bias, window, dilation):
    b, h, s, dh = q.shape
    span = window // dilation
    n_cls = s // dilation
    nb = -(-n_cls // BLOCK)
    pad = nb * BLOCK - n_cls

    def to_classes(t):
        t = t.reshape(b, h, n_cls, dilation, dh).transpose(0, 1, 3, 2, 4)
        t = jnp.pad(t, ((0, 0), (0, 0), (0, 0), (0, pad), (0, 0)))
        return t.reshape(b, h, dilation, nb, BLOCK, dh)

    def with_prev(t):
        prev = jnp.pad(t, ((0, 0), (0, 0), (0, 0), (1, 0), (0, 0), (0, 0)))[:, :, :, :nb]
        return jnp.concatenate([prev, t], axis=4)

    qc = to_classes(q)
    kk = with_prev(to_classes(k))
    vv = with_prev(to_classes(v))
    logits = jnp.einsum('bhrnqd,bhrnkd->bhrnqk', qc, kk).astype(jnp.float32) * dh ** -0.5

    qi = jnp.arange(BLOCK)[:, None]
    kj = jnp.arange(2 * BLOCK)[None, :]
    steps = qi + BLOCK - kj
    bias = rel_bias[t5_bucket(jnp.maximum(steps, 0) * dilation)].astype(jnp.float32)
    bias = bias.transpose(2, 0, 1)
    key_cls = (jnp.arange(nb)[:, None, None] - 1) * BLOCK + kj[None]
    valid = (steps >= 0) & (steps <= span) & (key_cls >= 0)
    logits = jnp.where(valid, logits + bias[None, :, None, None], NEG_INF)

    m = logits.max(-1, keepdims=True)
    p = jnp.exp(logits - m)
    denom = p.sum(-1, keepdims=True)
    o = jnp.einsum('bhrnqk,bhrnkd->bhrnqd', p.astype(vv.dtype), vv).astype(jnp.float32) / denom
    lse = (m + jnp.log(denom))[..., 0]

    def from_classes(t):
        t = t.reshape((b, h, dilation, nb * BLOCK) + t.shape[5:])[:, :, :, :n_cls]
        t = jnp.moveaxis(t, 2, 3)
        return t.reshape((b, h, s) + t.shape[4:])

    return from_classes(o), from_classes(lse)

def dilated_attention(q, k, v, rel_bias):
    outs, lses = [], []
    for window, dilation in DIL_PATTERNS:
        o, l = dilated_branch(q, k, v, rel_bias, window, dilation)
        outs.append(o)
        lses.append(l)
    w = jax.nn.softmax(jnp.stack(lses, 0), axis=0)
    return jnp.einsum('gbhs,gbhsd->bhsd', w, jnp.stack(outs, 0)).astype(q.dtype)

def token_mixer(x, w_in, g_sb, g_dil, w_out, rel_bias):
    b, s, _ = x.shape
    proj = jnp.einsum('bsd,de->bse', x, w_in)
    q_sb, k_sb, v_sb, q_dl, k_dl, v_dl = jnp.split(
        proj, [D_SB, 2 * D_SB, 3 * D_SB, 3 * D_SB + D_DIL, 3 * D_SB + 2 * D_DIL], axis=-1)
    to_heads = lambda t: t.reshape(b, s, -1, HEAD_DIM).transpose(0, 2, 1, 3)
    o_sb = stick_breaking_attention(to_heads(q_sb), to_heads(k_sb), to_heads(v_sb))
    o_dl = dilated_attention(to_heads(q_dl), to_heads(k_dl), to_heads(v_dl), rel_bias)
    y = jnp.concatenate([head_rms_merge(o_sb, g_sb), head_rms_merge(o_dl, g_dil)], axis=-1)
    return jnp.einsum('bse,ed->bsd', y, w_out)

def grouped_moe(x, w_router, b_router, w_gate, w_up, w_down):
    b, s, d = x.shape
    t = x.reshape(b * s, d)
    logits = (t @ w_router).astype(jnp.float32) + b_router.astype(jnp.float32)
    probs = jax.nn.softmax(logits, axis=-1)
    pg = probs.reshape(-1, N_GROUPS, EXPERTS_PER_GROUP)
    vals, idx = lax.top_k(pg, TOP_K)
    g_sel = jnp.argmax(vals.sum(-1), axis=-1)
    vals_sel = jnp.take_along_axis(vals, g_sel[:, None, None], axis=1)[:, 0]
    idx_sel = jnp.take_along_axis(idx, g_sel[:, None, None], axis=1)[:, 0]
    expert_ids = g_sel[:, None] * EXPERTS_PER_GROUP + idx_sel
    gates = vals_sel / vals_sel.sum(-1, keepdims=True)
    gate_dense = (jax.nn.one_hot(expert_ids, N_EXPERTS, dtype=jnp.float32) * gates[..., None]).sum(1)
    y = jnp.zeros_like(t)
    for e in range(N_EXPERTS):
        h = jax.nn.silu(t @ w_gate[e]) * (t @ w_up[e])
        y = y + gate_dense[:, e:e + 1].astype(t.dtype) * (h @ w_down[e])
    return y.reshape(b, s, d)

def first_inputs(seed: int = 0) -> dict:
    key = jax.random.key(seed)
    ks = jax.random.split(key, 20)
    f32 = jnp.float32
    d = D_MODEL
    s_in = d ** -0.5
    nrm = lambda k, shape: jax.random.normal(k, shape, f32)
    x = nrm(ks[0], (BATCH, SEQ, d))

    def qkv_cols(k, width):
        kq, kk, kv = jax.random.split(k, 3)
        return [nrm(kq, (DEPTH, d, width)) * s_in,
                nrm(kk, (DEPTH, d, width)) * s_in,
                nrm(kv, (DEPTH, d, width)) * (s_in * BETA)]

    w_in = jnp.concatenate(qkv_cols(ks[1], D_SB) + qkv_cols(ks[2], D_DIL), axis=-1)
    g_sb = 1.0 + 0.05 * nrm(ks[3], (DEPTH, D_SB))
    g_dil = 1.0 + 0.05 * nrm(ks[4], (DEPTH, D_DIL))
    w_out = nrm(ks[5], (DEPTH, d, d)) * (s_in * BETA)
    ln1_g = 1.0 + 0.05 * nrm(ks[6], (DEPTH, d))
    ln1_b = 0.02 * nrm(ks[7], (DEPTH, d))
    ln2_g = 1.0 + 0.05 * nrm(ks[8], (DEPTH, d))
    ln2_b = 0.02 * nrm(ks[9], (DEPTH, d))
    rel_bias = 0.5 * nrm(ks[10], (N_BUCKETS, N_HEADS_DIL))
    w_router = nrm(ks[11], (d, N_EXPERTS)) * s_in
    b_router = 0.01 * nrm(ks[12], (N_EXPERTS,))
    w_gate = nrm(ks[13], (DEPTH, N_EXPERTS, d, D_FF_EXPERT)) * s_in
    w_up = nrm(ks[14], (DEPTH, N_EXPERTS, d, D_FF_EXPERT)) * (s_in * BETA)
    w_down = nrm(ks[15], (DEPTH, N_EXPERTS, D_FF_EXPERT, d)) * (D_FF_EXPERT ** -0.5 * BETA)
    return {"x": x, "w_in": w_in, "g_sb": g_sb, "g_dil": g_dil, "w_out": w_out,
            "ln1_g": ln1_g, "ln1_b": ln1_b, "ln2_g": ln2_g, "ln2_b": ln2_b,
            "rel_bias": rel_bias, "w_router": w_router, "b_router": b_router,
            "w_gate": w_gate, "w_up": w_up, "w_down": w_down}

def first_block(x, w_in, g_sb, g_dil, w_out, ln1_g, ln1_b, ln2_g, ln2_b,
              rel_bias, w_router, b_router, w_gate, w_up, w_down):
    for l in range(DEPTH):
        h = token_mixer(x, w_in[l], g_sb[l], g_dil[l], w_out[l], rel_bias)
        x = layer_norm(ALPHA * x + h, ln1_g[l], ln1_b[l])
        h = grouped_moe(x, w_router, b_router, w_gate[l], w_up[l], w_down[l])
        x = layer_norm(ALPHA * x + h, ln2_g[l], ln2_b[l])
    return x


CTX_LEN = 256
GRID_W = 64
N_RET_HEADS = 4
RET_QK_DIM = 256
RET_V_DIM = 512
RET_CHUNK = 128
N_MLA_HEADS = 8
MLA_Q_RANK = 384
MLA_KV_RANK = 256
MLA_QK_NOPE = 128
MLA_QK_ROPE = 64
MLA_V_DIM = 128
Q_BLOCK = 128
N_EXPERTS_2 = 32
TOP_K_2 = 4
D_FF_EXPERT_2 = D_MODEL
SWIGLU_LIMIT = 7.0
SWIGLU_ALPHA = 1.702
MOE_BLOCK = 128
ROPE_BASE = 10000.0
EPS = 1e-6
IN_COLS = (2 * N_RET_HEADS * RET_QK_DIM + 2 * N_RET_HEADS * RET_V_DIM
           + MLA_Q_RANK + MLA_KV_RANK + MLA_QK_ROPE + 2 * D_MODEL)


def rms_norm(t, g):
    tf = t.astype(jnp.float32)
    n = tf * lax.rsqrt(jnp.mean(tf * tf, axis=-1, keepdims=True) + EPS)
    return n.astype(t.dtype) * g

def head_rms(t):
    tf = t.astype(jnp.float32)
    return (tf * lax.rsqrt(jnp.mean(tf * tf, axis=-1, keepdims=True) + EPS)).astype(t.dtype)

def ada_mod(cvec, w, b):
    m = jax.nn.silu(cvec) @ w + b
    return jnp.split(m[:, None, :], 6, axis=-1)

def modulate(t, shift, scale):
    return t * (1.0 + scale) + shift

def rope_1d(t, pos):
    half = t.shape[-1] // 2
    freqs = ROPE_BASE ** (-jnp.arange(half, dtype=jnp.float32) / half)
    ang = pos.astype(jnp.float32)[:, None] * freqs[None, :]
    cos = jnp.cos(ang)[None, :, None, :].astype(t.dtype)
    sin = jnp.sin(ang)[None, :, None, :].astype(t.dtype)
    t1, t2 = t[..., :half], t[..., half:]
    return jnp.concatenate([t1 * cos - t2 * sin, t1 * sin + t2 * cos], axis=-1)

def rope_2d(t, rows, cols):
    half = t.shape[-1] // 2
    return jnp.concatenate([rope_1d(t[..., :half], rows), rope_1d(t[..., half:], cols)], axis=-1)

def split_proj(z):
    sizes = (N_RET_HEADS * RET_QK_DIM, N_RET_HEADS * RET_QK_DIM, N_RET_HEADS * RET_V_DIM,
             N_RET_HEADS * RET_V_DIM, MLA_Q_RANK, MLA_KV_RANK, MLA_QK_ROPE, D_MODEL, D_MODEL)
    idx, acc = [], 0
    for s in sizes[:-1]:
        acc += s
        idx.append(acc)
    return jnp.split(z, idx, axis=-1)

def retention_qkv(rq, rk, rv, rope_fn):
    B, L, _ = rq.shape
    q = rq.reshape(B, L, N_RET_HEADS, RET_QK_DIM)
    k = rk.reshape(B, L, N_RET_HEADS, RET_QK_DIM)
    v = rv.reshape(B, L, N_RET_HEADS, RET_V_DIM)
    if rope_fn is not None:
        q, k = rope_fn(q), rope_fn(k)
    return q, k * (RET_QK_DIM ** -0.5), v

def retention_state(k, v, lg):
    L = k.shape[1]
    w = jnp.exp(lg[:, None] * (L - 1 - jnp.arange(L, dtype=jnp.float32))[None, :]).astype(v.dtype)
    return jnp.einsum('blhd,blhe,hl->bhde', k, v, w)

def retention_chunked(q, k, v, lg, init_state, include_diag):
    B, L, H, dk = q.shape
    dv = v.shape[-1]
    nc = L // RET_CHUNK
    idx = jnp.arange(RET_CHUNK, dtype=jnp.float32)
    diff = idx[:, None] - idx[None, :]
    mask = (diff >= 0) if include_diag else (diff > 0)
    intra = jnp.where(mask[None], jnp.exp(lg[:, None, None] * jnp.maximum(diff, 0.0)[None]), 0.0).astype(v.dtype)
    q_dec = jnp.exp(lg[:, None] * (idx + 1.0)[None, :]).astype(v.dtype)
    k_dec = jnp.exp(lg[:, None] * (RET_CHUNK - 1.0 - idx)[None, :]).astype(v.dtype)
    chunk_dec = jnp.exp(lg * RET_CHUNK).astype(v.dtype)

    def to_chunks(t):
        return t.reshape(B, nc, RET_CHUNK, H, t.shape[-1]).transpose(1, 0, 3, 2, 4)

    def step(state, blk):
        qc, kc, vc = blk
        s = jnp.einsum('bhid,bhjd->bhij', qc, kc) * intra[None]
        o = (jnp.einsum('bhij,bhje->bhie', s, vc)
             + jnp.einsum('bhid,bhde->bhie', qc * q_dec[None, :, :, None], state))
        state = (state * chunk_dec[None, :, None, None]
                 + jnp.einsum('bhjd,bhje->bhde', kc * k_dec[None, :, :, None], vc))
        return state, o

    _, o = lax.scan(step, init_state, (to_chunks(q), to_chunks(k), to_chunks(v)))
    return o.transpose(1, 0, 3, 2, 4).reshape(B, L, H, dv)

def bidir_retention(q, k, v, lg_f, lg_b, s_f, s_b):
    fwd = retention_chunked(q, k, v, lg_f, s_f, True)
    bwd = retention_chunked(jnp.flip(q, 1), jnp.flip(k, 1), jnp.flip(v, 1), lg_b, s_b, False)
    return fwd + jnp.flip(bwd, 1)

def mla_qkv(cq, ckv, kr, q_norm_g, w_uq, kv_norm_g, w_ukv, rope_fn):
    B, L, _ = cq.shape
    q = (rms_norm(cq, q_norm_g) @ w_uq).reshape(B, L, N_MLA_HEADS, MLA_QK_NOPE + MLA_QK_ROPE)
    q_nope, q_rope = q[..., :MLA_QK_NOPE], q[..., MLA_QK_NOPE:]
    kv = (rms_norm(ckv, kv_norm_g) @ w_ukv).reshape(B, L, N_MLA_HEADS, MLA_QK_NOPE + MLA_V_DIM)
    k_nope, v = kv[..., :MLA_QK_NOPE], kv[..., MLA_QK_NOPE:]
    k_rope = kr[:, :, None, :]
    if rope_fn is not None:
        q_rope, k_rope = rope_fn(q_rope), rope_fn(k_rope)
    return q_nope, q_rope, k_nope, k_rope[:, :, 0, :], v

def mla_attention(q_nope, q_rope, k_nope, k_rope, v):
    B, Lq, H, _ = q_nope.shape
    nb = Lq // Q_BLOCK
    scale = (MLA_QK_NOPE + MLA_QK_ROPE) ** -0.5

    def blocks(t):
        return t.reshape(B, nb, Q_BLOCK, H, t.shape[-1]).swapaxes(0, 1)

    def one_block(qb):
        qn, qr = qb
        s = (jnp.einsum('bqhd,bkhd->bhqk', qn, k_nope)
             + jnp.einsum('bqhd,bkd->bhqk', qr, k_rope)) * scale
        p = jax.nn.softmax(s.astype(jnp.float32), axis=-1).astype(v.dtype)
        return jnp.einsum('bhqk,bkhd->bqhd', p, v)

    o = lax.map(one_block, (blocks(q_nope), blocks(q_rope)))
    return o.swapaxes(0, 1).reshape(B, Lq, H, MLA_V_DIM)

def merge_branches(ret_o, ret_gate, att_o, g_ret, g_mla, w_branch_ret, w_branch_mla, w_out):
    B, L = ret_o.shape[:2]
    r = head_rms(ret_o).reshape(B, L, N_RET_HEADS * RET_V_DIM) * jax.nn.silu(ret_gate)
    m = att_o.reshape(B, L, N_MLA_HEADS * MLA_V_DIM)
    merged = jax.nn.sigmoid(g_ret) * (r @ w_branch_ret) + jax.nn.sigmoid(g_mla) * (m @ w_branch_mla)
    return merged @ w_out

def token_mixers(h_lat, h_ctx, rope_fn, need_ctx, w_in, ret_decay_fwd, ret_decay_bwd, mla_q_norm_g,
                 mla_w_uq, mla_kv_norm_g, mla_w_ukv, w_branch_ret, w_branch_mla, w_out):
    zl = split_proj(h_lat @ w_in)
    zc = split_proj(h_ctx @ w_in)
    lg_f = jax.nn.log_sigmoid(ret_decay_fwd.astype(jnp.float32))
    lg_b = jax.nn.log_sigmoid(ret_decay_bwd.astype(jnp.float32))
    ql, kl, vl = retention_qkv(zl[0], zl[1], zl[2], rope_fn)
    qc, kc, vc = retention_qkv(zc[0], zc[1], zc[2], None)
    s_f = retention_state(kc, vc, lg_f)
    s_b = retention_state(jnp.flip(kc, 1), jnp.flip(vc, 1), lg_b)
    ret_lat = bidir_retention(ql, kl, vl, lg_f, lg_b, s_f, s_b)
    ml = mla_qkv(zl[4], zl[5], zl[6], mla_q_norm_g, mla_w_uq, mla_kv_norm_g, mla_w_ukv, rope_fn)
    mc = mla_qkv(zc[4], zc[5], zc[6], mla_q_norm_g, mla_w_uq, mla_kv_norm_g, mla_w_ukv, None)
    att_lat = mla_attention(ml[0], ml[1], jnp.concatenate([mc[2], ml[2]], axis=1),
                            jnp.concatenate([mc[3], ml[3]], axis=1), jnp.concatenate([mc[4], ml[4]], axis=1))
    y_lat = merge_branches(ret_lat, zl[3], att_lat, zl[7], zl[8], w_branch_ret, w_branch_mla, w_out)
    y_ctx = None
    if need_ctx:
        zeros = jnp.zeros_like(s_f)
        ret_ctx = bidir_retention(qc, kc, vc, lg_f, lg_b, zeros, zeros)
        att_ctx = mla_attention(mc[0], mc[1], mc[2], mc[3], mc[4])
        y_ctx = merge_branches(ret_ctx, zc[3], att_ctx, zc[7], zc[8], w_branch_ret, w_branch_mla, w_out)
    return y_lat, y_ctx

def moe(h, router_w, router_b, w_gu, b_gu, w_down, b_down):
    B, L, D = h.shape
    tok = h.reshape(-1, D)
    n_tok = tok.shape[0]
    logits = tok @ router_w + router_b
    top_val, top_idx = lax.top_k(logits, TOP_K_2)
    gates = jax.nn.softmax(top_val.astype(jnp.float32), axis=-1)
    nk = n_tok * TOP_K_2
    flat_e = top_idx.reshape(-1)
    flat_tok = jnp.arange(nk, dtype=jnp.int32) // TOP_K_2
    order = jnp.argsort(flat_e)
    sorted_e = flat_e[order]
    sorted_tok = flat_tok[order]
    sorted_gate = gates.reshape(-1)[order]
    counts = jnp.zeros((N_EXPERTS_2,), jnp.int32).at[flat_e].add(1)
    padded = (counts + MOE_BLOCK - 1) // MOE_BLOCK * MOE_BLOCK
    start = jnp.cumsum(counts) - counts
    pad_end = jnp.cumsum(padded)
    pad_start = pad_end - padded
    dest = pad_start[sorted_e] + (jnp.arange(nk, dtype=jnp.int32) - start[sorted_e])
    n_rows = nk + N_EXPERTS_2 * MOE_BLOCK
    n_blocks = n_rows // MOE_BLOCK
    xs = jnp.zeros((n_rows, D), tok.dtype).at[dest].set(tok[sorted_tok])
    block_e = jnp.minimum(jnp.searchsorted(pad_end, jnp.arange(n_blocks, dtype=jnp.int32) * MOE_BLOCK,
                                           side='right'), N_EXPERTS_2 - 1)

    def expert_block(args):
        xb, e = args
        gu = xb @ w_gu[e] + b_gu[e]
        gate, up = gu[:, :D_FF_EXPERT_2], gu[:, D_FF_EXPERT_2:]
        gate = jnp.minimum(gate, SWIGLU_LIMIT)
        up = jnp.clip(up, -SWIGLU_LIMIT, SWIGLU_LIMIT)
        glu = gate * jax.nn.sigmoid(SWIGLU_ALPHA * gate)
        return ((up + 1.0) * glu) @ w_down[e] + b_down[e]

    ys = lax.map(expert_block, (xs.reshape(n_blocks, MOE_BLOCK, D), block_e)).reshape(n_rows, D)
    out = jnp.zeros_like(tok).at[sorted_tok].add(ys[dest] * sorted_gate[:, None].astype(ys.dtype))
    return out.reshape(B, L, D)

def second_inputs(seed: int = 0) -> dict:
    key = jax.random.key(seed)
    ks = jax.random.split(key, 25)
    f32 = jnp.float32

    def nrm(k, shape, scale):
        return jax.random.normal(k, shape, f32) * scale

    ret_base = jnp.log(jnp.exp2(5.0 + jnp.arange(N_RET_HEADS, dtype=f32)) - 1.0)
    ret_v_w = N_RET_HEADS * RET_V_DIM
    mla_v_w = N_MLA_HEADS * MLA_V_DIM
    return {
        'x': nrm(ks[0], (BATCH, SEQ, D_MODEL), 1.0),
        'c': nrm(ks[1], (BATCH, D_MODEL), 1.0),
        'ctx': nrm(ks[2], (BATCH, CTX_LEN, D_MODEL), 1.0),
        'c_ctx': nrm(ks[3], (D_MODEL,), 1.0),
        'norm1_g': 1.0 + nrm(ks[4], (DEPTH, D_MODEL), 0.02),
        'norm2_g': 1.0 + nrm(ks[5], (DEPTH, D_MODEL), 0.02),
        'ada_w': nrm(ks[6], (DEPTH, D_MODEL, 6 * D_MODEL), 0.5 * D_MODEL ** -0.5),
        'ada_b': nrm(ks[7], (DEPTH, 6 * D_MODEL), 0.01),
        'w_in': nrm(ks[8], (DEPTH, D_MODEL, IN_COLS), D_MODEL ** -0.5),
        'ret_decay_fwd': ret_base[None, :] + nrm(ks[9], (DEPTH, N_RET_HEADS), 0.1),
        'ret_decay_bwd': ret_base[None, :] + nrm(ks[10], (DEPTH, N_RET_HEADS), 0.1),
        'mla_q_norm_g': 1.0 + nrm(ks[11], (DEPTH, MLA_Q_RANK), 0.02),
        'mla_w_uq': nrm(ks[12], (DEPTH, MLA_Q_RANK, N_MLA_HEADS * (MLA_QK_NOPE + MLA_QK_ROPE)), MLA_Q_RANK ** -0.5),
        'mla_kv_norm_g': 1.0 + nrm(ks[13], (DEPTH, MLA_KV_RANK), 0.02),
        'mla_w_ukv': nrm(ks[14], (DEPTH, MLA_KV_RANK, N_MLA_HEADS * (MLA_QK_NOPE + MLA_V_DIM)), MLA_KV_RANK ** -0.5),
        'w_branch_ret': nrm(ks[15], (DEPTH, ret_v_w, D_MODEL), ret_v_w ** -0.5),
        'w_branch_mla': nrm(ks[16], (DEPTH, mla_v_w, D_MODEL), mla_v_w ** -0.5),
        'w_out': nrm(ks[17], (DEPTH, D_MODEL, D_MODEL), D_MODEL ** -0.5),
        'router_w': nrm(ks[18], (DEPTH, D_MODEL, N_EXPERTS_2), D_MODEL ** -0.5),
        'router_b': nrm(ks[19], (DEPTH, N_EXPERTS_2), 0.01),
        'exp_w_gu': nrm(ks[20], (DEPTH, N_EXPERTS_2, D_MODEL, 2 * D_FF_EXPERT_2), D_MODEL ** -0.5),
        'exp_b_gu': nrm(ks[21], (DEPTH, N_EXPERTS_2, 2 * D_FF_EXPERT_2), 0.01),
        'exp_w_down': nrm(ks[22], (DEPTH, N_EXPERTS_2, D_FF_EXPERT_2, D_MODEL), D_FF_EXPERT_2 ** -0.5),
        'exp_b_down': nrm(ks[23], (DEPTH, N_EXPERTS_2, D_MODEL), 0.01),
        'final_norm_g': 1.0 + nrm(ks[24], (D_MODEL,), 0.02),
    }

def second_block(x, c, ctx, c_ctx, norm1_g, norm2_g, ada_w, ada_b, w_in, ret_decay_fwd, ret_decay_bwd,
              mla_q_norm_g, mla_w_uq, mla_kv_norm_g, mla_w_ukv, w_branch_ret, w_branch_mla, w_out,
              router_w, router_b, exp_w_gu, exp_b_gu, exp_w_down, exp_b_down, final_norm_g):
    L = x.shape[1]
    n_grid_rows = L // GRID_W
    rows = jnp.repeat(jnp.arange(n_grid_rows, dtype=jnp.int32), GRID_W)
    cols = jnp.tile(jnp.arange(GRID_W, dtype=jnp.int32), n_grid_rows)
    rope_fn = lambda t: rope_2d(t, rows, cols)
    for layer in range(DEPTH):
        need_ctx = layer < DEPTH - 1
        m_lat = ada_mod(c, ada_w[layer], ada_b[layer])
        m_ctx = ada_mod(c_ctx[None, :], ada_w[layer], ada_b[layer])
        h_lat = modulate(rms_norm(x, norm1_g[layer]), m_lat[0], m_lat[1])
        h_ctx = modulate(rms_norm(ctx, norm1_g[layer]), m_ctx[0], m_ctx[1])
        y_lat, y_ctx = token_mixers(h_lat, h_ctx, rope_fn, need_ctx, w_in[layer], ret_decay_fwd[layer],
                                    ret_decay_bwd[layer], mla_q_norm_g[layer], mla_w_uq[layer],
                                    mla_kv_norm_g[layer], mla_w_ukv[layer], w_branch_ret[layer],
                                    w_branch_mla[layer], w_out[layer])
        x = x + m_lat[2] * y_lat
        h2 = modulate(rms_norm(x, norm2_g[layer]), m_lat[3], m_lat[4])
        x = x + m_lat[5] * moe(h2, router_w[layer], router_b[layer], exp_w_gu[layer], exp_b_gu[layer],
                               exp_w_down[layer], exp_b_down[layer])
        if need_ctx:
            ctx = ctx + m_ctx[2] * y_ctx
            h2c = modulate(rms_norm(ctx, norm2_g[layer]), m_ctx[3], m_ctx[4])
            ctx = ctx + m_ctx[5] * moe(h2c, router_w[layer], router_b[layer], exp_w_gu[layer],
                                       exp_b_gu[layer], exp_w_down[layer], exp_b_down[layer])
    return rms_norm(x, final_norm_g)


def setup_inputs(seed=0):
    out = dict(first_inputs(seed))
    for name, value in second_inputs(seed + 1).items():
        if name != "x":
            out[name + "_2"] = value
    return out


def reference(
    x, w_in, g_sb, g_dil, w_out, ln1_g, ln1_b, ln2_g, ln2_b, rel_bias, w_router, b_router,
    w_gate, w_up, w_down, c_2, ctx_2, c_ctx_2, norm1_g_2, norm2_g_2, ada_w_2, ada_b_2, w_in_2,
    ret_decay_fwd_2, ret_decay_bwd_2, mla_q_norm_g_2, mla_w_uq_2, mla_kv_norm_g_2, mla_w_ukv_2,
    w_branch_ret_2, w_branch_mla_2, w_out_2, router_w_2, router_b_2, exp_w_gu_2, exp_b_gu_2,
    exp_w_down_2, exp_b_down_2, final_norm_g_2,
):
    x = first_block(
        x, w_in, g_sb, g_dil, w_out, ln1_g, ln1_b, ln2_g, ln2_b, rel_bias, w_router, b_router,
        w_gate, w_up, w_down,
    )
    return second_block(
        x, c_2, ctx_2, c_ctx_2, norm1_g_2, norm2_g_2, ada_w_2, ada_b_2, w_in_2, ret_decay_fwd_2,
        ret_decay_bwd_2, mla_q_norm_g_2, mla_w_uq_2, mla_kv_norm_g_2, mla_w_ukv_2,
        w_branch_ret_2, w_branch_mla_2, w_out_2, router_w_2, router_b_2, exp_w_gu_2, exp_b_gu_2,
        exp_w_down_2, exp_b_down_2, final_norm_g_2,
    )


_drawn_inputs = setup_inputs


def setup_inputs(seed=0):
    import zlib

    import numpy as np

    out = dict(_drawn_inputs(seed))
    spreads = {}
    factors = {'b_router': 5.929,
     'norm1_g_2': 7.927,
     'norm2_g_2': 3.806,
     'ada_b_2': 3.651,
     'mla_q_norm_g_2': 8.0,
     'mla_w_uq_2': 3.077,
     'mla_kv_norm_g_2': 8.0,
     'router_b_2': 6.555,
     'exp_b_gu_2': 22.782,
     'exp_b_down_2': 64.0,
     'final_norm_g_2': 8.149}
    for name, (base, spread) in spreads.items():
        noise = np.random.default_rng([zlib.crc32(name.encode()), seed]).standard_normal(out[name].shape)
        drawn = base * np.exp(spread * noise) if base else spread * noise
        out[name] = __import__('jax').numpy.asarray(drawn.astype(out[name].dtype))
    for name, factor in factors.items():
        out[name] = (out[name] * factor).astype(out[name].dtype)
    return out
```

```python
import math
from contextlib import ExitStack

import numpy as np

import concourse.bass as bass
from concourse import mybir

F32 = mybir.dt.float32
I32 = mybir.dt.int32
ALU = mybir.AluOpType
ACT = mybir.ActivationFunctionType
AX_X = mybir.AxisListType.X

P = 128
T = 256
TC = T // P
D = 1024
KC = D // P
HD = 64
HEADS = 8
SLOTS = 6
SLOT = 4096
BUF = 2048
CAP = 64
FF = 1024
E1, TOP1, GRP = 16, 2, 4
E2, TOP2 = 32, 4
NB1 = E1 + T * TOP1 // CAP + 1
NB2 = E2 + T * TOP2 // CAP + 1
ALPHA = 2.0 ** 0.25
LN_EPS = 1e-5
RMS_EPS = 1e-6
NEG = -1e30
RH, RQK, RV = 4, 256, 512
MH, QR, KVR, NOPE, ROPE, MV = 8, 384, 256, 128, 64, 128
LIMIT, SWIGLU = 7.0, 1.702
OFF = dict(rq=0, rk=1024, rv=2048, rg=4096, cq=6144, ck=6528, gr=6848, gm=7872)
CKR = KVR + ROPE

DVE_STAGES = (
    "vec_ready bias_rows_ready y_ready mod_ready x1_ready m1_shifted m1_chosen m1_placed m1_laid m1_table "
    "m1_sum x2_ready ctxn_ready xn_ready lag_ready krT_ready diag_ready x3_ready n2_ready m2_shifted m2_chosen "
    "m2_placed m2_laid m2_table m2_sum x4_ready out_ready").split()
ACT_STAGES = (
    "silc_ready m1_exp ctx_ss x2_ss decay_log x3_ss m2_exp x4_ss").split()

VEC = {}
_row = 0
for _name, _rows in (("g_sb", 4), ("g_dil", 4), ("n1g", 8), ("n2g", 8), ("qng", 3), ("kvg", 2), ("c", 8),
                     ("cctx", 8), ("ada_b", 48)):
    VEC[_name] = (_row, _row + _rows)
    _row += _rows
NVEC = _row


def shape_constants():
    f = np.float32
    p = np.arange(P)
    parts = {}
    parts["ident"] = np.eye(P)
    parts["flip"] = np.eye(P)[::-1]
    parts["suffix"] = (p[:, None] >= p[None, :])
    parts["before"] = (p[:, None] < p[None, :])
    parts["ones"] = np.ones((P, P))
    strict = np.where(p[:, None] < p[None, :], 0.0, NEG)
    parts["sb_mask"] = np.concatenate([strict, np.zeros((P, P)), strict], axis=1)
    j = np.arange(384)
    dist = 255 - j
    exact = 16
    big = exact + (np.log(np.maximum(dist, 1).astype(f) / f(exact)) / f(math.log(2048 / exact)) * f(16)).astype(np.int32)
    bucket = np.where(dist < exact, np.maximum(dist, 0), np.minimum(big, 31))
    count = np.where(dist >= 0, (dist <= 128).astype(int) + (dist % 4 == 0) + (dist % 16 == 0), 0)
    hot = np.zeros((P, 384))
    hot[bucket, j] = count > 0
    hot[32] = np.where(count > 0, np.log(np.maximum(count, 1)), NEG)
    parts["bias_hot"] = hot
    parts["iota"] = np.broadcast_to(np.arange(P), (P, P))
    parts["pidx"] = p[:, None]
    parts["lag"] = j[None, :] - P - p[:, None]
    tok = np.arange(T)
    pos = np.stack([tok // 64, tok % 64])

    def rope(half):
        freq = f(10000.0) ** (-np.arange(half, dtype=f) / f(half))
        ang = pos.astype(f)[:, :, None] * freq
        cos = np.cos(ang).transpose(1, 0, 2).reshape(TC, P, 2, 1, half)
        sin = np.sin(ang).transpose(1, 0, 2).reshape(TC, P, 2, half)
        cos = np.broadcast_to(cos, (TC, P, 2, 2, half))
        return (cos.transpose(1, 0, 2, 3, 4).reshape(P, -1), sin.transpose(1, 0, 2, 3).reshape(P, -1))

    parts["rcos"], parts["rsin"] = rope(64)
    parts["mcos"], parts["msin"] = rope(16)
    where, at = {}, 0
    for name, a in parts.items():
        where[name] = (at, at + a.shape[1])
        at += a.shape[1]
    return np.ascontiguousarray(np.concatenate([np.asarray(a, f) for a in parts.values()], axis=1)), where


CONSTS, CAT = shape_constants()


def two_block_kernel(nc, a, consts, bias_rows, out):
    with ExitStack() as ctx:
        def sb(name, cols, dt=F32):
            return ctx.enter_context(nc.sbuf_tensor(name, [P, cols], dt))

        sems = {}

        def S(name):
            if name not in sems:
                sems[name] = ctx.enter_context(nc.semaphore(name))
            return sems[name]

        def stage(name):
            if name in DVE_STAGES:
                return S("dve_stage"), DVE_STAGES.index(name) + 1
            return S("act_stage"), ACT_STAGES.index(name) + 1

        ring = sb("ring", SLOTS * SLOT)
        pool = sb("pool", 11 * BUF)
        cst = sb("cst", CONSTS.shape[1])
        vecT = sb("vecT", NVEC)
        rel33 = sb("rel33", HEADS)
        rw1 = sb("rw1", KC * E1)
        rw2 = sb("rw2", KC * E2)
        rb1 = sb("rb1", E1)
        rb2 = sb("rb2", E2)
        decay = sb("decay", 2 * RH)
        lg = sb("lg", 8 * 2 * RH)
        silc = sb("silc", 16)
        mod = sb("mod", 96)
        sc1 = sb("sc1", 16)
        sc2 = sb("sc2", 8)
        misc = sb("misc", 768)
        stat = sb("stat", 112)
        root = sb("root", 32)
        power = sb("power", 32)
        posb = sb("posb", TC * NB2)
        gateb = sb("gateb", TC * NB2)
        junk = sb("junk", 512)
        table = sb("table", NB2 + 1, I32)
        banks = [ctx.enter_context(nc.psum_tensor(f"bank{i}", [P, 512], F32)) for i in range(8)]

        def C(name, rows=P):
            lo, hi = CAT[name]
            return cst[0:rows, lo:hi]

        def B(i, cols=BUF, at=0):
            return pool[:, i * BUF + at:i * BUF + at + cols]

        def slot(n):
            return ring[:, (n % SLOTS) * SLOT:(n % SLOTS + 1) * SLOT]

        bias8, lagf, lagb, krT = misc[:, 0:384], misc[:, 0:384], misc[:, 384:768], misc[:, 0:512]
        vrows = junk[:, 0:P]

        ident, ones, before, suffix, flip = C("ident"), C("ones"), C("before"), C("suffix"), C("flip")

        x_rows = B(0).rearrange("p (t d) -> p t d", t=TC)
        xT = B(1).rearrange("p (k t) -> p k t", k=KC)
        qk_sb = [B(2, 1024, 1024 * i).rearrange("p (m t) -> p m t", m=4) for i in range(2)]
        qk_dl = [B(3, 1024, 1024 * i).rearrange("p (m t) -> p m t", m=4) for i in range(2)]
        v_sb, v_dl = (B(4, 1024, 1024 * i).rearrange("p (t c) -> p t c", t=TC) for i in range(2))
        hankel = B(5).rearrange("p (h k) -> p h k", h=HEADS)
        y_rows = B(6).rearrange("p (t d) -> p t d", t=TC)
        yT = B(7).rearrange("p (k t) -> p k t", k=KC)
        SBW = 768
        sb_work = pool[:, 8 * BUF:11 * BUF].rearrange("p (b w c) -> p b w c", b=2, w=4)
        dl_p = B(8, 768).rearrange("p (b c) -> p b c", b=2)
        dl_pT = B(8, 768, 768).rearrange("p (b c) -> p b c", b=2)
        ln1 = B(9).rearrange("p (w d) -> p w d", w=2)
        ln2 = B(10).rearrange("p (w d) -> p w d", w=2)

        y_acc = B(2).rearrange("p (t d) -> p t d", t=TC)
        xgT = B(3, 512).rearrange("p (k s) -> p k s", k=KC)
        hidT = B(3, 512, 512)
        act_g = B(3, 512, 1024)
        pick = B(3, 128, 1536).rearrange("p (t s) -> p t s", t=TC)
        pick_g = B(3, 256, 1664).rearrange("p (t f s) -> p t f s", t=TC, f=2)
        y_slot, hid, up_1, gate_1 = (B(4, 512, 512 * i) for i in range(4))
        put = junk[:, 0:T]
        this_expert = junk[0:E2, T:T + CAP]

        ctx_rows = B(6).rearrange("p (t d) -> p t d", t=TC)
        xn_rows = B(5).rearrange("p (t d) -> p t d", t=TC)
        latT = B(1).rearrange("p (k t) -> p k t", k=KC)
        ctxT = B(2).rearrange("p (k t) -> p k t", k=KC)
        rq_rows = B(3).rearrange("p (t d) -> p t d", t=TC)
        rk_rows = B(9).rearrange("p (t d) -> p t d", t=TC)
        rqT = B(4).rearrange("p (c t) -> p c t", c=8)
        rkT = pool[:, 5 * BUF:7 * BUF].rearrange("p (c t) -> p c t", c=8)
        rv = [B(7 + i).rearrange("p (j c) -> p j c", j=4) for i in range(2)]
        dec = B(3, 1024).rearrange("p (j t) -> p j t", j=4)
        dec2 = B(3, 1024, 1024).rearrange("p (j t) -> p j t", j=4)
        ret = pool[:, 9 * BUF:11 * BUF].rearrange("p (t c) -> p t c", t=TC)
        rope_tmp = B(7, 512)
        sig_gr = B(5).rearrange("p (t d) -> p t d", t=TC)
        sig_gm = B(1).rearrange("p (t d) -> p t d", t=TC)
        retT = pool[:, 7 * BUF:9 * BUF].rearrange("p (c t) -> p c t", c=16)
        merged = B(6).rearrange("p (t d) -> p t d", t=TC)
        cqn = B(3, 768).rearrange("p (t c) -> p t c", t=TC)
        ckn = B(3, 1024, 768).rearrange("p (j c) -> p j c", j=4)
        kr2 = B(4, 512).rearrange("p (j c) -> p j c", j=4)
        mrope_tmp = B(4, 256, 512)
        cqnT = B(4, 768, 1024).rearrange("p (c t) -> p c t", c=3)
        cknT = B(2, 1024).rearrange("p (c t) -> p c t", c=2)
        qnT = B(7).rearrange("p (h t) -> p h t", h=MH)
        qr_rows = B(8, 1024).rearrange("p (t c) -> p t c", t=TC)
        qrT = B(8, 1024, 1024).rearrange("p (m t) -> p m t", m=4)
        knT = pool[:, 9 * BUF:11 * BUF].rearrange("p (h t) -> p h t", h=MH)
        mv = [B(3).rearrange("p (j c) -> p j c", j=2), B(5).rearrange("p (j c) -> p j c", j=2)]
        mp = B(2, 1024, 1024).rearrange("p (b c) -> p b c", b=2)
        mpT = B(8, 1024).rearrange("p (j t) -> p j t", j=4)
        mT = B(4).rearrange("p (h t) -> p h t", h=MH)
        mergedT = B(2).rearrange("p (k t) -> p k t", k=KC)
        diag = B(10).rearrange("p (k c) -> p k c", k=16)
        gate_bc = B(7).rearrange("p (w d) -> p w d", w=2)
        n2_rows = B(1).rearrange("p (t d) -> p t d", t=TC)
        h2T = B(5).rearrange("p (k t) -> p k t", k=KC)
        bgu_rows = pool[0:E2, 8 * BUF:9 * BUF]
        bdn_rows = pool[0:E2, 9 * BUF:9 * BUF + 1024]
        fng = B(10, 1024)

        def cols(w, at, n):
            return w[:, at:at + n].rearrange("(k p) f -> p k f", p=P)

        def rows4(w, u):
            return w[u * 512:(u + 1) * 512, :].rearrange("(k p) f -> p k f", p=P)

        def part(n, k, f):
            return slot(n)[:, 0:k * f].rearrange("p (k f) -> p k f", k=k)

        units_a = [(cols(a["w_in"][0], 512 * u, 512), 8, 512) for u in range(6)]
        units_a += [(cols(a["ada_w_2"][0], 512 * u, 512), 8, 512) for u in range(12)]
        units_a += [(rows4(a["w_out"][0], u), 4, 1024) for u in range(2)]
        ADA0, WOUT0 = 6, 18
        w2 = a["w_in_2"][0]
        units_b, UB = [], {}

        def unit_b(name, src, k, f):
            UB[name] = len(units_b)
            units_b.append((src, k, f))

        for n in ("rq", "rk"):
            for u in range(2):
                unit_b((n, u), cols(w2, OFF[n] + 512 * u, 512), 8, 512)
        for h in range(RH):
            unit_b(("rv", h), cols(w2, OFF["rv"] + RV * h, RV), 8, RV)
            unit_b(("rg", h), cols(w2, OFF["rg"] + RV * h, RV), 8, RV)
        for u in range(2):
            unit_b(("gr", u), cols(w2, OFF["gr"] + 512 * u, 512), 8, 512)
        unit_b("cq", cols(w2, OFF["cq"], QR), 8, QR)
        unit_b("ck", cols(w2, OFF["ck"], CKR), 8, CKR)
        for u in range(2):
            unit_b(("gm", u), cols(w2, OFF["gm"] + 512 * u, 512), 8, 512)
        for u in range(4):
            unit_b(("br", u), rows4(a["w_branch_ret_2"][0], u), 4, 1024)
        for u in range(2):
            unit_b(("uq", u), cols(a["mla_w_uq_2"][0], 768 * u, 768), 3, 768)
        unit_b("ukv", cols(a["mla_w_ukv_2"][0], 0, 2048), 2, 2048)
        for u in range(2):
            unit_b(("bm", u), rows4(a["w_branch_mla_2"][0], u), 4, 1024)
        for u in range(2):
            unit_b(("wo", u), rows4(a["w_out_2"][0], u), 4, 1024)

        def moe_units(m, e):
            if m == "m1":
                cut = [(w, 0) for w in (a["w_gate"][0], a["w_up"][0], a["w_down"][0])]
            else:
                cut = [(a["exp_w_gu_2"][0], 0), (a["exp_w_gu_2"][0], FF), (a["exp_w_down_2"][0], 0)]
            return [w[bass.ds(e, 1), 512 * i:512 * i + 512, lo:lo + 1024].rearrange("o (k p) f -> p (o k) f", p=P)
                    for w, lo in cut for i in range(2)]

        MOE = {"m1": (E1, NB1), "m2": (E2, NB2)}

        def scratch_of(m):
            return B(5) if m == "m1" else B(6)

        def rt_logits(m):
            return scratch_of(m)[:, 1024:1024 + TC * MOE[m][0]]

        def route_parts(m):
            E, NB = MOE[m]
            at = 0
            got = []
            for rows, n in ((P, 2 * E), (P, 2 * E), (P, 2 * E), (E, 1), (E, T), (E, T), (E, NB), (E, NB)):
                got.append(scratch_of(m)[0:rows, at:at + n])
                at += n
            return got

        tiles, uses, turn = {}, [0] * 8, [0]

        def open_tile(pe, name, bank=None, among=8):
            if bank is None:
                bank = turn[0] % among
                turn[0] += 1
            tiles[name] = (bank, uses[bank])
            if uses[bank]:
                pe.wait_ge(S(f"bank_free{bank}"), uses[bank])
            uses[bank] += 1
            return banks[bank]

        def filled(ins, name):
            ins.then_inc(S(f"bank_full{tiles[name][0]}"), 1)

        def tile(eng, name):
            bank, use = tiles[name]
            eng.wait_ge(S(f"bank_full{bank}"), use + 1)
            return banks[bank]

        unit_done, counted = {}, {"a": 0, "b": 0}

        def multiplied(phase, n, by):
            if by in tiles:
                unit_done[phase, n] = (S(f"bank_full{tiles[by][0]}"), tiles[by][1] + 1)
            else:
                counted[phase] += 1
                by.then_inc(S(f"{phase}_used"), 1)
                unit_done[phase, n] = (S(f"{phase}_used"), counted[phase])

        def freed(ins, name):
            ins.then_inc(S(f"bank_free{tiles[name][0]}"), 1)

        block = ctx.enter_context(nc.Block())

        @block.tensor
        def _(pe):
            mm = nc.tensor.matmul
            tp = nc.tensor.transpose

            def landed(phase, n):
                pe.wait_ge(S(f"{phase}_full{n % SLOTS}"), 16 * (n // SLOTS + 1))

            def transposes(name, src, pairs, among=8):
                for cp in range(pairs):
                    ps = open_tile(pe, (name, cp), among=among)
                    for c in range(2):
                        for t in range(TC):
                            i = tp(ps[:, c * T + t * P:c * T + t * P + P],
                                   src[:, t, (2 * cp + c) * P:(2 * cp + c + 1) * P], ident)
                    filled(i, (name, cp))

            def by_columns(name, phase, n, w, src, among=8):
                landed(phase, n)
                for mp_ in range(2):
                    ps = open_tile(pe, (name, mp_), among=among)
                    for m in range(2):
                        for k in range(KC):
                            i = mm(ps[:, m * T:(m + 1) * T], w[:, k, (2 * mp_ + m) * P:(2 * mp_ + m + 1) * P],
                                   src[:, k, :], start=(k == 0), stop=(k == KC - 1))
                    filled(i, (name, mp_))
                multiplied(phase, n, (name, 1))

            def by_rows(names, phase, n, w, srcs, width, among=8, last=True):
                landed(phase, n)
                for name, (src, t) in zip(names, srcs):
                    ps = open_tile(pe, name, among=among)
                    for k in range(w.shape[1]):
                        i = mm(ps[:, 0:width], src[:, k, t * P:(t + 1) * P], w[:, k, 0:width],
                               start=(k == 0), stop=(k == w.shape[1] - 1))
                    filled(i, name)
                if last:
                    multiplied(phase, n, names[-1])

            def down_proj(name, phase, n0, units, srcT, among=8):
                ps = {(t, f): open_tile(pe, (name, t, f), among=among) for t in range(TC) for f in range(2)}
                for u in range(units):
                    landed(phase, n0 + u)
                    w = part(n0 + u, 4, 1024)
                    for k in range(4):
                        kk = 4 * u + k
                        for t in range(TC):
                            for f in range(2):
                                i = mm(ps[t, f][:, :], srcT[:, kk, t * P:(t + 1) * P], w[:, k, f * 512:(f + 1) * 512],
                                       start=(kk == 0), stop=(kk == 4 * units - 1))
                                if kk == 4 * units - 1:
                                    filled(i, (name, t, f))
                    multiplied(phase, n0 + u, i if u < units - 1 else (name, 1, 1))

            pe.wait_ge(S("ld_const"), 16)
            pe.wait_ge(S("ld_vec"), 16 * 9)
            ps = open_tile(pe, "vec", among=4)
            filled(tp(ps[:, 0:NVEC], vrows[0:NVEC, :], ident[0:NVEC, 0:NVEC]), "vec")
            pe.wait_ge(S("ld_rel"), 16)
            pe.wait_ge(S("root_set"), 3)
            ps = open_tile(pe, "rel", among=4)
            filled(mm(ps[0:HEADS, 0:384], rel33[0:33, :], C("bias_hot", 33), start=True, stop=True), "rel")
            pe.wait_ge(S("ld_x"), 16)
            transposes("xT", x_rows, 4, among=4)

            pe.wait_ge(S("xT_ready"), 4)
            for u, kind in enumerate(("q_sb", "k_sb", "v_sb", "q_dl", "k_dl", "v_dl")):
                w = part(u, KC, 512)
                if kind[0] == "v":
                    by_rows([(kind, t) for t in range(TC)], "a", u, w, [(xT, t) for t in range(TC)], 512, among=4)
                else:
                    by_columns(kind, "a", u, w, xT, among=4)

            ada = open_tile(pe, "ada", bank=4)

            def ada_unit(u):
                if u == 0:
                    pe.wait_ge(*stage("silc_ready"))
                landed("a", ADA0 + u)
                w = part(ADA0 + u, KC, 512)
                for m in range(4):
                    at = (4 * u + m) * 2
                    for k in range(KC):
                        i = mm(ada[:, at:at + 2], w[:, k, m * P:(m + 1) * P], silc[:, k:k + KC + 1:KC],
                               start=(k == 0), stop=(k == KC - 1))
                if u == 11:
                    filled(i, "ada")
                multiplied("a", ADA0 + u, i if u < 11 else "ada")

            pe.wait_ge(S("qk_ready"), 4)
            pe.wait_ge(S("v_ready"), 2)

            def sb_logits(p):
                for h in (2 * p, 2 * p + 1):
                    lo = HD * (h % 2)
                    q, k = (w[lo:lo + HD, h // 2, :] for w in qk_sb)
                    ps = open_tile(pe, ("z", h), among=4)
                    mm(ps[:, 0:256], k[:, 0:128], q[:, :], start=True, stop=True)
                    filled(mm(ps[:, 256:384], k[:, 128:256], q[:, 128:256], start=True, stop=True), ("z", h))

            def sb_suffix(p):
                pe.wait_ge(S("sb_softplus"), p + 1)
                for j, h in enumerate((2 * p, 2 * p + 1)):
                    sp = sb_work[:, p % 2, 2, j * 384:(j + 1) * 384]
                    ps = open_tile(pe, ("R", h), among=4)
                    mm(ps[:, 0:256], suffix, sp[:, 0:256], start=True, stop=False, skip_group_check=True)
                    mm(ps[:, 128:256], ones, sp[:, 256:384], start=False, stop=False, skip_group_check=True)
                    filled(mm(ps[:, 256:384], suffix, sp[:, 256:384], start=False, stop=True, skip_group_check=True),
                           ("R", h))

            sb_o = [open_tile(pe, ("sb_o", t), bank=6 + t) for t in range(TC)]

            def sb_values(p):
                pe.wait_ge(S("sb_weights"), p + 1)
                for j, h in enumerate((2 * p, 2 * p + 1)):
                    w = sb_work[:, p % 2, 3, j * 384:(j + 1) * 384]
                    c = slice(h * HD, (h + 1) * HD)
                    i0 = mm(sb_o[0][:, c], w[:, 0:128], v_sb[:, 0, c], start=True, stop=True)
                    if h == HEADS - 1:
                        filled(i0, ("sb_o", 0))
                    mm(sb_o[1][:, c], w[:, 128:256], v_sb[:, 0, c], start=True, stop=False)
                    i1 = mm(sb_o[1][:, c], w[:, 256:384], v_sb[:, 1, c], start=False, stop=True)
                if p < 3:
                    i1.then_inc(S("sb_values_done"), 1)
                else:
                    filled(i1, ("sb_o", 1))

            sb_logits(0)
            ada_unit(0)
            for p in range(4):
                if p < 3:
                    sb_logits(p + 1)
                ada_unit(1 + 2 * p)
                sb_suffix(p)
                ada_unit(2 + 2 * p)
                if p > 0:
                    sb_values(p - 1)
            sb_values(3)

            pe.wait_ge(S("qk_ready"), 8)
            pe.wait_ge(S("v_ready"), 4)
            pe.wait_ge(S("ld_hankel"), 16)

            def dl_logits(h):
                lo = HD * (h % 2)
                q, k = (w[lo:lo + HD, h // 2, :] for w in qk_dl)
                ps = open_tile(pe, ("L", h), among=4)
                mm(ps[:, 0:256], q[:, 128:256], k[:, :], start=True, stop=False)
                mm(ps[:, 0:256], flip, hankel[:, h, :], start=False, stop=True)
                mm(ps[:, 256:384], q[:, 0:128], k[:, 0:128], start=True, stop=False)
                filled(mm(ps[:, 256:384], flip, hankel[:, h, 128:256], start=False, stop=True), ("L", h))

            def dl_turn(h):
                pe.wait_ge(S("dl_exp"), 2 * (h + 1))
                ps = open_tile(pe, ("pT", h), among=4)
                for j in range(3):
                    i = tp(ps[:, j * P:(j + 1) * P], dl_p[:, h % 2, j * P:(j + 1) * P], ident)
                filled(i, ("pT", h))

            dl_o = [open_tile(pe, ("dl_o", t), bank=(5, 7)[t]) for t in range(TC)]

            def dl_values(h):
                pe.wait_ge(S("dl_pT_ready"), h + 1)
                c = slice(h * HD, (h + 1) * HD)
                w = dl_pT[:, h % 2, :]
                mm(dl_o[1][:, c], w[:, 0:128], v_dl[:, 0, c], start=True, stop=False)
                i1 = mm(dl_o[1][:, c], w[:, 128:256], v_dl[:, 1, c], start=False, stop=True)
                i0 = mm(dl_o[0][:, c], w[:, 256:384], v_dl[:, 0, c], start=True, stop=True)
                if h < HEADS - 1:
                    i0.then_inc(S("dl_values_done"), 1)
                else:
                    filled(i1, ("dl_o", 1))
                    filled(i0, ("dl_o", 0))

            dl_logits(0)
            for h in range(HEADS + 1):
                if h < 3:
                    ada_unit(9 + h)
                if h + 1 < HEADS:
                    dl_logits(h + 1)
                if h < HEADS:
                    dl_turn(h)
                if h > 0:
                    dl_values(h - 1)

            pe.wait_ge(*stage("y_ready"))
            transposes("yT", y_rows, 4, among=4)
            pe.wait_ge(S("yT_ready"), 8)
            down_proj("wo1", "a", WOUT0, 2, yT, among=4)
            pe.wait_ge(*stage("x1_ready"))
            transposes("x1T", x_rows, 4, among=4)

            def router(m, srcT, ready, n, w):
                E, _ = MOE[m]
                pe.wait_ge(S(ready), n)
                pe.wait_ge(S("ld_router"), 16 * 6)
                ps = open_tile(pe, (m, "logits"))
                for t in range(TC):
                    for k in range(KC):
                        i = mm(ps[:, t * E:(t + 1) * E], srcT[:, k, t * P:(t + 1) * P], w[:, k * E:(k + 1) * E],
                               start=(k == 0), stop=(k == KC - 1))
                filled(i, (m, "logits"))

            def block_table(m):
                E, NB = MOE[m]
                sel, gate, posm, nb, selT, gateT, bsel, rnd = route_parts(m)
                pe.wait_ge(*stage(f"{m}_chosen"))
                ps = open_tile(pe, (m, "pos"))
                mm(ps[:, 0:E], before, sel[:, 0:E], start=True, stop=True)
                mm(ps[:, E:2 * E], ones, sel[:, 0:E], start=True, stop=False)
                filled(mm(ps[:, E:2 * E], before, sel[:, E:2 * E], start=False, stop=True), (m, "pos"))
                ps = open_tile(pe, (m, "count"))
                mm(ps[0:E, 0:1], sel[:, 0:E], ones[:, 0:1], start=True, stop=False)
                filled(mm(ps[0:E, 0:1], sel[:, E:2 * E], ones[:, 0:1], start=False, stop=True), (m, "count"))
                pe.wait_ge(*stage(f"{m}_placed"))
                ps = open_tile(pe, (m, "turned"))
                for t in range(TC):
                    tp(ps[0:E, t * P:(t + 1) * P], posm[:, t * E:(t + 1) * E], ident)
                    i = tp(ps[0:E, T + t * P:T + (t + 1) * P], gate[:, t * E:(t + 1) * E], ident)
                filled(i, (m, "turned"))
                ps = open_tile(pe, (m, "start"))
                filled(mm(ps[0:E, 0:1], before[0:E, 0:E], nb, start=True, stop=True), (m, "start"))
                ps = open_tile(pe, (m, "blocks"))
                filled(mm(ps[0:1, 0:1], nb, ones[0:E, 0:1], start=True, stop=True), (m, "blocks"))
                pe.wait_ge(*stage(f"{m}_laid"))
                ps = open_tile(pe, (m, "posb"))
                for t in range(TC):
                    mm(ps[:, t * NB:(t + 1) * NB], selT[:, t * P:(t + 1) * P], bsel, start=True, stop=False)
                    i = mm(ps[:, t * NB:(t + 1) * NB], ones[0:E, :], rnd, start=False, stop=True)
                filled(i, (m, "posb"))
                ps = open_tile(pe, (m, "gateb"))
                for t in range(TC):
                    i = mm(ps[:, t * NB:(t + 1) * NB], gateT[:, t * P:(t + 1) * P], bsel, start=True, stop=True)
                filled(i, (m, "gateb"))
                ps = open_tile(pe, (m, "experts"))
                filled(mm(ps[0:1, 0:NB], C("pidx", E), bsel, start=True, stop=True), (m, "experts"))
                if m == "m2":
                    pe.wait_ge(S("ld_moe_bias"), 32)
                    for t in range(TC):
                        for f in range(2):
                            ps = open_tile(pe, (m, "bdown", t, f))
                            filled(mm(ps[:, :], gateT[:, t * P:(t + 1) * P], bdn_rows[:, f * 512:(f + 1) * 512],
                                      start=True, stop=True), (m, "bdown", t, f))

            def moe(m, src):
                XG, G, U, DN, Y0, Y1, PT, HT = banks
                for b in range(8):
                    pe.wait_ge(S(f"bank_free{b}"), uses[b])
                pe.wait_ge(*stage(f"{m}_table"))
                n = pe.value_load(table[0:1, NB2:NB2 + 1], min_val=1, max_val=MOE[m][1] - 1)
                full = [S(f"{m}_full{j}") for j in range(SLOTS)]
                free = [S(f"{m}_free{j}") for j in range(SLOTS)]
                weights = [part(j, 4, 1024) for j in range(SLOTS)]
                half = [slice(f * CAP, (f + 1) * CAP) for f in range(2)]

                def gather():
                    for k in range(KC):
                        for t in range(TC):
                            i = mm(XG[:, k * CAP:(k + 1) * CAP], src[:, t, k * P:(k + 1) * P], pick[:, t, :],
                                   start=(t == 0), stop=(t == TC - 1))
                    i.then_inc(S(f"{m}_gathered"), 1)

                def biases():
                    for w, dst in ((0, G), (1, U)):
                        for f in range(2):
                            at = w * FF + f * 512
                            i = mm(dst[half[f], :], this_expert, bgu_rows[:, at:at + 512], start=True, stop=False)
                    i.then_inc(S(f"{m}_biased"), 1)

                def product(dst, chunks, j, biased=False):
                    for k in range(4):
                        kk = 4 * (j % 2) + k
                        for f in range(2):
                            i = mm(dst[half[f], :], chunks[kk], weights[j][:, k, f * 512:(f + 1) * 512],
                                   start=(kk == 0 and not biased), stop=(kk == KC - 1))
                    i.then_inc(free[j], 1)

                def scatter(before_):
                    for q in range(4):
                        t, f = q // 2, q % 2
                        pe.wait_ge(S(f"{m}_added"), before_ + q + 1)
                        mm((Y0, Y1)[f][:, :], put[half[f], t * P:(t + 1) * P], y_slot[half[f], :],
                           start=True, stop=True).then_inc(S(f"{m}_scattered"), 1)

                token_chunks = [xgT[:, k, :] for k in range(KC)]
                hid_chunks = [hidT[:, c * P + f * CAP:c * P + (f + 1) * CAP] for f in range(2) for c in range(4)]
                biased = m == "m2"
                for j in range(SLOTS):
                    pe.nop().then_inc(free[j], 1)
                pe.nop().then_inc(S(f"{m}_put_ps"), 1)
                pe.wait_ge(S(f"{m}_pick"), 1)
                gather()
                with pe.Fori(0, n) as i:
                    if biased:
                        pe.wait_ge(S(f"{m}_expert"), i + 1)
                        biases()
                    pe.wait_ge(S(f"{m}_xgT"), i + 1)
                    pe.wait_ge(full[0], 16 * i + 16)
                    product(G, token_chunks, 0, biased)
                    pe.wait_ge(S(f"{m}_y_slot"), i + 1)
                    pe.wait_ge(S(f"{m}_put"), i + 1)
                    scatter(4 * i)
                    pe.wait_ge(full[1], 16 * i + 16)
                    product(G, token_chunks, 1, biased)
                    for j in (2, 3):
                        pe.wait_ge(full[j], 16 * i + 16)
                        product(U, token_chunks, j, biased)
                    pe.wait_ge(S(f"{m}_pick"), i + 2)
                    gather()
                    pe.wait_ge(S(f"{m}_hid"), i + 2)
                    for c in range(4):
                        ins = tp(HT[:, c * P:(c + 1) * P], hid[:, c * P:(c + 1) * P], ident)
                    ins.then_inc(S(f"{m}_turned"), 1)
                    pe.wait_ge(S(f"{m}_pick_g"), i + 1)
                    for t in range(TC):
                        ins = tp(PT[:, t * P:(t + 1) * P], pick_g[:, t, :, :], ident)
                    ins.then_inc(S(f"{m}_put_ps"), 1)
                    pe.wait_ge(S(f"{m}_hidT"), i + 1)
                    for j in (4, 5):
                        pe.wait_ge(full[j], 16 * i + 16)
                        product(DN, hid_chunks, j)
                pe.wait_ge(S(f"{m}_y_slot"), n + 1)
                pe.wait_ge(S(f"{m}_put"), n + 1)
                scatter(4 * n)
                pe.wait_ge(*stage(f"{m}_sum"))

            router("m1", xT, "x1T_ready", 4, rw1)
            block_table("m1")
            moe("m1", x_rows)

            pe.wait_ge(*stage("ctxn_ready"))
            transposes("cT", ctx_rows, 4)
            pe.wait_ge(*stage("xn_ready"))
            transposes("lT", xn_rows, 4)
            pe.wait_ge(S("ctxT_ready"), 8)
            pe.wait_ge(S("latT_ready"), 8)

            for u in range(2):
                n = UB["rq", u]
                by_rows([("rq", u, t) for t in range(TC)], "b", n, part(n, KC, 512), [(latT, t) for t in range(TC)], 512)
            for u in range(2):
                n = UB["rk", u]
                by_rows([("rk", u, t) for t in range(TC)], "b", n, part(n, KC, 512), [(latT, t) for t in range(TC)], 512,
                        last=False)
                by_columns(("kc", u), "b", n, part(n, KC, 512), ctxT)
            pe.wait_ge(S("rotated"), 4)
            transposes("rqT", rq_rows, 4)
            pe.wait_ge(S("rotated"), 8)
            transposes("rkT", rk_rows, 4)
            pe.wait_ge(S("rkT_ready"), 8)
            pe.wait_ge(S("rqT_ready"), 4)
            both = [(ctxT, 0), (ctxT, 1), (latT, 0), (latT, 1)]
            for h in range(RH):
                n = UB["rv", h]
                by_rows([("rv", h, j) for j in range(4)], "b", n, part(n, KC, RV), both, RV)
                for jp in range(2):
                    ps = open_tile(pe, ("S", h, jp))
                    for j in range(2):
                        for c in range(2):
                            at = (2 * jp + j) * P
                            i = mm(ps[:, j * T:(j + 1) * T], rkT[:, 2 * h + c, at:at + P], rqT[:, 2 * h + c, :],
                                   start=(c == 0), stop=(c == 1))
                    filled(i, ("S", h, jp))
                n = UB["rg", h]
                by_rows([("rg", h, t) for t in range(TC)], "b", n, part(n, KC, RV), [(latT, t) for t in range(TC)], RV)
                pe.wait_ge(S("rv_ready"), 4 * (h + 1))
                pe.wait_ge(S("ret_weights"), 2 * (h + 1))
                for t in range(TC):
                    ps = open_tile(pe, ("ro", h, t))
                    for j in range(4):
                        i = mm(ps[:, :], dec2[:, j, t * P:(t + 1) * P], rv[h % 2][:, j, :], start=(j == 0), stop=(j == 3))
                    filled(i, ("ro", h, t))

            for u in range(2):
                n = UB["gr", u]
                by_rows([("gr", u, t) for t in range(TC)], "b", n, part(n, KC, 512), [(latT, t) for t in range(TC)], 512)
            n = UB["cq"]
            by_rows([("cq", t) for t in range(TC)], "b", n, part(n, KC, QR), [(latT, t) for t in range(TC)], QR)
            n = UB["ck"]
            by_rows([("ck", j) for j in range(4)], "b", n, part(n, KC, CKR), both, CKR)
            for u in range(2):
                n = UB["gm", u]
                by_rows([("gm", u, t) for t in range(TC)], "b", n, part(n, KC, 512), [(latT, t) for t in range(TC)], 512)

            pe.wait_ge(S("ret_ready"), RH)
            transposes("retT", ret, 8)
            pe.wait_ge(S("retT_ready"), 8)
            down_proj("br", "b", UB["br", 0], 4, retT)

            pe.wait_ge(S("cqn_ready"), 2)
            for name, cs in ((("cqT", 0), (0, 1)), (("cqT", 1), (2,))):
                ps = open_tile(pe, name)
                for c in cs:
                    for t in range(TC):
                        i = tp(ps[:, (c % 2) * T + t * P:(c % 2) * T + (t + 1) * P], cqn[:, t, c * P:(c + 1) * P], ident)
                filled(i, name)
            pe.wait_ge(S("ckn_ready"), 4)
            for c in range(2):
                ps = open_tile(pe, ("ckT", c))
                for j in range(4):
                    i = tp(ps[:, j * P:(j + 1) * P], ckn[:, j, c * P:(c + 1) * P], ident)
                filled(i, ("ckT", c))
            ps = open_tile(pe, "krT")
            pe.wait_ge(S("kr_ready"), 4)
            for j in range(4):
                i = tp(ps[:, j * P:(j + 1) * P], kr2[:, j, :], ident)
            filled(i, "krT")
            pe.wait_ge(S("cqnT_ready"), 3)
            for u in range(2):
                n = UB["uq", u]
                w = part(n, 3, 768)
                landed("b", n)
                for hp in range(2):
                    name = ("qn", 2 * u + hp)
                    ps = open_tile(pe, name)
                    for j in range(2):
                        f = (2 * hp + j) * (NOPE + ROPE)
                        for k in range(3):
                            i = mm(ps[:, j * T:(j + 1) * T], w[:, k, f:f + NOPE], cqnT[:, k, :], start=(k == 0), stop=(k == 2))
                    filled(i, name)
                for t in range(TC):
                    name = ("qr", u, t)
                    ps = open_tile(pe, name)
                    for k in range(3):
                        heads = w[:, k, :].rearrange("p (h f) -> p h f", h=4)[:, :, NOPE:]
                        i = mm(ps[:, 0:256].rearrange("p (h f) -> p h f", h=4), cqnT[:, k, t * P:(t + 1) * P], heads,
                               start=(k == 0), stop=(k == 2))
                    filled(i, name)
                multiplied("b", n, ("qr", u, 1))
            pe.wait_ge(S("cknT_ready"), 2)
            n = UB["ukv"]
            w = part(n, 2, 2048)
            landed("b", n)
            for h in range(MH):
                ps = open_tile(pe, ("kn", h))
                for k in range(2):
                    f = h * (NOPE + MV)
                    i = mm(ps[:, :], w[:, k, f:f + NOPE], cknT[:, k, :], start=(k == 0), stop=(k == 1))
                filled(i, ("kn", h))
            for j in range(4):
                for g in range(2):
                    ps = open_tile(pe, ("mv", j, g))
                    for k in range(2):
                        heads = w[:, k, :].rearrange("p (h f) -> p h f", h=MH)[:, 4 * g:4 * g + 4, NOPE:]
                        i = mm(ps[:, :].rearrange("p (h f) -> p h f", h=4), cknT[:, k, j * P:(j + 1) * P], heads,
                               start=(k == 0), stop=(k == 1))
                    filled(i, ("mv", j, g))
            multiplied("b", n, ("mv", 3, 1))
            pe.wait_ge(S("qr_ready"), 4)
            for pp in range(2):
                ps = open_tile(pe, ("qrT", pp))
                for m in range(2):
                    for t in range(TC):
                        c = (2 * pp + m) * P
                        i = tp(ps[:, m * T + t * P:m * T + (t + 1) * P], qr_rows[:, t, c:c + P], ident)
                filled(i, ("qrT", pp))

            pe.wait_ge(S("qnT_ready"), 4)
            pe.wait_ge(S("knT_ready"), MH)
            pe.wait_ge(S("qrT_ready"), 2)
            pe.wait_ge(*stage("krT_ready"))
            pe.wait_ge(S("mv_ready"), 8)

            def mla_logits(j):
                h, t = j // TC, j % TC
                lo = ROPE * (h % 2)
                ps = open_tile(pe, ("s", j))
                mm(ps[:, :], qnT[:, h, t * P:(t + 1) * P], knT[:, h, :], start=True, stop=False)
                filled(mm(ps[:, :], qrT[lo:lo + ROPE, h // 2, t * P:(t + 1) * P], krT[lo:lo + ROPE, :],
                          start=False, stop=True), ("s", j))

            def mla_turn(j):
                pe.wait_ge(S("mla_probs"), j + 1)
                ps = open_tile(pe, ("mpT", j))
                for c in range(4):
                    i = tp(ps[:, c * P:(c + 1) * P], mp[:, j % 2, c * P:(c + 1) * P], ident)
                filled(i, ("mpT", j))

            def mla_values(h):
                pe.wait_ge(S("mpT_ready"), TC * (h + 1))
                ps = open_tile(pe, ("mo", h))
                for c in range(4):
                    i = mm(ps[:, 0:T], mv[c // 2][:, c % 2, h * MV:(h + 1) * MV], mpT[:, c, :], start=(c == 0), stop=(c == 3))
                filled(i, ("mo", h))

            N_J = MH * TC
            mla_logits(0)
            mla_logits(1)
            for j in range(N_J):
                if j + 2 < N_J:
                    mla_logits(j + 2)
                mla_turn(j)
                if j % TC == TC - 1:
                    mla_values(j // TC)
            pe.wait_ge(S("mT_ready"), MH)
            down_proj("bm", "b", UB["bm", 0], 2, mT)

            pe.wait_ge(*stage("diag_ready"))
            for j in range(4):
                ps = open_tile(pe, ("bc", j))
                for k in range(4):
                    i = mm(ps[:, k * P:(k + 1) * P], ones, diag[:, 4 * j + k, :], start=True, stop=True)
                filled(i, ("bc", j))

            pe.wait_ge(S("merged_ready"), 4)
            transposes("mgT", merged, 4)
            pe.wait_ge(S("mgT_ready"), 4)
            down_proj("yo", "b", UB["wo", 0], 2, mergedT)
            pe.wait_ge(*stage("n2_ready"))
            transposes("nT", n2_rows, 4)
            router("m2", h2T, "h2T_ready", 8, rw2)
            block_table("m2")
            moe("m2", n2_rows)

        @block.sync
        def _(sp):
            def stream(phase, units):
                for n, (src, k, f) in enumerate(units):
                    if n >= SLOTS:
                        sp.wait_ge(*unit_done[phase, n - SLOTS])
                    sp.dma_start(part(n, k, f), src).then_inc(S(f"{phase}_full{n % SLOTS}"), 16)

            def drained(phase, units):
                for n in range(len(units) - SLOTS, len(units)):
                    sp.wait_ge(*unit_done[phase, n])

            def experts(m):
                E, NB = MOE[m]
                sp.wait_ge(*stage(f"{m}_table"))
                n = sp.value_load(table[0:1, NB2:NB2 + 1], min_val=1, max_val=NB - 1)
                with sp.Fori(0, n) as i:
                    e = sp.value_load(table[0:1, bass.ds(i, 1)], min_val=0, max_val=E - 1)
                    for j, src in enumerate(moe_units(m, e)):
                        sp.wait_ge(S(f"{m}_free{j}"), i + 1)
                        sp.dma_start(part(j, 4, 1024), src).then_inc(S(f"{m}_full{j}"), 16)
                for j in range(SLOTS):
                    sp.wait_ge(S(f"{m}_free{j}"), n + 1)

            stream("a", units_a)
            drained("a", units_a)
            experts("m1")
            stream("b", units_b)
            drained("b", units_b)
            experts("m2")
            sp.wait_ge(*stage("out_ready"))
            sp.dma_start(out[0].rearrange("(t p) d -> p t d", p=P), y_acc).then_inc(S("stored"), 16)
            sp.wait_ge(S("stored"), 16)

        @block.gpsimd
        def _(pool_eng):
            def load(dst, src, sem):
                pool_eng.dma_start(dst, src).then_inc(S(sem), 16)

            def spread(ap, n):
                return ap.partition_broadcast(n)

            roots = [0]

            def inverse_roots(n):
                for _ in range(n):
                    roots[0] += 1
                    pool_eng.wait_ge(S("root_asked"), roots[0])
                    nc.gpsimd.tensor_tensor(root[:, :], root[:, :], power[:, :], ALU.pow).then_inc(S("root_given"), 1)

            nc.gpsimd.memset(power[:, :], -0.5).then_inc(S("root_set"), 1)
            pool_eng.wait_ge(S("root_set"), 1)
            nc.gpsimd.memset(root[:, :], 1.0).then_inc(S("root_set"), 1)
            pool_eng.wait_ge(S("root_set"), 2)
            load(x_rows, a["x"][0].rearrange("(t p) d -> p t d", p=P), "ld_x")
            load(cst[:, :], consts, "ld_const")
            nc.gpsimd.memset(rel33[32:33, :], 1.0).then_inc(S("root_set"), 1)
            load(rel33[0:32, :], a["rel_bias"], "ld_rel")
            rows = {"g_sb": a["g_sb"][0], "g_dil": a["g_dil"][0], "n1g": a["norm1_g_2"][0], "n2g": a["norm2_g_2"][0],
                    "qng": a["mla_q_norm_g_2"][0], "kvg": a["mla_kv_norm_g_2"][0], "c": a["c_2"][0],
                    "cctx": a["c_ctx_2"], "ada_b": a["ada_b_2"][0]}
            for name, v in rows.items():
                lo, hi = VEC[name]
                load(vrows[lo:hi, :], v.rearrange("(k p) -> k p", p=P), "ld_vec")
            load(rw1[:, :].rearrange("p (k e) -> p k e", k=KC), a["w_router"].rearrange("(k p) e -> p k e", p=P), "ld_router")
            load(rw2[:, :].rearrange("p (k e) -> p k e", k=KC), a["router_w_2"][0].rearrange("(k p) e -> p k e", p=P),
                 "ld_router")
            load(rb1[:, :], spread(a["b_router"], P), "ld_router")
            load(rb2[:, :], spread(a["router_b_2"][0], P), "ld_router")
            load(decay[:, 0:RH], spread(a["ret_decay_fwd_2"][0], P), "ld_router")
            load(decay[:, RH:2 * RH], spread(a["ret_decay_bwd_2"][0], P), "ld_router")
            pool_eng.wait_ge(*stage("bias_rows_ready"))
            load(bias_rows, bias8[0:HEADS, :], "bias_stored")
            pool_eng.wait_ge(S("bias_stored"), 16)
            shifted = bass.AP(bias_rows.tensor, 0, [[1, P], [384, HEADS], [1, 256]])
            load(hankel, shifted, "ld_hankel")
            tile(pool_eng, ("sb_o", 1))
            load(ln1[:, 0, :], spread(a["ln1_g"][0], P), "ld_ln")
            load(ln1[:, 1, :], spread(a["ln1_b"][0], P), "ld_ln")
            load(ln2[:, 0, :], spread(a["ln2_g"][0], P), "ld_ln")
            load(ln2[:, 1, :], spread(a["ln2_b"][0], P), "ld_ln")
            inverse_roots(1)
            pool_eng.wait_ge(S("yT_ready"), 8)
            load(ctx_rows, a["ctx_2"][0].rearrange("(t p) d -> p t d", p=P), "ld_ctx")
            inverse_roots(4 + 2 + RH + 2)
            pool_eng.wait_ge(S("mT_ready"), MH)
            load(bgu_rows, a["exp_b_gu_2"][0], "ld_moe_bias")
            load(bdn_rows, a["exp_b_down_2"][0], "ld_moe_bias")
            pool_eng.wait_ge(S("bc_ready"), 4)
            load(fng, spread(a["final_norm_g_2"], P), "ld_fng")
            inverse_roots(2)

        @block.scalar
        def _(act):
            af = nc.scalar.activation
            chain = [0]

            def link(ins):
                chain[0] += 1
                ins.then_inc(S("act_chain"), 1)
                act.wait_ge(S("act_chain"), chain[0])

            def evac(dst, name, view, sem, scale=1.0, func=ACT.Copy):
                ps = tile(act, name)
                freed(af(dst, view(ps), func, scale=scale), name)
                act.wait_ge(S(f"bank_free{tiles[name][0]}"), tiles[name][1] + 1)
                act.nop().then_inc(S(sem), 1)

            def pairs(dst, cp):
                return dst[:, 2 * cp:2 * cp + 2, :]

            def two(ps):
                return ps[:, :].rearrange("p (c t) -> p c t", c=2)

            act.wait_ge(*stage("vec_ready"))
            lo = VEC["c"][0]
            af(silc[:, :], vecT[:, lo:lo + 16], ACT.Silu).then_inc(stage("silc_ready")[0], 1)
            for cp in range(4):
                evac(pairs(xT, cp), ("xT", cp), two, "xT_ready")
            for kind, dst in (("q_sb", qk_sb[0]), ("k_sb", qk_sb[1]), ("q_dl", qk_dl[0]), ("k_dl", qk_dl[1])):
                for mp_ in range(2):
                    evac(pairs(dst, mp_), (kind, mp_), two, "qk_ready", HD ** -0.5 if kind[0] == "q" else 1.0)

            def sb_log(p):
                zm, e = sb_work[:, p % 2, 0, :], sb_work[:, p % 2, 1, :]
                act.wait_ge(S("sb_masked"), p + 1)
                if p >= 2:
                    act.wait_ge(S("sb_softplus"), p - 1)
                link(af(e, zm, ACT.Abs))
                link(af(e, e, ACT.Exp, scale=-1.0))
                af(e, e, ACT.Ln, bias=1.0).then_inc(S("sb_log"), 1)

            def sb_exp(p):
                act.wait_ge(S("sb_exponent"), p + 1)
                if p >= 2:
                    act.wait_ge(S("sb_values_done"), p - 1)
                af(sb_work[:, p % 2, 3, :], sb_work[:, p % 2, 0, :], ACT.Exp).then_inc(S("sb_weights"), 1)

            sb_log(0)
            for p in range(4):
                if p < 3:
                    sb_log(p + 1)
                sb_exp(p)

            den = stat[:, 0:16].rearrange("p (h t) -> p h t", t=2)
            nmx = stat[:, 16:32].rearrange("p (h t) -> p h t", t=2)
            for h in range(HEADS):
                ps = tile(act, ("L", h))
                act.wait_ge(S("dl_max"), h + 1)
                if h >= 2:
                    act.wait_ge(S("dl_pT_ready"), h - 1)
                if h == 0:
                    tile(act, ("sb_o", 1))
                af(dl_p[:, h % 2, 0:256], ps[:, 0:256], ACT.Exp, bias=nmx[:, h, 0:1],
                   accum_out=den[:, h, 0:1]).then_inc(S("dl_exp"), 1)
                af(dl_p[:, h % 2, 256:384], ps[:, 256:384], ACT.Exp, bias=nmx[:, h, 1:2],
                   accum_out=den[:, h, 1:2]).then_inc(S("dl_exp"), 1)
                act.wait_ge(S("dl_exp"), 2 * h + 2)
                freed(act.nop(), ("L", h))

            for cp in range(4):
                evac(pairs(xT, cp), ("x1T", cp), two, "x1T_ready")

            def gates_exp(m):
                E, _ = MOE[m]
                act.wait_ge(*stage(f"{m}_shifted"))
                L = rt_logits(m)
                af(L, L, ACT.Exp).then_inc(stage(f"{m}_exp")[0], 1)

            def moe(m):
                _, G, _, DN, _, _, _, _ = banks
                act.wait_ge(*stage(f"{m}_table"))
                n = act.value_load(table[0:1, NB2:NB2 + 1], min_val=1, max_val=MOE[m][1] - 1)
                with act.Fori(0, n) as i:
                    if m == "m1":
                        act.wait_ge(S(f"{m}_free1"), i + 2)
                        act.wait_ge(S(f"{m}_hid"), i + 1)
                        af(act_g, G[:, :], ACT.Silu).then_inc(S(f"{m}_act"), 1)
                    else:
                        act.wait_ge(S(f"{m}_gate"), i + 1)
                        act.wait_ge(S(f"{m}_hid"), i + 1)
                        af(act_g, gate_1, ACT.Sigmoid, scale=SWIGLU).then_inc(S(f"{m}_act"), 1)
                    act.wait_ge(S(f"{m}_free5"), i + 2)
                    act.wait_ge(S(f"{m}_scattered"), 4 * i + 4)
                    act.activation(y_slot, DN[:, :], ACT.Copy).then_inc(S(f"{m}_y_slot"), 1)

            gates_exp("m1")
            moe("m1")

            ss = stat[:, 32:36]
            act.wait_ge(S("ld_ctx"), 16)
            act.wait_ge(*stage("m1_sum"))
            for t in range(TC):
                i = af(B(4, 1024, 1024 * t), ctx_rows[:, t, :], ACT.Square, accum_out=ss[:, t:t + 1])
            i.then_inc(stage("ctx_ss")[0], 1)
            act.wait_ge(*stage("x2_ready"))
            for t in range(TC):
                i = af(B(3, 1024, 1024 * t), x_rows[:, t, :], ACT.Square, accum_out=ss[:, 2 + t:3 + t])
            i.then_inc(stage("x2_ss")[0], 1)

            act.wait_ge(*stage("mod_ready"))
            for cp in range(4):
                ps = tile(act, ("cT", cp))
                for c in range(2):
                    k = 2 * cp + c
                    i = af(ctxT[:, k, :], ps[:, c * T:(c + 1) * T], ACT.Identity, scale=sc1[:, 2 * k + 1:2 * k + 2],
                           bias=mod[:, 2 * k + 1:2 * k + 2])
                    i.then_inc(S("ctxT_ready"), 1)
                act.wait_ge(S("ctxT_ready"), 2 * cp + 2)
                freed(act.nop(), ("cT", cp))

            act.wait_ge(S("ld_router"), 16 * 6)
            link(af(lg[:, 8:16], decay[:, :], ACT.Abs))
            link(af(lg[:, 8:16], lg[:, 8:16], ACT.Exp, scale=-1.0))
            af(lg[:, 8:16], lg[:, 8:16], ACT.Ln, bias=1.0).then_inc(stage("decay_log")[0], 1)

            def ret_decay(h):
                if h:
                    act.wait_ge(S("ret_out"), 2 * h)
                else:
                    act.wait_ge(*stage("lag_ready"))
                    act.wait_ge(S("rqT_ready"), 4)
                for j in range(2):
                    u = P * (1 - j)
                    span = slice(u, u + T)
                    lag = C("lag")[:, span]
                    af(dec[:, j, :], lag, ACT.Exp, scale=lg[:, h:h + 1], bias=lg[:, 16 + h:17 + h])
                    af(dec2[:, j, :], lag, ACT.Exp, scale=lg[:, 28 + h:29 + h], bias=lg[:, 20 + h:21 + h])
                    af(dec[:, 2 + j, :], lagf[:, span], ACT.Exp, scale=lg[:, h:h + 1])
                    i = af(dec2[:, 2 + j, :], lagb[:, span], ACT.Exp, scale=lg[:, 4 + h:5 + h])
                i.then_inc(S("ret_decays"), 1)

            for u in range(2):
                for mp_ in range(2):
                    evac(rkT[:, 4 * u + 2 * mp_:4 * u + 2 * mp_ + 2, 0:T], (("kc", u), mp_), two, "rkT_ready", RQK ** -0.5)
            for cp in range(4):
                evac(pairs(rqT, cp), ("rqT", cp), two, "rqT_ready")
            for cp in range(4):
                evac(rkT[:, 2 * cp:2 * cp + 2, T:2 * T], ("rkT", cp), two, "rkT_ready", RQK ** -0.5)
            ret_decay(0)
            rss = stat[:, 36:44]
            for h in range(RH):
                for j in range(4):
                    if h >= 2 and j == 0:
                        act.wait_ge(S("ret_out"), 2 * (h - 1))
                    evac(rv[h % 2][:, j, :], ("rv", h, j), lambda ps: ps[:, :], "rv_ready")
                for t in range(TC):
                    evac(ret[:, t, h * RV:(h + 1) * RV], ("rg", h, t), lambda ps: ps[:, :], "ret_gate", func=ACT.Silu)
                for t in range(TC):
                    ps = tile(act, ("ro", h, t))
                    af(junk[:, :], ps[:, :], ACT.Square, accum_out=rss[:, 2 * h + t:2 * h + t + 1]).then_inc(S("ret_ss"), 1)
                    act.wait_ge(S("ret_ss"), 2 * h + t + 1)
                if h + 1 < RH:
                    ret_decay(h + 1)
            for u in range(2):
                for t in range(TC):
                    evac(sig_gr[:, t, u * 512:(u + 1) * 512], ("gr", u, t), lambda ps: ps[:, :], "sig_gr_ready", func=ACT.Sigmoid)

            mss = stat[:, 44:50]
            for t in range(TC):
                ps = tile(act, ("cq", t))
                af(junk[:, 0:QR], ps[:, 0:QR], ACT.Square, accum_out=mss[:, t:t + 1]).then_inc(S("mla_ss"), 1)
                act.wait_ge(S("mla_ss"), t + 1)
            for j in range(4):
                ps = tile(act, ("ck", j))
                af(junk[:, 0:KVR], ps[:, 0:KVR], ACT.Square, accum_out=mss[:, 2 + j:3 + j]).then_inc(S("mla_ss"), 1)
                act.wait_ge(S("mla_ss"), TC + j + 1)
            tile(act, ("gm", 1, 1))
            for u in range(2):
                for t in range(TC):
                    evac(sig_gm[:, t, u * 512:(u + 1) * 512], ("gm", u, t), lambda ps: ps[:, :], "sig_gm_ready", func=ACT.Sigmoid)
            for cp in range(8):
                evac(pairs(retT, cp), ("retT", cp), two, "retT_ready")
            for hp in range(4):
                evac(pairs(qnT, hp), ("qn", hp), two, "qnT_ready")
            for h in range(MH):
                evac(knT[:, h, :], ("kn", h), lambda ps: ps[:, :], "knT_ready")
            for pp in range(2):
                evac(pairs(qrT, pp), ("qrT", pp), two, "qrT_ready")

            mden, mnm = stat[:, 50:66], stat[:, 66:82]
            scale = (NOPE + ROPE) ** -0.5
            for j in range(MH * TC):
                ps = tile(act, ("s", j))
                act.wait_ge(S("mla_max"), j + 1)
                if j >= 2:
                    act.wait_ge(S("mpT_ready"), j - 1)
                freed(af(mp[:, j % 2, :], ps[:, :], ACT.Exp, scale=scale, bias=mnm[:, j:j + 1],
                         accum_out=mden[:, j:j + 1]), ("s", j))
                act.wait_ge(S(f"bank_free{tiles['s', j][0]}"), tiles["s", j][1] + 1)
                act.nop().then_inc(S("mla_exp"), 1)
                if j % TC == 0 and j:
                    evac(mT[:, j // TC - 1, :], ("mo", j // TC - 1), lambda ps: ps[:, 0:T], "mT_ready")
            evac(mT[:, MH - 1, :], ("mo", MH - 1), lambda ps: ps[:, 0:T], "mT_ready")
            for j in range(4):
                evac(gate_bc[:, j // 2, (j % 2) * 512:(j % 2) * 512 + 512], ("bc", j), lambda ps: ps[:, :], "bc_ready")
            for cp in range(4):
                evac(pairs(mergedT, cp), ("mgT", cp), two, "mgT_ready")
            act.wait_ge(*stage("x3_ready"))
            for t in range(TC):
                i = af(B(3, 1024, 1024 * t), x_rows[:, t, :], ACT.Square, accum_out=stat[:, 82 + t:83 + t])
            i.then_inc(stage("x3_ss")[0], 1)
            gates_exp("m2")
            moe("m2")
            act.wait_ge(*stage("x4_ready"))
            for t in range(TC):
                i = af(B(3, 1024, 1024 * t), y_acc[:, t, :], ACT.Square, accum_out=stat[:, 84 + t:85 + t])
            i.then_inc(stage("x4_ss")[0], 1)

        @block.vector
        def _(dve):
            v = nc.vector
            tt, ts, stt = v.tensor_tensor, v.tensor_scalar, v.scalar_tensor_tensor
            chain = [0]
            chain_root = [0]
            marks = {}

            def link(ins):
                chain[0] += 1
                ins.then_inc(S("dve_chain"), 1)
                dve.wait_ge(S("dve_chain"), chain[0])

            def mark(ins, name):
                marks[name] = marks.get(name, 0) + 1
                sem, value = stage(name) if name in DVE_STAGES else (S(name), marks[name])
                ins.then_inc(sem, 1)
                dve.wait_ge(sem, value)

            def rsqrt(x, scale, eps):
                chain_root[0] += 1
                r = root[:, 0:x.shape[1]]
                ts(r, x, scale, eps, ALU.mult, ALU.add).then_inc(S("root_asked"), 1)
                dve.wait_ge(S("root_given"), chain_root[0])
                link(v.tensor_copy(x, r))

            def bcast(x, n):
                return x.unsqueeze(2).to_broadcast([x.shape[0], x.shape[1], n])

            def two(ps):
                return ps[:, :].rearrange("p (c t) -> p c t", c=2)

            ps = tile(dve, "vec")
            link(v.tensor_copy(vecT[:, :], ps[:, 0:NVEC]))
            freed(dve.nop(), "vec")
            dve.nop().then_inc(stage("vec_ready")[0], 1)
            ps = tile(dve, "rel")
            link(v.tensor_copy(bias8[0:HEADS, :], ps[0:HEADS, 0:384]))
            freed(dve.nop(), "rel")
            dve.nop().then_inc(stage("bias_rows_ready")[0], 1)
            for kind, dst in (("v_sb", v_sb), ("v_dl", v_dl)):
                for t in range(TC):
                    ps = tile(dve, (kind, t))
                    link(v.tensor_copy(dst[:, t, :], ps[:, :]))
                    freed(dve.nop(), (kind, t))
                    dve.nop().then_inc(S("v_ready"), 1)

            def sb_mask(p):
                for j in range(2):
                    h = 2 * p + j
                    ps = tile(dve, ("z", h))
                    link(tt(sb_work[:, p % 2, 0, j * 384:(j + 1) * 384], ps[:, 0:384], C("sb_mask"), ALU.add))
                    freed(dve.nop(), ("z", h))
                dve.nop().then_inc(S("sb_masked"), 1)

            def sb_softplus(p):
                dve.wait_ge(S("sb_log"), p + 1)
                w = sb_work[:, p % 2]
                stt(w[:, 2, :], w[:, 0, :], 0.0, w[:, 1, :], ALU.max, ALU.add).then_inc(S("sb_softplus"), 1)

            def sb_exponent(p):
                for j in range(2):
                    h = 2 * p + j
                    ps = tile(dve, ("R", h))
                    z = sb_work[:, p % 2, 0, j * 384:(j + 1) * 384]
                    link(tt(z, z, ps[:, 0:384], ALU.subtract))
                    freed(dve.nop(), ("R", h))
                dve.nop().then_inc(S("sb_exponent"), 1)

            sb_mask(0)
            for p in range(4):
                if p < 3:
                    if p >= 1:
                        dve.wait_ge(S("sb_weights"), p)
                    sb_mask(p + 1)
                sb_softplus(p)
                sb_exponent(p)

            nmx = stat[:, 16:32].rearrange("p (h t) -> p h t", t=2)
            den = stat[:, 0:16].rearrange("p (h t) -> p h t", t=2)

            def dl_max(h):
                ps = tile(dve, ("L", h))
                v.tensor_reduce(nmx[:, h, 0:1], ps[:, 0:256], AX_X, ALU.max, negate=True)
                v.tensor_reduce(nmx[:, h, 1:2], ps[:, 256:384], AX_X, ALU.max, negate=True).then_inc(S("dl_max"), 1)

            def dl_copy(h):
                ps = tile(dve, ("pT", h))
                if h >= 2:
                    dve.wait_ge(S("dl_values_done"), h - 1)
                link(v.tensor_copy(dl_pT[:, h % 2, :], ps[:, 0:384]))
                freed(dve.nop(), ("pT", h))
                dve.nop().then_inc(S("dl_pT_ready"), 1)

            for t in range(TC):
                ps = tile(dve, ("sb_o", t))
                link(v.tensor_copy(y_rows[:, t, 0:512], ps[:, :]))
                freed(dve.nop(), ("sb_o", t))
            for h in range(HEADS + 1):
                if h < HEADS:
                    dl_max(h)
                if h > 0:
                    dl_copy(h - 1)

            dve.wait_ge(S("root_set"), 2)
            dve.wait_ge(S("dl_exp"), 2 * HEADS)
            link(v.reciprocal(stat[:, 0:16], stat[:, 0:16]))
            for t in range(TC):
                ps = tile(dve, ("dl_o", t))
                link(tt(y_rows[:, t, 512:1024].rearrange("p (h c) -> p h c", h=HEADS),
                        ps[:, :].rearrange("p (h c) -> p h c", h=HEADS), bcast(den[:, :, 1 - t], HD), ALU.mult))
                freed(dve.nop(), ("dl_o", t))
            y_heads = B(6).rearrange("p (g c) -> p g c", c=HD)
            sq = B(7).rearrange("p (g c) -> p g c", c=HD)
            hs = stat[:, 0:32]
            link(tt(sq, y_heads, y_heads, ALU.mult))
            link(v.tensor_reduce(hs, sq, AX_X, ALU.add))
            rsqrt(hs, 1.0 / HD, 1e-6)
            mark(tt(y_heads, y_heads, bcast(hs, HD), ALU.mult), "y_ready")
            g0 = VEC["g_sb"][0]
            for cp in range(4):
                ps = tile(dve, ("yT", cp))
                for c in range(2):
                    k = 2 * cp + c
                    mark(ts(yT[:, k, :], ps[:, c * T:(c + 1) * T], vecT[:, g0 + k:g0 + k + 1], None, ALU.mult), "yT_ready")
                freed(dve.nop(), ("yT", cp))

            ps = tile(dve, "ada")
            b0 = VEC["ada_b"][0]
            m3 = mod[:, :].rearrange("p (c w) -> p c w", w=2)
            link(tt(m3, ps[:, 0:96].rearrange("p (c w) -> p c w", w=2), bcast(vecT[:, b0:b0 + 48], 2), ALU.add))
            freed(dve.nop(), "ada")
            n1, n2 = VEC["n1g"], VEC["n2g"]
            link(stt(sc1[:, :].rearrange("p (c w) -> p c w", w=2), m3[:, 8:16, :], 1.0, bcast(vecT[:, n1[0]:n1[1]], 2),
                     ALU.add, ALU.mult))
            mark(stt(sc2[:, :], m3[:, 32:40, 0], 1.0, vecT[:, n2[0]:n2[1]], ALU.add, ALU.mult), "mod_ready")

            def layer_norm(rows, gb, sem):
                st = stat[:, 96:108]
                for t in range(TC):
                    for f in range(2):
                        link(v.bn_stats(st[:, 6 * f:6 * f + 6], rows[:, t, f * 512:(f + 1) * 512]))
                    link(v.bn_aggr(stat[:, 88:90], st))
                    rsqrt(stat[:, 89:90], 1.0, LN_EPS)
                    link(ts(rows[:, t, :], rows[:, t, :], stat[:, 88:89], stat[:, 89:90], ALU.subtract, ALU.mult))
                    link(tt(rows[:, t, :], rows[:, t, :], gb[:, 0, :], ALU.mult))
                    link(tt(rows[:, t, :], rows[:, t, :], gb[:, 1, :], ALU.add))
                mark(dve.nop(), sem)

            for t in range(TC):
                for f in range(2):
                    ps = tile(dve, ("wo1", t, f))
                    xs = x_rows[:, t, f * 512:(f + 1) * 512]
                    link(stt(xs, xs, ALPHA, ps[:, :], ALU.mult, ALU.add))
                    freed(dve.nop(), ("wo1", t, f))
            dve.wait_ge(S("ld_ln"), 64)
            layer_norm(x_rows, ln1, "x1_ready")

            def ranks(dst, vals, groups, n, cmp):
                big = cmp[:, 0:groups * n * n].rearrange("p (g i j) -> p g i j", g=groups, i=n)
                tie = cmp[:, groups * n * n:groups * n * n + n * n].rearrange("p (i j) -> p i j", i=n)
                eq = cmp[:, 1024 + n * n:1024 + n * n + groups * n * n].rearrange("p (g i j) -> p g i j", g=groups, i=n)
                row = C("iota")[:, 0:n]
                vj = vals.unsqueeze(2).to_broadcast([P, groups, n, n])
                vi = vals.unsqueeze(3).to_broadcast([P, groups, n, n])
                link(tt(tie, row.unsqueeze(1).to_broadcast([P, n, n]), bcast(row, n), ALU.is_lt))
                link(tt(eq, vj, vi, ALU.is_equal))
                link(tt(eq, eq, tie.unsqueeze(1).to_broadcast([P, groups, n, n]), ALU.mult))
                link(tt(big, vj, vi, ALU.is_gt))
                link(tt(big, big, eq, ALU.add))
                link(v.tensor_reduce(dst, big, AX_X, ALU.add))

            def choose(m, bias, scratch):
                E, NB = MOE[m]
                sel, gate = route_parts(m)[:2]
                sel3, gate3 = (w.rearrange("p (t e) -> p t e", t=TC) for w in (sel, gate))
                L = rt_logits(m)
                L3 = L.rearrange("p (t e) -> p t e", t=TC)
                mx = stat[:, 86:88]
                ps = tile(dve, (m, "logits"))
                link(tt(L3, ps[:, 0:TC * E].rearrange("p (t e) -> p t e", t=TC),
                        bias.unsqueeze(1).to_broadcast([P, TC, E]), ALU.add))
                freed(dve.nop(), (m, "logits"))
                if m == "m2":
                    for t in range(TC):
                        ranks(sel3[:, t:t + 1, :], L3[:, t:t + 1, :], 1, E, scratch)
                    link(ts(sel, sel, float(TOP2), None, ALU.is_lt))
                link(v.tensor_reduce(mx, L3, AX_X, ALU.max))
                tt(L3, L3, bcast(mx, E), ALU.subtract).then_inc(stage(f"{m}_shifted")[0], 1)
                dve.wait_ge(*stage(f"{m}_exp"))
                if m == "m1":
                    link(v.tensor_reduce(mx, L3, AX_X, ALU.add))
                    link(v.reciprocal(mx, mx))
                    link(tt(L3, L3, bcast(mx, E), ALU.mult))
                    G = E // GRP
                    Lg = L.rearrange("p (g e) -> p g e", e=GRP)
                    sg = sel.rearrange("p (g e) -> p g e", e=GRP)
                    gs = stat[:, 0:TC * G]
                    gr = stat[:, 8:8 + TC * G]
                    ranks(sg, Lg, TC * G, GRP, scratch)
                    link(ts(sel, sel, float(TOP1), None, ALU.is_lt))
                    link(tt(gate, L, sel, ALU.mult))
                    link(v.tensor_reduce(gs, gate.rearrange("p (g e) -> p g e", e=GRP), AX_X, ALU.add))
                    ranks(gr.rearrange("p (t g) -> p t g", t=TC), gs.rearrange("p (t g) -> p t g", t=TC), TC, G, scratch)
                    link(ts(gr, gr, 1.0, None, ALU.is_lt))
                    link(tt(sg, sg, bcast(gr, GRP), ALU.mult))
                link(tt(gate, L, sel, ALU.mult))
                link(v.tensor_reduce(mx, gate3, AX_X, ALU.add))
                link(v.reciprocal(mx, mx))
                mark(tt(gate3, gate3, bcast(mx, E), ALU.mult), f"{m}_chosen")

            def block_table(m):
                E, NB = MOE[m]
                sel, gate, posm, nb, selT, gateT, bsel, rnd = route_parts(m)
                ps = tile(dve, (m, "pos"))
                link(stt(posm, sel, 1e6, ps[:, 0:2 * E], ALU.mult, ALU.add))
                freed(dve.nop(), (m, "pos"))
                link(ts(posm, posm, -1e6, None, ALU.add))
                ps = tile(dve, (m, "count"))
                cnt, first, last = (stat[0:E, 90 + i:91 + i] for i in range(3))
                link(v.tensor_copy(cnt, ps[0:E, 0:1]))
                freed(dve.nop(), (m, "count"))
                link(ts(nb, cnt, 0.0, None, ALU.is_gt))
                for r in range(1, T // CAP):
                    link(stt(nb, cnt, float(CAP * r), nb, ALU.is_gt, ALU.add))
                mark(dve.nop(), f"{m}_placed")
                ps = tile(dve, (m, "turned"))
                link(v.tensor_copy(selT, ps[0:E, 0:T]))
                link(v.tensor_copy(gateT, ps[0:E, T:2 * T]))
                freed(dve.nop(), (m, "turned"))
                ps = tile(dve, (m, "start"))
                link(v.tensor_copy(first, ps[0:E, 0:1]))
                freed(dve.nop(), (m, "start"))
                link(tt(last, first, nb, ALU.add))
                row = C("iota", E)[:, 0:NB]
                link(ts(rnd, row, first, None, ALU.is_ge))
                link(stt(bsel, row, last, rnd, ALU.is_lt, ALU.mult))
                link(ts(rnd, row, first, -float(CAP), ALU.subtract, ALU.mult))
                mark(tt(rnd, rnd, bsel, ALU.mult), f"{m}_laid")
                for name, dst in (("posb", posb), ("gateb", gateb)):
                    ps = tile(dve, (m, name))
                    link(v.tensor_copy(dst[:, 0:TC * NB], ps[:, 0:TC * NB]))
                    freed(dve.nop(), (m, name))
                ps = tile(dve, (m, "blocks"))
                link(v.tensor_copy(table[0:1, NB2:NB2 + 1], ps[0:1, 0:1]))
                freed(dve.nop(), (m, "blocks"))
                ps = tile(dve, (m, "experts"))
                link(v.tensor_copy(table[0:1, 0:NB], ps[0:1, 0:NB]))
                freed(dve.nop(), (m, "experts"))
                if m == "m2":
                    for t in range(TC):
                        for f in range(2):
                            ps = tile(dve, (m, "bdown", t, f))
                            link(v.tensor_copy(y_acc[:, t, f * 512:(f + 1) * 512], ps[:, :]))
                            freed(dve.nop(), (m, "bdown", t, f))
                mark(dve.nop(), f"{m}_table")

            def moe(m):
                E, NB = MOE[m]
                XG, G, U, _, Y0, Y1, PT, HT = banks
                n = dve.value_load(table[0:1, NB2:NB2 + 1], min_val=1, max_val=NB - 1)
                pos3 = posb[:, 0:TC * NB].rearrange("p (t b) -> p t b", t=TC)
                gat3 = gateb[:, 0:TC * NB].rearrange("p (t b) -> p t b", t=TC)
                row = C("iota")[:, 0:CAP]

                def picks(i):
                    for t in range(TC):
                        ins = ts(pick[:, t, :], row, pos3[:, t, bass.ds(i, 1)], None, ALU.is_equal)
                    ins.then_inc(S(f"{m}_pick"), 1)

                def gathered():
                    xg = XG[:, :].rearrange("p (k s) -> p k s", k=KC)
                    if m == "m1":
                        v.tensor_copy(xgT, xg).then_inc(S(f"{m}_xgT"), 1)
                    else:
                        tt(xgT, xg, bcast(sc2[:, :], CAP), ALU.mult).then_inc(S("m2_scaled"), 1)

                def shifted():
                    if m == "m2":
                        tt(xgT, xgT, bcast(m3[:, 24:32, 0], CAP), ALU.add).then_inc(S(f"{m}_xgT"), 1)

                def expert(i):
                    bsel = route_parts(m)[6]
                    v.tensor_copy(this_expert, bsel[:, bass.ds(i, 1)].to_broadcast([E2, CAP])).then_inc(S("m2_expert"), 1)

                def add(before_, q):
                    dve.wait_ge(S(f"{m}_scattered"), before_ + q + 1)
                    t, f = q // 2, q % 2
                    ys = y_acc[:, t, f * 512:(f + 1) * 512]
                    tt(ys, ys, (Y0, Y1)[f][:, :], ALU.add).then_inc(S(f"{m}_added"), 1)

                v.memset(put, 0.0).then_inc(S(f"{m}_put"), 1)
                v.memset(y_slot, 0.0).then_inc(S(f"{m}_y_slot"), 1)
                dve.nop().then_inc(S(f"{m}_added"), 1)
                dve.nop().then_inc(S(f"{m}_added"), 1)
                dve.nop().then_inc(S(f"{m}_hid"), 1)
                picks(0)
                if m == "m2":
                    expert(0)
                dve.wait_ge(S(f"{m}_gathered"), 1)
                gathered()
                if m == "m2":
                    dve.wait_ge(S("m2_scaled"), 1)
                    shifted()
                with dve.Fori(0, n) as i:
                    dve.wait_ge(S(f"{m}_gathered"), i + 1)
                    picks(i + 1)
                    dve.wait_ge(S(f"{m}_put_ps"), i + 1)
                    for t in range(TC):
                        ins = ts(pick_g[:, t, :, :], row.unsqueeze(1).to_broadcast([P, 2, CAP]), pos3[:, t, bass.ds(i, 1)],
                                 gat3[:, t, bass.ds(i, 1)], ALU.is_equal, ALU.mult)
                    ins.then_inc(S(f"{m}_pick_g"), 1)
                    if m == "m2":
                        dve.wait_ge(S("m2_biased"), i + 1)
                        expert(i + 1)
                    for q in range(4):
                        add(4 * i, q)
                    if m == "m1":
                        dve.wait_ge(S(f"{m}_act"), i + 1)
                        dve.wait_ge(S(f"{m}_free3"), i + 2)
                        tt(hid, act_g, U[:, :], ALU.mult).then_inc(S(f"{m}_hid"), 1)
                    else:
                        dve.wait_ge(S(f"{m}_free1"), i + 2)
                        ts(gate_1, G[:, :], LIMIT, None, ALU.min).then_inc(S(f"{m}_gate"), 1)
                        dve.wait_ge(S(f"{m}_act"), i + 1)
                        tt(gate_1, gate_1, act_g, ALU.mult).then_inc(S("m2_glu"), 1)
                        dve.wait_ge(S(f"{m}_free3"), i + 2)
                        ts(up_1, U[:, :], LIMIT, -LIMIT, ALU.min, ALU.max).then_inc(S("m2_up"), 1)
                        dve.wait_ge(S("m2_glu"), i + 1)
                        dve.wait_ge(S("m2_up"), i + 1)
                        stt(hid, up_1, 1.0, gate_1, ALU.add, ALU.mult).then_inc(S(f"{m}_hid"), 1)
                    dve.wait_ge(S(f"{m}_gathered"), i + 2)
                    gathered()
                    dve.wait_ge(S(f"{m}_turned"), i + 1)
                    v.tensor_copy(hidT, HT[:, :]).then_inc(S(f"{m}_hidT"), 1)
                    if m == "m2":
                        dve.wait_ge(S("m2_scaled"), i + 2)
                        shifted()
                    dve.wait_ge(S(f"{m}_put_ps"), i + 2)
                    v.tensor_copy(put, PT[:, 0:T]).then_inc(S(f"{m}_put"), 1)
                for q in range(4):
                    add(4 * n, q)
                dve.wait_ge(S(f"{m}_added"), 4 * n + 6)
                mark(dve.nop(), f"{m}_sum")

            choose("m1", rb1[:, :], pool[:, 7 * BUF:9 * BUF])
            block_table("m1")
            link(ts(B(2), B(0), ALPHA, None, ALU.mult))
            moe("m1")

            link(v.tensor_copy(B(0), B(2)))
            dve.wait_ge(S("ld_ln"), 64)
            layer_norm(x_rows, ln2, "x2_ready")
            ss = stat[:, 32:36]
            dve.wait_ge(*stage("ctx_ss"))
            rsqrt(ss[:, 0:2], 1.0 / D, RMS_EPS)
            for t in range(TC):
                link(ts(ctx_rows[:, t, :], ctx_rows[:, t, :], ss[:, t:t + 1], None, ALU.mult))
            mark(dve.nop(), "ctxn_ready")
            dve.wait_ge(*stage("x2_ss"))
            rsqrt(ss[:, 2:4], 1.0 / D, RMS_EPS)
            for t in range(TC):
                link(ts(xn_rows[:, t, :], x_rows[:, t, :], ss[:, 2 + t:3 + t], None, ALU.mult))
            mark(dve.nop(), "xn_ready")
            for cp in range(4):
                ps = tile(dve, ("lT", cp))
                for c in range(2):
                    k = 2 * cp + c
                    mark(ts(latT[:, k, :], ps[:, c * T:(c + 1) * T], sc1[:, 2 * k:2 * k + 1], mod[:, 2 * k:2 * k + 1],
                            ALU.mult, ALU.add), "latT_ready")
                freed(dve.nop(), ("lT", cp))

            dve.wait_ge(*stage("decay_log"))
            link(stt(lg[:, 0:8], decay[:, :], 0.0, lg[:, 8:16], ALU.min, ALU.subtract))
            link(ts(lg[:, 16:24], lg[:, 0:8], float(T), None, ALU.mult))
            link(ts(lg[:, 24:32], lg[:, 0:8], -1.0, None, ALU.mult))
            link(ts(lagf[:, :], C("lag"), 0.0, None, ALU.max))
            link(ts(lagb[:, :], C("lag"), -1.0, 0.0, ALU.mult, ALU.max))
            mark(dve.nop(), "lag_ready")

            def rope(dst, z, heads, f, cos, sin, tmp):
                w = 4 * f
                d4, z4, t4 = (x.rearrange("p (a t f) -> p a t f", t=2, f=f) for x in (dst, z, tmp))
                link(tt(dst.rearrange("p (h w) -> p h w", w=w), z.rearrange("p (h w) -> p h w", w=w),
                        cos.unsqueeze(1).to_broadcast([P, heads, w]), ALU.mult))
                for h in range(heads):
                    link(tt(t4[:, 2 * h:2 * h + 2, 0, :], z4[:, 2 * h:2 * h + 2, 1, :], sin, ALU.mult))
                    link(tt(t4[:, 2 * h:2 * h + 2, 1, :], z4[:, 2 * h:2 * h + 2, 0, :], sin, ALU.mult))
                link(tt(d4[:, :, 0, :], d4[:, :, 0, :], t4[:, :, 0, :], ALU.subtract))
                link(tt(d4[:, :, 1, :], d4[:, :, 1, :], t4[:, :, 1, :], ALU.add))

            rcos = C("rcos").rearrange("p (t w) -> p t w", t=TC)
            rsin = C("rsin").rearrange("p (t h f) -> p t h f", t=TC, h=2)
            for kind, dst in (("rq", rq_rows), ("rk", rk_rows)):
                for u in range(2):
                    for t in range(TC):
                        ps = tile(dve, (kind, u, t))
                        rope(dst[:, t, u * 512:(u + 1) * 512], ps[:, :], 2, 64, rcos[:, t, :], rsin[:, t], rope_tmp)
                        freed(dve.nop(), (kind, u, t))
                        mark(dve.nop(), "rotated")

            rss = stat[:, 36:44]
            for h in range(RH):
                dve.wait_ge(S("ret_decays"), h + 1)
                link(tt(dec[:, 0:2, :], dec[:, 0:2, :], dec2[:, 0:2, :], ALU.add))
                link(tt(dec[:, 2:4, :], dec[:, 2:4, :], dec2[:, 2:4, :], ALU.mult))
                for jp in range(2):
                    ps = tile(dve, ("S", h, jp))
                    mark(tt(dec2[:, 2 * jp:2 * jp + 2, :], two(ps), dec[:, 2 * jp:2 * jp + 2, :], ALU.mult), "ret_weights")
                    freed(dve.nop(), ("S", h, jp))
                dve.wait_ge(S("ret_ss"), 2 * h + 2)
                rsqrt(rss[:, 2 * h:2 * h + 2], 1.0 / RV, RMS_EPS)
                dve.wait_ge(S("ret_gate"), 2 * h + 2)
                for t in range(TC):
                    ps = tile(dve, ("ro", h, t))
                    r = ret[:, t, h * RV:(h + 1) * RV]
                    mark(stt(r, ps[:, :], rss[:, 2 * h + t:2 * h + t + 1], r, ALU.mult, ALU.mult), "ret_out")
                    freed(dve.nop(), ("ro", h, t))
                mark(dve.nop(), "ret_ready")

            mss = stat[:, 44:50]
            mcos = C("mcos").rearrange("p (t w) -> p t w", t=TC)
            msin = C("msin").rearrange("p (t h f) -> p t h f", t=TC, h=2)
            dve.wait_ge(S("mla_ss"), 6)
            rsqrt(mss[:, 0:2], 1.0 / QR, RMS_EPS)
            rsqrt(mss[:, 2:6], 1.0 / KVR, RMS_EPS)
            for t in range(TC):
                ps = tile(dve, ("cq", t))
                mark(ts(cqn[:, t, :], ps[:, 0:QR], mss[:, t:t + 1], None, ALU.mult), "cqn_ready")
                freed(dve.nop(), ("cq", t))
            for j in range(4):
                ps = tile(dve, ("ck", j))
                mark(ts(ckn[:, j, :], ps[:, 0:KVR], mss[:, 2 + j:3 + j], None, ALU.mult), "ckn_ready")
                if j < TC:
                    link(v.tensor_copy(kr2[:, j, 0:ROPE], ps[:, KVR:CKR]))
                else:
                    rope(kr2[:, j, 0:ROPE], ps[:, KVR:CKR], 1, 16, mcos[:, j - TC, :], msin[:, j - TC], mrope_tmp[:, 0:ROPE])
                freed(dve.nop(), ("ck", j))
                mark(v.tensor_copy(kr2[:, j, ROPE:2 * ROPE], kr2[:, j, 0:ROPE]), "kr_ready")

            dve.wait_ge(S("sig_gr_ready"), 4)
            for t in range(TC):
                for f in range(2):
                    ps = tile(dve, ("br", t, f))
                    c = slice(f * 512, (f + 1) * 512)
                    link(tt(merged[:, t, c], ps[:, :], sig_gr[:, t, c], ALU.mult))
                    freed(dve.nop(), ("br", t, f))

            q0, k0 = VEC["qng"][0], VEC["kvg"][0]
            for c in range(3):
                name = ("cqT", c // 2)
                ps = tile(dve, name)
                mark(ts(cqnT[:, c, :], ps[:, (c % 2) * T:(c % 2 + 1) * T], vecT[:, q0 + c:q0 + c + 1], None, ALU.mult),
                     "cqnT_ready")
                if c:
                    freed(dve.nop(), name)
            for c in range(2):
                ps = tile(dve, ("ckT", c))
                mark(ts(cknT[:, c, :], ps[:, :], vecT[:, k0 + c:k0 + c + 1], None, ALU.mult), "cknT_ready")
                freed(dve.nop(), ("ckT", c))
            ps = tile(dve, "krT")
            mark(v.tensor_copy(krT[:, :], ps[:, :]), "krT_ready")
            freed(dve.nop(), "krT")
            for u in range(2):
                for t in range(TC):
                    ps = tile(dve, ("qr", u, t))
                    rope(qr_rows[:, t, u * 256:(u + 1) * 256], ps[:, 0:256], 4, 16, mcos[:, t, :], msin[:, t], mrope_tmp)
                    freed(dve.nop(), ("qr", u, t))
                    mark(dve.nop(), "qr_ready")
            for j in range(4):
                for g in range(2):
                    ps = tile(dve, ("mv", j, g))
                    mark(v.tensor_copy(mv[j // 2][:, j % 2, g * 512:(g + 1) * 512], ps[:, :]), "mv_ready")
                    freed(dve.nop(), ("mv", j, g))

            mden, mnm = stat[:, 50:66], stat[:, 66:82]
            scale = (NOPE + ROPE) ** -0.5

            def mla_max(j):
                ps = tile(dve, ("s", j))
                link(v.tensor_reduce(mnm[:, j:j + 1], ps[:, :], AX_X, ALU.max))
                mark(ts(mnm[:, j:j + 1], mnm[:, j:j + 1], -scale, None, ALU.mult), "mla_max")

            mla_max(0)
            for j in range(MH * TC):
                if j + 1 < MH * TC:
                    mla_max(j + 1)
                dve.wait_ge(S("mla_exp"), j + 1)
                link(v.reciprocal(mden[:, j:j + 1], mden[:, j:j + 1]))
                mark(ts(mp[:, j % 2, :], mp[:, j % 2, :], mden[:, j:j + 1], None, ALU.mult), "mla_probs")
                if j >= TC and j % TC == 0:
                    tile(dve, ("mo", j // TC - 1))
                ps = tile(dve, ("mpT", j))
                t = j % TC
                mark(v.tensor_copy(mpT[:, :, t * P:(t + 1) * P], ps[:, :].rearrange("p (c q) -> p c q", c=4)), "mpT_ready")
                freed(dve.nop(), ("mpT", j))

            tile(dve, ("mo", MH - 1))
            for w, c0 in enumerate((16, 40)):
                i = tt(diag[:, 8 * w:8 * w + 8, :], ident.unsqueeze(1).to_broadcast([P, 8, P]), bcast(m3[:, c0:c0 + 8, 0], P),
                       ALU.mult)
                link(i)
            mark(dve.nop(), "diag_ready")

            dve.wait_ge(S("sig_gm_ready"), 4)
            for t in range(TC):
                for f in range(2):
                    ps = tile(dve, ("bm", t, f))
                    c = slice(f * 512, (f + 1) * 512)
                    link(tt(sig_gm[:, t, c], ps[:, :], sig_gm[:, t, c], ALU.mult))
                    freed(dve.nop(), ("bm", t, f))
                    mark(tt(merged[:, t, c], merged[:, t, c], sig_gm[:, t, c], ALU.add), "merged_ready")

            dve.wait_ge(S("bc_ready"), 4)
            for t in range(TC):
                for f in range(2):
                    ps = tile(dve, ("yo", t, f))
                    c = slice(f * 512, (f + 1) * 512)
                    link(tt(merged[:, t, c], ps[:, :], gate_bc[:, 0, c], ALU.mult))
                    freed(dve.nop(), ("yo", t, f))
                    link(tt(x_rows[:, t, c], x_rows[:, t, c], merged[:, t, c], ALU.add))
            mark(dve.nop(), "x3_ready")
            dve.wait_ge(*stage("x3_ss"))
            rsqrt(stat[:, 82:84], 1.0 / D, RMS_EPS)
            for t in range(TC):
                link(ts(n2_rows[:, t, :], x_rows[:, t, :], stat[:, 82 + t:83 + t], None, ALU.mult))
            mark(dve.nop(), "n2_ready")
            for cp in range(4):
                ps = tile(dve, ("nT", cp))
                for c in range(2):
                    k = 2 * cp + c
                    mark(ts(h2T[:, k, :], ps[:, c * T:(c + 1) * T], sc2[:, k:k + 1], mod[:, 48 + 2 * k:49 + 2 * k],
                            ALU.mult, ALU.add), "h2T_ready")
                freed(dve.nop(), ("nT", cp))
            choose("m2", rb2[:, :], pool[:, 2 * BUF:5 * BUF])
            block_table("m2")
            moe("m2")

            for t in range(TC):
                link(tt(y_acc[:, t, :], y_acc[:, t, :], gate_bc[:, 1, :], ALU.mult))
            link(tt(B(2), B(2), B(0), ALU.add))
            mark(dve.nop(), "x4_ready")
            dve.wait_ge(*stage("x4_ss"))
            rsqrt(stat[:, 84:86], 1.0 / D, RMS_EPS)
            dve.wait_ge(S("ld_fng"), 16)
            for t in range(TC):
                link(stt(y_acc[:, t, :], y_acc[:, t, :], stat[:, 84 + t:85 + t], fng, ALU.mult, ALU.mult))
            mark(dve.nop(), "out_ready")


_NAMES = ("x w_in g_sb g_dil w_out ln1_g ln1_b ln2_g ln2_b rel_bias w_router b_router w_gate w_up w_down c_2 ctx_2 c_ctx_2 "
          "norm1_g_2 norm2_g_2 ada_w_2 ada_b_2 w_in_2 ret_decay_fwd_2 ret_decay_bwd_2 mla_q_norm_g_2 mla_w_uq_2 "
          "mla_kv_norm_g_2 mla_w_ukv_2 w_branch_ret_2 w_branch_mla_2 w_out_2 router_w_2 router_b_2 exp_w_gu_2 exp_b_gu_2 "
          "exp_w_down_2 exp_b_down_2 final_norm_g_2").split()


def kernel(**inputs):
    import concourse.bacc as bacc
    from concourse.bass_utils import run_bass_kernel_spmd

    nc = bacc.Bacc("TRN2", target_bir_lowering=False, num_devices=1)
    arrays, aps = {}, {}
    for name in _NAMES:
        arrays["in_" + name] = v = np.ascontiguousarray(inputs[name])
        aps[name] = nc.dram_tensor("in_" + name, v.shape, F32, kind="ExternalInput").ap()
    arrays["shape_constants"] = CONSTS
    consts = nc.dram_tensor("shape_constants", CONSTS.shape, F32, kind="ExternalInput").ap()
    bias_rows = nc.dram_tensor("bias_rows", [HEADS, 384], F32, kind="Internal").ap()
    out = nc.dram_tensor("out", [1, T, D], F32, kind="ExternalOutput").ap()
    two_block_kernel(nc, aps, consts, bias_rows, out)
    got = run_bass_kernel_spmd(nc, [arrays], core_ids=[0])
    return got.results[0]["out"]
```

```python
import math
from contextlib import ExitStack

import numpy as np

import concourse.bass as bass
from concourse import mybir

F32 = mybir.dt.float32
I32 = mybir.dt.int32
ALU = mybir.AluOpType
ACT = mybir.ActivationFunctionType
AX_X = mybir.AxisListType.X

P = 128
T = 256
TC = T // P
D = 1024
KC = D // P
HD = 64
HEADS = 8
SLOTS = 6
SLOT = 4096
BUF = 2048
CAP = 64
FF = 1024
E1, TOP1, GRP = 16, 2, 4
E2, TOP2 = 32, 4
NB1 = E1 + T * TOP1 // CAP + 1
NB2 = E2 + T * TOP2 // CAP + 1
ALPHA = 2.0 ** 0.25
LN_EPS = 1e-5
RMS_EPS = 1e-6
NEG = -1e30
RH, RQK, RV = 4, 256, 512
MH, QR, KVR, NOPE, ROPE, MV = 8, 384, 256, 128, 64, 128
LIMIT, SWIGLU = 7.0, 1.702
OFF = dict(rq=0, rk=1024, rv=2048, rg=4096, cq=6144, ck=6528, gr=6848, gm=7872)
CKR = KVR + ROPE

DVE_STAGES = (
    "vec_ready bias_rows_ready y_sb_ready mod_ready y_ready ctxn_ready x1_ready m1_shifted m1_chosen m1_placed m1_laid m1_table "
    "m1_sum x2_ready xn_ready lag_ready krT_ready diag_ready x3_half x3_ready n2_ready m2_shifted m2_chosen "
    "m2_placed m2_laid m2_table m2_sum x4_half x4_ready out_half out_ready").split()
ACT_STAGES = (
    "silc_ready ctx_ss m1_exp x2_ss decay_log x3_ss m2_exp x4_ss").split()

VEC = {}
_row = 0
for _name, _rows in (("g_sb", 4), ("g_dil", 4), ("n1g", 8), ("n2g", 8), ("qng", 3), ("kvg", 2), ("c", 8),
                     ("cctx", 8), ("ada_b", 48)):
    VEC[_name] = (_row, _row + _rows)
    _row += _rows
NVEC = _row


def shape_constants():
    f = np.float32
    p = np.arange(P)
    parts = {}
    parts["ident"] = np.eye(P)
    parts["flip"] = np.eye(P)[::-1]
    parts["suffix"] = (p[:, None] >= p[None, :])
    parts["before"] = (p[:, None] < p[None, :])
    parts["ones"] = np.ones((P, P))
    strict = np.where(p[:, None] < p[None, :], 0.0, NEG)
    parts["sb_mask"] = np.concatenate([strict, np.zeros((P, P)), strict], axis=1)
    j = np.arange(384)
    dist = 255 - j
    exact = 16
    big = exact + (np.log(np.maximum(dist, 1).astype(f) / f(exact)) / f(math.log(2048 / exact)) * f(16)).astype(np.int32)
    bucket = np.where(dist < exact, np.maximum(dist, 0), np.minimum(big, 31))
    count = np.where(dist >= 0, (dist <= 128).astype(int) + (dist % 4 == 0) + (dist % 16 == 0), 0)
    hot = np.zeros((P, 384))
    hot[bucket, j] = count > 0
    hot[32] = np.where(count > 0, np.log(np.maximum(count, 1)), NEG)
    parts["bias_hot"] = hot
    parts["iota"] = np.broadcast_to(np.arange(P), (P, P))
    parts["pidx"] = p[:, None]
    parts["fold"] = p[:, None] % 32 == np.arange(32)[None, :]
    parts["lag"] = j[None, :] - P - p[:, None]
    tok = np.arange(T)
    pos = np.stack([tok // 64, tok % 64])

    def rope(half):
        freq = f(10000.0) ** (-np.arange(half, dtype=f) / f(half))
        ang = pos.astype(f)[:, :, None] * freq
        cos = np.cos(ang).transpose(1, 0, 2).reshape(TC, P, 2, 1, half)
        sin = np.sin(ang).transpose(1, 0, 2).reshape(TC, P, 2, half)
        cos = np.broadcast_to(cos, (TC, P, 2, 2, half))
        return (cos.transpose(1, 0, 2, 3, 4).reshape(P, -1), sin.transpose(1, 0, 2, 3).reshape(P, -1))

    parts["rcos"], parts["rsin"] = rope(64)
    parts["mcos"], parts["msin"] = rope(16)
    where, at = {}, 0
    for name, a in parts.items():
        where[name] = (at, at + a.shape[1])
        at += a.shape[1]
    return np.ascontiguousarray(np.concatenate([np.asarray(a, f) for a in parts.values()], axis=1)), where


CONSTS, CAT = shape_constants()


def two_block_kernel(nc, a, consts, bias_rows, out):
    with ExitStack() as ctx:
        def sb(name, cols, dt=F32):
            return ctx.enter_context(nc.sbuf_tensor(name, [P, cols], dt))

        sems = {}

        def S(name):
            if name not in sems:
                sems[name] = ctx.enter_context(nc.semaphore(name))
            return sems[name]

        def stage(name):
            if name in DVE_STAGES:
                return S("dve_stage"), DVE_STAGES.index(name) + 1
            return S("act_stage"), ACT_STAGES.index(name) + 1

        ring = sb("ring", SLOTS * SLOT)
        pool = sb("pool", 11 * BUF)
        cst = sb("cst", CONSTS.shape[1])
        vecT = sb("vecT", NVEC)
        rel33 = sb("rel33", HEADS)
        rw1 = sb("rw1", KC * 32)
        rw2 = sb("rw2", KC * 32)
        rb1 = sb("rb1", E1)
        rb2 = sb("rb2", E2)
        decay = sb("decay", 2 * RH)
        lg = sb("lg", 8 * 2 * RH)
        mod = sb("mod", 96)
        sc1 = sb("sc1", 16)
        sc2 = sb("sc2", 8)
        misc = sb("misc", 768)
        stat = sb("stat", 112)
        root = sb("root", 32)
        power = sb("power", 32)
        posb = sb("posb", TC * NB2)
        gateb = sb("gateb", TC * NB2)
        junk = sb("junk", 512)
        table = sb("table", NB2 + 1, I32)
        banks = [ctx.enter_context(nc.psum_tensor(f"bank{i}", [P, 512], F32)) for i in range(8)]

        def C(name, rows=P):
            lo, hi = CAT[name]
            return cst[0:rows, lo:hi]

        def B(i, cols=BUF, at=0):
            return pool[:, i * BUF + at:i * BUF + at + cols]

        def slot(phase, n):
            at = (FIRST_SLOT[phase] + n) % SLOTS
            return ring[:, at * SLOT:(at + 1) * SLOT]

        bias8, lagf, lagb, krT = misc[:, 0:384], misc[:, 0:384], misc[:, 384:768], misc[:, 0:512]
        vrows = junk[:, 0:P]
        silc = junk[:, T:2 * T].rearrange("p (k v) -> p k v", k=KC)

        ident, ones, before, suffix, flip = C("ident"), C("ones"), C("before"), C("suffix"), C("flip")

        x_rows = B(0).rearrange("p (t d) -> p t d", t=TC)
        xT = B(1).rearrange("p (k t) -> p k t", k=KC)
        qk_sb = [B(2, 1024, 1024 * i).rearrange("p (m t) -> p m t", m=4) for i in range(2)]
        qk_dl = [B(3, 1024, 1024 * i).rearrange("p (m t) -> p m t", m=4) for i in range(2)]
        v_sb, v_dl = (B(4, 1024, 1024 * i).rearrange("p (t c) -> p t c", t=TC) for i in range(2))
        hankel = B(5).rearrange("p (h k) -> p h k", h=HEADS)
        y_rows = B(6).rearrange("p (t d) -> p t d", t=TC)
        yT = B(7).rearrange("p (k t) -> p k t", k=KC)
        ada_rows = B(1, 1536)
        sb_work = pool[:, 8 * BUF:11 * BUF].rearrange("p (b w c) -> p b w c", b=2, w=4)
        dl_p = B(8, 768).rearrange("p (b c) -> p b c", b=2)
        dl_pT = B(8, 768, 768).rearrange("p (b c) -> p b c", b=2)
        ln1 = B(9).rearrange("p (w d) -> p w d", w=2)
        ln2 = B(10).rearrange("p (w d) -> p w d", w=2)

        y_sum = {"m1": B(5), "m2": B(2)}
        y_acc = {m: y.rearrange("p (t d) -> p t d", t=TC) for m, y in y_sum.items()}
        xgT = B(3, 512).rearrange("p (k s) -> p k s", k=KC)
        hidT = B(3, 512, 512)
        act_g = B(3, 512, 1024)
        pick = B(3, 128, 1536).rearrange("p (t s) -> p t s", t=TC)
        pick_g = B(3, 256, 1664).rearrange("p (t f s) -> p t f s", t=TC, f=2)
        y_slot, hid, up_1, gate_1 = (B(4, 512, 512 * i) for i in range(4))
        put = junk[:, 0:T]
        lgT = junk[:, 0:T]
        this_expert = junk[0:E2, T:T + CAP]

        ctx_rows = B(3).rearrange("p (t d) -> p t d", t=TC)
        xn_rows = B(8).rearrange("p (t d) -> p t d", t=TC)
        latT = B(1).rearrange("p (k t) -> p k t", k=KC)
        ctxT = B(2).rearrange("p (k t) -> p k t", k=KC)
        rq_rows = B(3).rearrange("p (t d) -> p t d", t=TC)
        rk_rows = B(9).rearrange("p (t d) -> p t d", t=TC)
        rqT = B(4).rearrange("p (c t) -> p c t", c=8)
        rkT = pool[:, 5 * BUF:7 * BUF].rearrange("p (c t) -> p c t", c=8)
        rv = [B(7 + i).rearrange("p (j c) -> p j c", j=4) for i in range(2)]
        dec = B(3, 1024).rearrange("p (j t) -> p j t", j=4)
        dec2 = B(3, 1024, 1024).rearrange("p (j t) -> p j t", j=4)
        ret = pool[:, 9 * BUF:11 * BUF].rearrange("p (t c) -> p t c", t=TC)
        rope_tmp = B(7, 512)
        sig_gr = B(5).rearrange("p (t d) -> p t d", t=TC)
        sig_gm = B(1).rearrange("p (t d) -> p t d", t=TC)
        retT = pool[:, 7 * BUF:9 * BUF].rearrange("p (c t) -> p c t", c=16)
        merged = B(6).rearrange("p (t d) -> p t d", t=TC)
        cqn = B(3, 768).rearrange("p (t c) -> p t c", t=TC)
        ckn = B(3, 1024, 768).rearrange("p (j c) -> p j c", j=4)
        kr2 = B(4, 512).rearrange("p (j c) -> p j c", j=4)
        mrope_tmp = B(4, 256, 512)
        cqnT = B(4, 768, 1024).rearrange("p (c t) -> p c t", c=3)
        cknT = B(2, 1024).rearrange("p (c t) -> p c t", c=2)
        qnT = B(7).rearrange("p (h t) -> p h t", h=MH)
        qr_rows = B(8, 1024).rearrange("p (t c) -> p t c", t=TC)
        qrT = B(8, 1024, 1024).rearrange("p (m t) -> p m t", m=4)
        knT = pool[:, 9 * BUF:11 * BUF].rearrange("p (h t) -> p h t", h=MH)
        mv = [B(3).rearrange("p (j c) -> p j c", j=2), B(5).rearrange("p (j c) -> p j c", j=2)]
        mp = B(2, 1024, 1024).rearrange("p (b c) -> p b c", b=2)
        mpT = [B(i, 1024).rearrange("p (j t) -> p j t", j=4) for i in (8, 2)]
        mT = B(4).rearrange("p (h t) -> p h t", h=MH)
        mergedT = B(2).rearrange("p (k t) -> p k t", k=KC)
        diag = B(10).rearrange("p (k c) -> p k c", k=16)
        gate_bc = B(7).rearrange("p (w d) -> p w d", w=2)
        n2_rows = B(1).rearrange("p (t d) -> p t d", t=TC)
        h2T = B(5).rearrange("p (k t) -> p k t", k=KC)
        bgu_rows = pool[0:E2, 8 * BUF:9 * BUF]
        bdn_rows = pool[0:E2, 9 * BUF:9 * BUF + 1024]
        fng = B(10, 1024)

        def cols(w, at, n):
            return w[:, at:at + n].rearrange("(k p) f -> p k f", p=P)

        def rows4(w, u):
            return w[u * 512:(u + 1) * 512, :].rearrange("(k p) f -> p k f", p=P)

        def part(phase, n, k, f):
            return slot(phase, n)[:, 0:k * f].rearrange("p (k f) -> p k f", k=k)

        units_a = [(cols(a["w_in"][0], 512 * u, 512), 8, 512) for u in range(6)]
        units_a += [(cols(a["ada_w_2"][0], 512 * u, 512), 8, 512) for u in range(12)]
        units_a += [(rows4(a["w_out"][0], u), 4, 1024) for u in range(2)]
        ADA0, WOUT0 = 6, 18
        w2 = a["w_in_2"][0]
        units_b, UB = [], {}

        def unit_b(name, src, k, f):
            UB[name] = len(units_b)
            units_b.append((src, k, f))

        for n in ("rk", "rq"):
            for u in range(2):
                unit_b((n, u), cols(w2, OFF[n] + 512 * u, 512), 8, 512)
        for h in range(RH):
            unit_b(("rv", h), cols(w2, OFF["rv"] + RV * h, RV), 8, RV)
            unit_b(("rg", h), cols(w2, OFF["rg"] + RV * h, RV), 8, RV)
        for u in range(2):
            unit_b(("gr", u), cols(w2, OFF["gr"] + 512 * u, 512), 8, 512)
        unit_b("cq", cols(w2, OFF["cq"], QR), 8, QR)
        unit_b("ck", cols(w2, OFF["ck"], CKR), 8, CKR)
        for u in range(2):
            unit_b(("gm", u), cols(w2, OFF["gm"] + 512 * u, 512), 8, 512)
        for u in range(4):
            unit_b(("br", u), rows4(a["w_branch_ret_2"][0], u), 4, 1024)
        for u in range(2):
            unit_b(("uq", u), cols(a["mla_w_uq_2"][0], 768 * u, 768), 3, 768)
        unit_b("ukv", cols(a["mla_w_ukv_2"][0], 0, 2048), 2, 2048)
        for u in range(2):
            unit_b(("bm", u), rows4(a["w_branch_mla_2"][0], u), 4, 1024)
        for u in range(2):
            unit_b(("wo", u), rows4(a["w_out_2"][0], u), 4, 1024)

        def moe_units(m, e):
            if m == "m1":
                cut = [(w, 0) for w in (a["w_gate"][0], a["w_up"][0], a["w_down"][0])]
            else:
                cut = [(a["exp_w_gu_2"][0], 0), (a["exp_w_gu_2"][0], FF), (a["exp_w_down_2"][0], 0)]
            return [w[bass.ds(e, 1), 512 * i:512 * i + 512, lo:lo + 1024].rearrange("o (k p) f -> p (o k) f", p=P)
                    for w, lo in cut for i in range(2)]

        MOE = {"m1": (E1, NB1), "m2": (E2, NB2)}
        FIRST_SLOT = {"a": 0, "m1": len(units_a), "b": len(units_a), "m2": len(units_a) + len(units_b)}

        def scratch_of(m):
            return B(5) if m == "m1" else B(6)

        def rt_logits(m):
            return scratch_of(m)[:, 1024:1024 + TC * MOE[m][0]]

        def route_parts(m):
            E, NB = MOE[m]
            at = 0
            got = []
            for rows, n in ((P, 2 * E), (P, 2 * E), (P, 2 * E), (E, 1), (E, T), (E, T), (E, NB), (E, NB)):
                got.append(scratch_of(m)[0:rows, at:at + n])
                at += n
            return got

        tiles, uses, turn = {}, [0] * 8, [0]

        def open_tile(pe, name, bank=None, among=8):
            if bank is None:
                bank = turn[0] % among
                turn[0] += 1
            tiles[name] = (bank, uses[bank])
            if uses[bank]:
                pe.wait_ge(S(f"bank_free{bank}"), uses[bank])
            uses[bank] += 1
            return banks[bank]

        def filled(ins, name):
            ins.then_inc(S(f"bank_full{tiles[name][0]}"), 1)

        def tile(eng, name):
            bank, use = tiles[name]
            eng.wait_ge(S(f"bank_full{bank}"), use + 1)
            return banks[bank]

        unit_done, counted = {}, {"a": 0, "b": 0}

        def multiplied(phase, n, by):
            if by in tiles:
                unit_done[phase, n] = (S(f"bank_full{tiles[by][0]}"), tiles[by][1] + 1)
            else:
                counted[phase] += 1
                by.then_inc(S(f"{phase}_used"), 1)
                unit_done[phase, n] = (S(f"{phase}_used"), counted[phase])

        def freed(ins, name):
            ins.then_inc(S(f"bank_free{tiles[name][0]}"), 1)

        block = ctx.enter_context(nc.Block())

        @block.tensor
        def _(pe):
            mm = nc.tensor.matmul
            tp = nc.tensor.transpose

            def landed(phase, n):
                pe.wait_ge(S(f"{phase}_full{n % SLOTS}"), 16 * (n // SLOTS + 1))

            def transposes(name, src, pairs, among=8, first=0, at=None):
                for cp in range(first, first + pairs):
                    ps = open_tile(pe, (name, cp), bank=None if at is None else at[cp - first], among=among)
                    for c in range(2):
                        for t in range(TC):
                            i = tp(ps[:, c * T + t * P:c * T + t * P + P],
                                   src[:, t, (2 * cp + c) * P:(2 * cp + c + 1) * P], ident)
                    filled(i, (name, cp))

            def by_columns(name, phase, n, w, src, among=8, last=True):
                landed(phase, n)
                for mp_ in range(2):
                    ps = open_tile(pe, (name, mp_), among=among)
                    for m in range(2):
                        for k in range(KC):
                            i = mm(ps[:, m * T:(m + 1) * T], w[:, k, (2 * mp_ + m) * P:(2 * mp_ + m + 1) * P],
                                   src[:, k, :], start=(k == 0), stop=(k == KC - 1))
                    filled(i, (name, mp_))
                if last:
                    multiplied(phase, n, (name, 1))

            def by_rows(names, phase, n, w, srcs, width, among=8, last=True):
                landed(phase, n)
                for name, (src, t) in zip(names, srcs):
                    ps = open_tile(pe, name, among=among)
                    for k in range(w.shape[1]):
                        i = mm(ps[:, 0:width], src[:, k, t * P:(t + 1) * P], w[:, k, 0:width],
                               start=(k == 0), stop=(k == w.shape[1] - 1))
                    filled(i, name)
                if last:
                    multiplied(phase, n, names[-1])

            def down_proj(name, phase, n0, units, srcT, among=8, before_last=None):
                ps = {(t, f): open_tile(pe, (name, t, f), among=among) for t in range(TC) for f in range(2)}
                for u in range(units):
                    if before_last and u == units - 1:
                        before_last()
                    landed(phase, n0 + u)
                    w = part(phase, n0 + u, 4, 1024)
                    for k in range(4):
                        kk = 4 * u + k
                        for t in range(TC):
                            for f in range(2):
                                i = mm(ps[t, f][:, :], srcT[:, kk, t * P:(t + 1) * P], w[:, k, f * 512:(f + 1) * 512],
                                       start=(kk == 0), stop=(kk == 4 * units - 1))
                                if kk == 4 * units - 1:
                                    filled(i, (name, t, f))
                    multiplied(phase, n0 + u, i if u < units - 1 else (name, 1, 1))

            pe.wait_ge(S("ld_x"), 16)
            pe.wait_ge(S("ld_ident"), 16)
            transposes("xT", x_rows, 4, among=4)

            pe.wait_ge(S("xT_ready"), 4)
            def small_vectors():
                pe.wait_ge(S("ld_const"), 16)
                pe.wait_ge(S("ld_vec"), 16 * 9)
                ps = open_tile(pe, "vec", among=4)
                filled(tp(ps[:, 0:NVEC], vrows[0:NVEC, :], ident[0:NVEC, 0:NVEC]), "vec")
                pe.wait_ge(S("ld_rel"), 16)
                pe.wait_ge(S("root_set"), 4)
                ps = open_tile(pe, "rel", among=4)
                filled(mm(ps[0:HEADS, 0:384], rel33[0:33, :], C("bias_hot", 33), start=True, stop=True), "rel")

            def sb_logits(p):
                heads = [(h, open_tile(pe, ("z", h), among=4), *(w[HD * (h % 2):HD * (h % 2 + 1), p, :] for w in qk_sb))
                         for h in (2 * p, 2 * p + 1)]
                for h, ps, q, k in heads:
                    mm(ps[:, 0:256], k[:, 0:128], q[:, :], start=True, stop=True)
                for h, ps, q, k in heads:
                    filled(mm(ps[:, 256:384], k[:, 128:256], q[:, 128:256], start=True, stop=True), ("z", h))

            for u, kind in enumerate(("q_sb", "k_sb", "v_sb", "q_dl", "k_dl", "v_dl")):
                w = part("a", u, KC, 512)
                if kind == "v_dl":
                    pe.wait_ge(S("qk_ready"), 4)
                    sb_logits(0)
                if kind[0] == "v":
                    by_rows([(kind, t) for t in range(TC)], "a", u, w, [(xT, t) for t in range(TC)], 512, among=4)
                else:
                    by_columns(kind, "a", u, w, xT, among=4)
                if kind == "v_sb":
                    small_vectors()

            def ada_round(q):
                if q == 0:
                    pe.wait_ge(*stage("silc_ready"))
                ps = open_tile(pe, ("ada", q), bank=4)
                units = [ADA0 + 4 * q + g for g in range(4)]
                for n in units:
                    landed("a", n)
                for k in range(KC):
                    for g, n in enumerate(units):
                        i = mm(ps[32 * g:32 * (g + 1), :], silc[:, k, :], part("a", n, KC, 512)[:, k, :],
                               start=(k == 0), stop=(k == KC - 1))
                        if k == KC - 1 and g == 3:
                            filled(i, ("ada", q))
                        if k == KC - 1:
                            multiplied("a", n, i if g < 3 else ("ada", q))

            def ada_turn(q):
                pe.wait_ge(S("ada_rows"), q + 1)
                ps = open_tile(pe, ("adaT", q), among=4)
                for c in range(4):
                    i = tp(ps[:, c * P:(c + 1) * P], ada_rows[:, (4 * q + c) * P:(4 * q + c + 1) * P], ident)
                filled(i, ("adaT", q))

            pe.wait_ge(S("v_ready"), 2)

            def sb_suffix(p):
                pe.wait_ge(S("sb_softplus"), p + 1)
                for j, h in enumerate((2 * p, 2 * p + 1)):
                    sp = sb_work[:, p % 2, 2, j * 384:(j + 1) * 384]
                    ps = open_tile(pe, ("R", h), among=4)
                    mm(ps[:, 0:256], suffix, sp[:, 0:256], start=True, stop=False, skip_group_check=True)
                    mm(ps[:, 128:256], ones, sp[:, 256:384], start=False, stop=False, skip_group_check=True)
                    filled(mm(ps[:, 256:384], suffix, sp[:, 256:384], start=False, stop=True, skip_group_check=True),
                           ("R", h))

            sb_o = [open_tile(pe, ("sb_o", t), bank=6 + t) for t in range(TC)]

            def sb_values(p):
                pe.wait_ge(S("sb_weights"), p + 1)
                for j, h in enumerate((2 * p, 2 * p + 1)):
                    w = sb_work[:, p % 2, 3, j * 384:(j + 1) * 384]
                    c = slice(h * HD, (h + 1) * HD)
                    i0 = mm(sb_o[0][:, c], w[:, 0:128], v_sb[:, 0, c], start=True, stop=True)
                    if h == HEADS - 1:
                        filled(i0, ("sb_o", 0))
                    mm(sb_o[1][:, c], w[:, 128:256], v_sb[:, 0, c], start=True, stop=False)
                    i1 = mm(sb_o[1][:, c], w[:, 256:384], v_sb[:, 1, c], start=False, stop=True)
                if p < 3:
                    i1.then_inc(S("sb_values_done"), 1)
                else:
                    filled(i1, ("sb_o", 1))

            for p in range(4):
                if p < 3:
                    sb_logits(p + 1)
                if p % 2:
                    ada_round(p // 2)
                sb_suffix(p)
                if p > 0:
                    sb_values(p - 1)
            sb_values(3)

            pe.wait_ge(S("qk_ready"), 8)
            pe.wait_ge(S("v_ready"), 4)
            pe.wait_ge(S("ld_hankel"), 16)

            def dl_logits(h):
                lo = HD * (h % 2)
                q, k = (w[lo:lo + HD, h // 2, :] for w in qk_dl)
                ps = open_tile(pe, ("L", h), among=4)
                mm(ps[:, 0:256], q[:, 128:256], k[:, :], start=True, stop=False)
                mm(ps[:, 0:256], flip, hankel[:, h, :], start=False, stop=True)
                mm(ps[:, 256:384], q[:, 0:128], k[:, 0:128], start=True, stop=False)
                filled(mm(ps[:, 256:384], flip, hankel[:, h, 128:256], start=False, stop=True), ("L", h))

            def dl_turn(h):
                pe.wait_ge(S("dl_exp"), 2 * (h + 1))
                ps = open_tile(pe, ("pT", h), among=4)
                for j in range(3):
                    i = tp(ps[:, j * P:(j + 1) * P], dl_p[:, h % 2, j * P:(j + 1) * P], ident)
                filled(i, ("pT", h))

            dl_o = [open_tile(pe, ("dl_o", t), bank=(5, 7)[t]) for t in range(TC)]

            def dl_values(h):
                pe.wait_ge(S("dl_pT_ready"), h + 1)
                c = slice(h * HD, (h + 1) * HD)
                w = dl_pT[:, h % 2, :]
                mm(dl_o[1][:, c], w[:, 0:128], v_dl[:, 0, c], start=True, stop=False)
                i1 = mm(dl_o[1][:, c], w[:, 128:256], v_dl[:, 1, c], start=False, stop=True)
                i0 = mm(dl_o[0][:, c], w[:, 256:384], v_dl[:, 0, c], start=True, stop=True)
                if h < HEADS - 1:
                    i0.then_inc(S("dl_values_done"), 1)
                else:
                    filled(i1, ("dl_o", 1))
                    filled(i0, ("dl_o", 0))

            dl_logits(0)
            for h in range(HEADS + 1):
                if h == 3:
                    ada_round(2)
                if h + 1 < HEADS:
                    dl_logits(h + 1)
                if h < HEADS:
                    dl_turn(h)
                if h > 0:
                    dl_values(h - 1)

            for q in range(3):
                ada_turn(q)
            pe.wait_ge(*stage("y_sb_ready"))
            transposes("yT", y_rows, 2, among=4)
            pe.wait_ge(S("yT_ready"), 4)

            def dilated_half():
                pe.wait_ge(*stage("y_ready"))
                transposes("yT", y_rows, 2, first=2, at=(4, 6))
                pe.wait_ge(S("yT_ready"), 8)

            down_proj("wo1", "a", WOUT0, 2, yT, among=4, before_last=dilated_half)
            pe.wait_ge(*stage("ctxn_ready"))
            transposes("cT", ctx_rows, 4, among=4)
            pe.wait_ge(*stage("x1_ready"))
            transposes("x1T", x_rows, 4, among=4)

            def router(m, srcT, ready, n, w):
                E, _ = MOE[m]
                pe.wait_ge(S(ready), n)
                pe.wait_ge(S("ld_router"), 16 * 6)
                ps = open_tile(pe, (m, "lgT"))
                for k in range(KC):
                    g = k % 4
                    i = mm(ps[32 * g:32 * (g + 1), 0:T], w[:, k * 32:(k + 1) * 32], srcT[:, k, :], start=(k < 4), stop=(k >= 4))
                filled(i, (m, "lgT"))
                pe.wait_ge(S("route_out"), 1 if m == "m1" else 2)
                ps = open_tile(pe, (m, "logits"))
                for t in range(TC):
                    i = mm(ps[:, t * E:(t + 1) * E], lgT[:, t * P:(t + 1) * P], C("fold")[:, 0:E], start=True, stop=True)
                filled(i, (m, "logits"))

            def block_table(m):
                E, NB = MOE[m]
                sel, gate, posm, nb, selT, gateT, bsel, rnd = route_parts(m)
                pe.wait_ge(*stage(f"{m}_chosen"))
                ps = open_tile(pe, (m, "pos"))
                mm(ps[:, 0:E], before, sel[:, 0:E], start=True, stop=True)
                mm(ps[:, E:2 * E], ones, sel[:, 0:E], start=True, stop=False)
                filled(mm(ps[:, E:2 * E], before, sel[:, E:2 * E], start=False, stop=True), (m, "pos"))
                ps = open_tile(pe, (m, "count"))
                mm(ps[0:E, 0:1], sel[:, 0:E], ones[:, 0:1], start=True, stop=False)
                filled(mm(ps[0:E, 0:1], sel[:, E:2 * E], ones[:, 0:1], start=False, stop=True), (m, "count"))
                pe.wait_ge(*stage(f"{m}_placed"))
                ps = open_tile(pe, (m, "turned"))
                for t in range(TC):
                    tp(ps[0:E, t * P:(t + 1) * P], posm[:, t * E:(t + 1) * E], ident)
                    i = tp(ps[0:E, T + t * P:T + (t + 1) * P], gate[:, t * E:(t + 1) * E], ident)
                filled(i, (m, "turned"))
                ps = open_tile(pe, (m, "start"))
                filled(mm(ps[0:E, 0:1], before[0:E, 0:E], nb, start=True, stop=True), (m, "start"))
                ps = open_tile(pe, (m, "blocks"))
                filled(mm(ps[0:1, 0:1], nb, ones[0:E, 0:1], start=True, stop=True), (m, "blocks"))
                pe.wait_ge(*stage(f"{m}_laid"))
                ps = open_tile(pe, (m, "posb"))
                for t in range(TC):
                    mm(ps[:, t * NB:(t + 1) * NB], selT[:, t * P:(t + 1) * P], bsel, start=True, stop=False)
                    i = mm(ps[:, t * NB:(t + 1) * NB], ones[0:E, :], rnd, start=False, stop=True)
                filled(i, (m, "posb"))
                ps = open_tile(pe, (m, "gateb"))
                for t in range(TC):
                    i = mm(ps[:, t * NB:(t + 1) * NB], gateT[:, t * P:(t + 1) * P], bsel, start=True, stop=True)
                filled(i, (m, "gateb"))
                ps = open_tile(pe, (m, "experts"))
                filled(mm(ps[0:1, 0:NB], C("pidx", E), bsel, start=True, stop=True), (m, "experts"))
                if m == "m2":
                    pe.wait_ge(S("ld_moe_bias"), 32)
                    for t in range(TC):
                        for f in range(2):
                            ps = open_tile(pe, (m, "bdown", t, f))
                            filled(mm(ps[:, :], gateT[:, t * P:(t + 1) * P], bdn_rows[:, f * 512:(f + 1) * 512],
                                      start=True, stop=True), (m, "bdown", t, f))

            def moe(m, src):
                XG, G, U, DN, Y0, Y1, PT, HT = banks
                for b in range(8):
                    pe.wait_ge(S(f"bank_free{b}"), uses[b])
                pe.wait_ge(*stage(f"{m}_table"))
                n = pe.value_load(table[0:1, NB2:NB2 + 1], min_val=1, max_val=MOE[m][1] - 1)
                full = [S(f"{m}_full{j}") for j in range(SLOTS)]
                free = [S(f"{m}_free{j}") for j in range(SLOTS)]
                weights = [part(m, j, 4, 1024) for j in range(SLOTS)]
                half = [slice(f * CAP, (f + 1) * CAP) for f in range(2)]

                def gather():
                    for k in range(KC):
                        for t in range(TC):
                            i = mm(XG[:, k * CAP:(k + 1) * CAP], src[:, t, k * P:(k + 1) * P], pick[:, t, :],
                                   start=(t == 0), stop=(t == TC - 1))
                    i.then_inc(S(f"{m}_gathered"), 1)

                def biases():
                    for w, dst in ((0, G), (1, U)):
                        for f in range(2):
                            at = w * FF + f * 512
                            i = mm(dst[half[f], :], this_expert, bgu_rows[:, at:at + 512], start=True, stop=False)
                    i.then_inc(S(f"{m}_biased"), 1)

                def product(dst, chunks, j, biased=False):
                    for k in range(4):
                        kk = 4 * (j % 2) + k
                        for f in range(2):
                            i = mm(dst[half[f], :], chunks[kk], weights[j][:, k, f * 512:(f + 1) * 512],
                                   start=(kk == 0 and not biased), stop=(kk == KC - 1))
                    i.then_inc(free[j], 1)

                def scatter(before_):
                    for q in range(4):
                        t, f = q // 2, q % 2
                        pe.wait_ge(S(f"{m}_added"), before_ + q + 1)
                        mm((Y0, Y1)[f][:, :], put[half[f], t * P:(t + 1) * P], y_slot[half[f], :],
                           start=True, stop=True).then_inc(S(f"{m}_scattered"), 1)

                token_chunks = [xgT[:, k, :] for k in range(KC)]
                hid_chunks = [hidT[:, c * P + f * CAP:c * P + (f + 1) * CAP] for f in range(2) for c in range(4)]
                biased = m == "m2"
                for j in range(SLOTS):
                    pe.nop().then_inc(free[j], 1)
                pe.nop().then_inc(S(f"{m}_put_ps"), 1)
                pe.wait_ge(S(f"{m}_pick"), 1)
                gather()
                with pe.Fori(0, n) as i:
                    if biased:
                        pe.wait_ge(S(f"{m}_expert"), i + 1)
                        biases()
                    pe.wait_ge(S(f"{m}_xgT"), i + 1)
                    pe.wait_ge(full[0], 16 * i + 16)
                    product(G, token_chunks, 0, biased)
                    pe.wait_ge(S(f"{m}_y_slot"), i + 1)
                    pe.wait_ge(S(f"{m}_put"), i + 1)
                    scatter(4 * i)
                    pe.wait_ge(full[1], 16 * i + 16)
                    product(G, token_chunks, 1, biased)
                    for j in (2, 3):
                        pe.wait_ge(full[j], 16 * i + 16)
                        product(U, token_chunks, j, biased)
                    pe.wait_ge(S(f"{m}_pick"), i + 2)
                    gather()
                    pe.wait_ge(S(f"{m}_hid"), i + 2)
                    for c in range(4):
                        ins = tp(HT[:, c * P:(c + 1) * P], hid[:, c * P:(c + 1) * P], ident)
                    ins.then_inc(S(f"{m}_turned"), 1)
                    pe.wait_ge(S(f"{m}_pick_g"), i + 1)
                    for t in range(TC):
                        ins = tp(PT[:, t * P:(t + 1) * P], pick_g[:, t, :, :], ident)
                    ins.then_inc(S(f"{m}_put_ps"), 1)
                    pe.wait_ge(S(f"{m}_hidT"), i + 1)
                    for j in (4, 5):
                        pe.wait_ge(full[j], 16 * i + 16)
                        product(DN, hid_chunks, j)
                pe.wait_ge(S(f"{m}_y_slot"), n + 1)
                pe.wait_ge(S(f"{m}_put"), n + 1)
                scatter(4 * n)
                pe.wait_ge(*stage(f"{m}_sum"))

            router("m1", xT, "x1T_ready", 4, rw1)
            block_table("m1")
            moe("m1", x_rows)

            pe.wait_ge(S("ctxT_ready"), 8)
            for u in range(2):
                n = UB["rk", u]
                by_columns(("kc", u), "b", n, part("b", n, KC, 512), ctxT, last=False)
            pe.wait_ge(*stage("xn_ready"))
            transposes("lT", xn_rows, 4)
            pe.wait_ge(S("latT_ready"), 8)
            for kind in ("rk", "rq"):
                for u in range(2):
                    n = UB[kind, u]
                    by_rows([(kind, u, t) for t in range(TC)], "b", n, part("b", n, KC, 512), [(latT, t) for t in range(TC)],
                            512)
            pe.wait_ge(S("rotated"), 4)
            transposes("rkT", rk_rows, 4)
            pe.wait_ge(S("rotated"), 8)
            transposes("rqT", rq_rows, 4)
            pe.wait_ge(S("rkT_ready"), 8)
            pe.wait_ge(S("rqT_ready"), 4)
            both = [(ctxT, 0), (ctxT, 1), (latT, 0), (latT, 1)]
            for h in range(RH):
                n = UB["rv", h]
                by_rows([("rv", h, j) for j in range(4)], "b", n, part("b", n, KC, RV), both, RV)
                for jp in range(2):
                    ps = open_tile(pe, ("S", h, jp))
                    for j in range(2):
                        for c in range(2):
                            at = (2 * jp + j) * P
                            i = mm(ps[:, j * T:(j + 1) * T], rkT[:, 2 * h + c, at:at + P], rqT[:, 2 * h + c, :],
                                   start=(c == 0), stop=(c == 1))
                    filled(i, ("S", h, jp))
                n = UB["rg", h]
                by_rows([("rg", h, t) for t in range(TC)], "b", n, part("b", n, KC, RV), [(latT, t) for t in range(TC)], RV)
                pe.wait_ge(S("rv_ready"), 4 * (h + 1))
                pe.wait_ge(S("ret_weights"), 2 * (h + 1))
                for t in range(TC):
                    ps = open_tile(pe, ("ro", h, t))
                    for j in range(4):
                        i = mm(ps[:, :], dec2[:, j, t * P:(t + 1) * P], rv[h % 2][:, j, :], start=(j == 0), stop=(j == 3))
                    filled(i, ("ro", h, t))

            for u in range(2):
                n = UB["gr", u]
                by_rows([("gr", u, t) for t in range(TC)], "b", n, part("b", n, KC, 512), [(latT, t) for t in range(TC)], 512)
            n = UB["cq"]
            by_rows([("cq", t) for t in range(TC)], "b", n, part("b", n, KC, QR), [(latT, t) for t in range(TC)], QR)
            n = UB["ck"]
            by_rows([("ck", j) for j in range(4)], "b", n, part("b", n, KC, CKR), both, CKR)
            for u in range(2):
                n = UB["gm", u]
                by_rows([("gm", u, t) for t in range(TC)], "b", n, part("b", n, KC, 512), [(latT, t) for t in range(TC)], 512)

            pe.wait_ge(S("cqn_ready"), 2)
            for name, cs in ((("cqT", 0), (0, 1)), (("cqT", 1), (2,))):
                ps = open_tile(pe, name)
                for c in cs:
                    for t in range(TC):
                        i = tp(ps[:, (c % 2) * T + t * P:(c % 2) * T + (t + 1) * P], cqn[:, t, c * P:(c + 1) * P], ident)
                filled(i, name)
            pe.wait_ge(S("ckn_ready"), 4)
            for c in range(2):
                ps = open_tile(pe, ("ckT", c))
                for j in range(4):
                    i = tp(ps[:, j * P:(j + 1) * P], ckn[:, j, c * P:(c + 1) * P], ident)
                filled(i, ("ckT", c))
            ps = open_tile(pe, "krT")
            pe.wait_ge(S("kr_ready"), 4)
            for j in range(4):
                i = tp(ps[:, j * P:(j + 1) * P], kr2[:, j, :], ident)
            filled(i, "krT")
            pe.wait_ge(S("ret_ready"), RH)
            transposes("retT", ret, 8)
            pe.wait_ge(S("retT_ready"), 8)
            down_proj("br", "b", UB["br", 0], 4, retT)

            pe.wait_ge(S("cqnT_ready"), 3)
            for u in range(2):
                n = UB["uq", u]
                w = part("b", n, 3, 768)
                landed("b", n)
                for hp in range(2):
                    name = ("qn", 2 * u + hp)
                    ps = open_tile(pe, name)
                    for j in range(2):
                        f = (2 * hp + j) * (NOPE + ROPE)
                        for k in range(3):
                            i = mm(ps[:, j * T:(j + 1) * T], w[:, k, f:f + NOPE], cqnT[:, k, :], start=(k == 0), stop=(k == 2))
                    filled(i, name)
                for t in range(TC):
                    name = ("qr", u, t)
                    ps = open_tile(pe, name)
                    for k in range(3):
                        heads = w[:, k, :].rearrange("p (h f) -> p h f", h=4)[:, :, NOPE:]
                        i = mm(ps[:, 0:256].rearrange("p (h f) -> p h f", h=4), cqnT[:, k, t * P:(t + 1) * P], heads,
                               start=(k == 0), stop=(k == 2))
                    filled(i, name)
                multiplied("b", n, ("qr", u, 1))
            pe.wait_ge(S("cknT_ready"), 2)
            n = UB["ukv"]
            w = part("b", n, 2, 2048)
            landed("b", n)
            for h in range(MH):
                ps = open_tile(pe, ("kn", h))
                for k in range(2):
                    f = h * (NOPE + MV)
                    i = mm(ps[:, :], w[:, k, f:f + NOPE], cknT[:, k, :], start=(k == 0), stop=(k == 1))
                filled(i, ("kn", h))
            for j in range(4):
                for g in range(2):
                    ps = open_tile(pe, ("mv", j, g))
                    for k in range(2):
                        heads = w[:, k, :].rearrange("p (h f) -> p h f", h=MH)[:, 4 * g:4 * g + 4, NOPE:]
                        i = mm(ps[:, :].rearrange("p (h f) -> p h f", h=4), cknT[:, k, j * P:(j + 1) * P], heads,
                               start=(k == 0), stop=(k == 1))
                    filled(i, ("mv", j, g))
            multiplied("b", n, ("mv", 3, 1))
            pe.wait_ge(S("qr_ready"), 4)
            for pp in range(2):
                ps = open_tile(pe, ("qrT", pp))
                for m in range(2):
                    for t in range(TC):
                        c = (2 * pp + m) * P
                        i = tp(ps[:, m * T + t * P:m * T + (t + 1) * P], qr_rows[:, t, c:c + P], ident)
                filled(i, ("qrT", pp))

            pe.wait_ge(S("qnT_ready"), 4)
            pe.wait_ge(S("knT_ready"), MH)
            pe.wait_ge(S("qrT_ready"), 2)
            pe.wait_ge(*stage("krT_ready"))
            pe.wait_ge(S("mv_ready"), 8)

            def mla_logits(p):
                hp, t = p // TC, p % TC
                ps = [open_tile(pe, ("s", 2 * p + e)) for e in range(2)]
                for e in range(2):
                    mm(ps[e][:, :], qnT[:, 2 * hp + e, t * P:(t + 1) * P], knT[:, 2 * hp + e, :], start=True, stop=False)
                for e in range(2):
                    half = slice(e * ROPE, (e + 1) * ROPE)
                    filled(mm(ps[e][:, :], qrT[half, hp, t * P:(t + 1) * P], krT[half, :], start=False, stop=True),
                           ("s", 2 * p + e))

            def mla_turn(j):
                pe.wait_ge(S("mla_probs"), j + 1)
                ps = open_tile(pe, ("mpT", j))
                for c in range(4):
                    i = tp(ps[:, c * P:(c + 1) * P], mp[:, j % 2, c * P:(c + 1) * P], ident)
                filled(i, ("mpT", j))

            def mla_values(hp):
                pe.wait_ge(S("mpT_ready"), 2 * TC * (hp + 1))
                for e in range(2):
                    h = 2 * hp + e
                    ps = open_tile(pe, ("mo", h))
                    for c in range(4):
                        i = mm(ps[:, 0:T], mv[c // 2][:, c % 2, h * MV:(h + 1) * MV], mpT[e][:, c, :], start=(c == 0),
                               stop=(c == 3))
                    filled(i, ("mo", h))

            PAIRS = MH // 2 * TC
            mla_logits(0)
            for p in range(PAIRS):
                if p + 1 < PAIRS:
                    mla_logits(p + 1)
                mla_turn(2 * p)
                if p and p % TC == 0:
                    mla_values(p // TC - 1)
                mla_turn(2 * p + 1)
            mla_values(PAIRS // TC - 1)
            pe.wait_ge(S("mT_ready"), MH)
            down_proj("bm", "b", UB["bm", 0], 2, mT)

            pe.wait_ge(*stage("diag_ready"))
            for j in range(4):
                ps = open_tile(pe, ("bc", j))
                for k in range(4):
                    i = mm(ps[:, k * P:(k + 1) * P], ones, diag[:, 4 * j + k, :], start=True, stop=True)
                filled(i, ("bc", j))

            pe.wait_ge(S("merged_ready"), 4)
            transposes("mgT", merged, 4)
            pe.wait_ge(S("mgT_ready"), 4)
            down_proj("yo", "b", UB["wo", 0], 2, mergedT)
            pe.wait_ge(*stage("n2_ready"))
            transposes("nT", n2_rows, 4)
            router("m2", h2T, "h2T_ready", 8, rw2)
            block_table("m2")
            moe("m2", n2_rows)

        @block.sync
        def _(sp):
            def stream(phase, units, free):
                for n, (src, k, f) in enumerate(units):
                    if n >= SLOTS:
                        sp.wait_ge(*unit_done[phase, n - SLOTS])
                    elif free:
                        sp.wait_ge(*free[n])
                    sp.dma_start(part(phase, n, k, f), src).then_inc(S(f"{phase}_full{n % SLOTS}"), 16)
                    if phase == "a" and n == 1:
                        sp.dma_start(cst[:, P:], consts[:, P:]).then_inc(S("ld_const"), 16)

            def experts(m, before_, units):
                E, NB = MOE[m]
                for j, src in enumerate(moe_units(m, 0)):
                    sp.wait_ge(*unit_done[before_, len(units) - SLOTS + j])
                    sp.dma_start(part(m, j, 4, 1024), src).then_inc(S(f"{m}_full{j}"), 16)
                sp.wait_ge(*stage(f"{m}_table"))
                n = sp.value_load(table[0:1, NB2:NB2 + 1], min_val=1, max_val=NB - 1)
                with sp.Fori(1, n) as i:
                    e = sp.value_load(table[0:1, bass.ds(i, 1)], min_val=0, max_val=E - 1)
                    for j, src in enumerate(moe_units(m, e)):
                        sp.wait_ge(S(f"{m}_free{j}"), i + 1)
                        sp.dma_start(part(m, j, 4, 1024), src).then_inc(S(f"{m}_full{j}"), 16)
                return [(S(f"{m}_free{j}"), n + 1) for j in range(SLOTS)]

            sp.dma_start(cst[:, 0:P], consts[:, 0:P]).then_inc(S("ld_ident"), 16)
            sp.dma_start(x_rows, a["x"][0].rearrange("(t p) d -> p t d", p=P)).then_inc(S("ld_x"), 16)
            stream("a", units_a, None)
            stream("b", units_b, experts("m1", "a", units_a))
            experts("m2", "b", units_b)
            for t in range(TC):
                sp.wait_ge(*stage(("out_half", "out_ready")[t]))
                sp.dma_start(out[0, t * P:(t + 1) * P, :], y_acc["m2"][:, t, :]).then_inc(S("stored"), 16)
            sp.wait_ge(S("stored"), 16 * TC)

        @block.gpsimd
        def _(pool_eng):
            def load(dst, src, sem):
                pool_eng.dma_start(dst, src).then_inc(S(sem), 16)

            def spread(ap, n):
                return ap.partition_broadcast(n)

            roots = [0]

            def inverse_roots(*widths):
                for n in widths:
                    roots[0] += 1
                    pool_eng.wait_ge(S("root_asked"), roots[0])
                    nc.gpsimd.tensor_tensor(root[:, 0:n], root[:, 0:n], power[:, 0:n], ALU.pow).then_inc(S("root_given"), 1)

            nc.gpsimd.memset(power[:, :], -0.5).then_inc(S("root_set"), 1)
            pool_eng.wait_ge(S("root_set"), 1)
            nc.gpsimd.memset(root[:, :], 1.0).then_inc(S("root_set"), 1)
            pool_eng.wait_ge(S("root_set"), 2)
            nc.gpsimd.memset(silc, 0.0).then_inc(S("root_set"), 1)
            pool_eng.wait_ge(S("root_set"), 3)
            nc.gpsimd.memset(rel33[32:33, :], 1.0).then_inc(S("root_set"), 1)
            pool_eng.wait_ge(S("root_set"), 4)
            nc.gpsimd.memset(rw1[:, :], 0.0).then_inc(S("root_set"), 1)
            pool_eng.wait_ge(S("root_set"), 5)
            load(rel33[0:32, :], a["rel_bias"], "ld_rel")
            rows = {"g_sb": a["g_sb"][0], "g_dil": a["g_dil"][0], "n1g": a["norm1_g_2"][0], "n2g": a["norm2_g_2"][0],
                    "qng": a["mla_q_norm_g_2"][0], "kvg": a["mla_kv_norm_g_2"][0], "c": a["c_2"][0],
                    "cctx": a["c_ctx_2"], "ada_b": a["ada_b_2"][0]}
            for name, v in rows.items():
                lo, hi = VEC[name]
                load(vrows[lo:hi, :], v.rearrange("(k p) -> k p", p=P), "ld_vec")
            load(rw1[:, :].rearrange("p (k e) -> p k e", k=KC)[:, :, 0:E1], a["w_router"].rearrange("(k p) e -> p k e", p=P), "ld_router")
            load(rw2[:, :].rearrange("p (k e) -> p k e", k=KC), a["router_w_2"][0].rearrange("(k p) e -> p k e", p=P),
                 "ld_router")
            load(rb1[:, :], spread(a["b_router"], P), "ld_router")
            load(rb2[:, :], spread(a["router_b_2"][0], P), "ld_router")
            load(decay[:, 0:RH], spread(a["ret_decay_fwd_2"][0], P), "ld_router")
            load(decay[:, RH:2 * RH], spread(a["ret_decay_bwd_2"][0], P), "ld_router")
            pool_eng.wait_ge(*stage("bias_rows_ready"))
            load(bias_rows, bias8[0:HEADS, :], "bias_stored")
            pool_eng.wait_ge(S("bias_stored"), 16)
            shifted = bass.AP(bias_rows.tensor, 0, [[1, P], [384, HEADS], [1, 256]])
            load(hankel, shifted, "ld_hankel")
            tile(pool_eng, ("sb_o", 1))
            load(ln1[:, 0, :], spread(a["ln1_g"][0], P), "ld_ln")
            load(ln1[:, 1, :], spread(a["ln1_b"][0], P), "ld_ln")
            load(ln2[:, 0, :], spread(a["ln2_g"][0], P), "ld_ln")
            load(ln2[:, 1, :], spread(a["ln2_b"][0], P), "ld_ln")
            inverse_roots(2 * HEADS)
            tile(pool_eng, ("L", HEADS - 1))
            load(ctx_rows, a["ctx_2"][0].rearrange("(t p) d -> p t d", p=P), "ld_ctx")
            inverse_roots(2 * HEADS)
            inverse_roots(*([TC] * (4 + RH + 1) + [2 * TC]))
            pool_eng.wait_ge(S("mT_ready"), MH)
            load(bgu_rows, a["exp_b_gu_2"][0], "ld_moe_bias")
            load(bdn_rows, a["exp_b_down_2"][0], "ld_moe_bias")
            pool_eng.wait_ge(S("bc_ready"), 4)
            load(fng, spread(a["final_norm_g_2"], P), "ld_fng")
            inverse_roots(TC, TC)

        @block.scalar
        def _(act):
            af = nc.scalar.activation
            chain = [0]

            def link(ins):
                chain[0] += 1
                ins.then_inc(S("act_chain"), 1)
                act.wait_ge(S("act_chain"), chain[0])

            def evac(dst, name, view, sem, scale=1.0, func=ACT.Copy):
                ps = tile(act, name)
                freed(af(dst, view(ps), func, scale=scale), name)
                act.wait_ge(S(f"bank_free{tiles[name][0]}"), tiles[name][1] + 1)
                act.nop().then_inc(S(sem), 1)

            def pairs(dst, cp):
                return dst[:, 2 * cp:2 * cp + 2, :]

            def two(ps):
                return ps[:, :].rearrange("p (c t) -> p c t", c=2)

            for cp in range(4):
                evac(pairs(xT, cp), ("xT", cp), two, "xT_ready")
            for kind, dst in (("q_sb", qk_sb[0]), ("k_sb", qk_sb[1]), ("q_dl", qk_dl[0]), ("k_dl", qk_dl[1])):
                if kind == "q_dl":
                    act.wait_ge(*stage("vec_ready"))
                    act.wait_ge(S("root_set"), 3)
                    lo = VEC["c"][0]
                    af(silc[:, :, 0:2].rearrange("p k v -> p v k"), vecT[:, lo:lo + 2 * KC].rearrange("p (v k) -> p v k", v=2),
                       ACT.Silu).then_inc(stage("silc_ready")[0], 1)
                for mp_ in range(2):
                    evac(pairs(dst, mp_), (kind, mp_), two, "qk_ready", HD ** -0.5 if kind[0] == "q" else 1.0)

            def sb_log(p):
                zm, e = sb_work[:, p % 2, 0, :], sb_work[:, p % 2, 1, :]
                act.wait_ge(S("sb_masked"), p + 1)
                if p >= 2:
                    act.wait_ge(S("sb_softplus"), p - 1)
                link(af(e, zm, ACT.Abs))
                link(af(e, e, ACT.Exp, scale=-1.0))
                af(e, e, ACT.Ln, bias=1.0).then_inc(S("sb_log"), 1)

            def sb_exp(p):
                act.wait_ge(S("sb_exponent"), p + 1)
                if p >= 2:
                    act.wait_ge(S("sb_values_done"), p - 1)
                af(sb_work[:, p % 2, 3, :], sb_work[:, p % 2, 0, :], ACT.Exp).then_inc(S("sb_weights"), 1)

            def ada_out(q):
                evac(ada_rows[:, 512 * q:512 * (q + 1)], ("ada", q), lambda ps: ps[:, :], "ada_rows")

            sb_log(0)
            for p in range(4):
                if p < 3:
                    sb_log(p + 1)
                if p % 2:
                    ada_out(p // 2)
                sb_exp(p)

            den = stat[:, 0:16].rearrange("p (h t) -> p h t", t=2)
            nmx = stat[:, 16:32].rearrange("p (h t) -> p h t", t=2)
            for h in range(HEADS):
                if h == 4:
                    ada_out(2)
                ps = tile(act, ("L", h))
                act.wait_ge(S("dl_max"), h + 1)
                if h >= 2:
                    act.wait_ge(S("dl_pT_ready"), h - 1)
                if h == 0:
                    tile(act, ("sb_o", 1))
                af(dl_p[:, h % 2, 0:256], ps[:, 0:256], ACT.Exp, bias=nmx[:, h, 0:1],
                   accum_out=den[:, h, 0:1]).then_inc(S("dl_exp"), 1)
                af(dl_p[:, h % 2, 256:384], ps[:, 256:384], ACT.Exp, bias=nmx[:, h, 1:2],
                   accum_out=den[:, h, 1:2]).then_inc(S("dl_exp"), 1)
                act.wait_ge(S("dl_exp"), 2 * h + 2)
                freed(act.nop(), ("L", h))

            ss = stat[:, 32:36]
            act.wait_ge(S("ld_ctx"), 16)
            for t in range(TC):
                i = af(B(2, 1024, 1024 * t), ctx_rows[:, t, :], ACT.Square, accum_out=ss[:, t:t + 1])
            i.then_inc(stage("ctx_ss")[0], 1)

            act.wait_ge(*stage("mod_ready"))
            for cp in range(4):
                ps = tile(act, ("cT", cp))
                for c in range(2):
                    k = 2 * cp + c
                    i = af(ctxT[:, k, :], ps[:, c * T:(c + 1) * T], ACT.Identity, scale=sc1[:, 2 * k + 1:2 * k + 2],
                           bias=mod[:, 2 * k + 1:2 * k + 2])
                    i.then_inc(S("ctxT_ready"), 1)
                act.wait_ge(S("ctxT_ready"), 2 * cp + 2)
                freed(act.nop(), ("cT", cp))

            for cp in range(4):
                evac(pairs(xT, cp), ("x1T", cp), two, "x1T_ready")

            def gates_exp(m):
                evac(lgT, (m, "lgT"), lambda ps: ps[:, 0:T], "route_out")
                act.wait_ge(*stage(f"{m}_shifted"))
                L = rt_logits(m)
                af(L, L, ACT.Exp).then_inc(stage(f"{m}_exp")[0], 1)

            def moe(m):
                _, G, _, DN, _, _, _, _ = banks
                act.wait_ge(*stage(f"{m}_table"))
                n = act.value_load(table[0:1, NB2:NB2 + 1], min_val=1, max_val=MOE[m][1] - 1)
                with act.Fori(0, n) as i:
                    if m == "m1":
                        act.wait_ge(S(f"{m}_free1"), i + 2)
                        act.wait_ge(S(f"{m}_hid"), i + 1)
                        af(act_g, G[:, :], ACT.Silu).then_inc(S(f"{m}_act"), 1)
                    else:
                        act.wait_ge(S(f"{m}_gate"), i + 1)
                        act.wait_ge(S(f"{m}_hid"), i + 1)
                        af(act_g, gate_1, ACT.Sigmoid, scale=SWIGLU).then_inc(S(f"{m}_act"), 1)
                    act.wait_ge(S(f"{m}_free5"), i + 2)
                    act.wait_ge(S(f"{m}_scattered"), 4 * i + 4)
                    act.activation(y_slot, DN[:, :], ACT.Copy).then_inc(S(f"{m}_y_slot"), 1)

            gates_exp("m1")
            moe("m1")

            act.wait_ge(*stage("x2_ready"))
            for t in range(TC):
                i = af(B(3, 1024, 1024 * t), x_rows[:, t, :], ACT.Square, accum_out=ss[:, 2 + t:3 + t])
            i.then_inc(stage("x2_ss")[0], 1)

            act.wait_ge(S("ld_router"), 16 * 6)
            link(af(lg[:, 8:16], decay[:, :], ACT.Abs))
            link(af(lg[:, 8:16], lg[:, 8:16], ACT.Exp, scale=-1.0))
            af(lg[:, 8:16], lg[:, 8:16], ACT.Ln, bias=1.0).then_inc(stage("decay_log")[0], 1)

            def ret_decay(h):
                if h:
                    act.wait_ge(S("ret_out"), 2 * h)
                else:
                    act.wait_ge(*stage("lag_ready"))
                    act.wait_ge(S("rqT_ready"), 4)
                for j in range(2):
                    u = P * (1 - j)
                    span = slice(u, u + T)
                    lag = C("lag")[:, span]
                    af(dec[:, j, :], lag, ACT.Exp, scale=lg[:, h:h + 1], bias=lg[:, 16 + h:17 + h])
                    af(dec2[:, j, :], lag, ACT.Exp, scale=lg[:, 28 + h:29 + h], bias=lg[:, 20 + h:21 + h])
                    af(dec[:, 2 + j, :], lagf[:, span], ACT.Exp, scale=lg[:, h:h + 1])
                    i = af(dec2[:, 2 + j, :], lagb[:, span], ACT.Exp, scale=lg[:, 4 + h:5 + h])
                i.then_inc(S("ret_decays"), 1)

            for u in range(2):
                for mp_ in range(2):
                    evac(rkT[:, 4 * u + 2 * mp_:4 * u + 2 * mp_ + 2, 0:T], (("kc", u), mp_), two, "rkT_ready", RQK ** -0.5)
            for cp in range(4):
                evac(rkT[:, 2 * cp:2 * cp + 2, T:2 * T], ("rkT", cp), two, "rkT_ready", RQK ** -0.5)
            for cp in range(4):
                evac(pairs(rqT, cp), ("rqT", cp), two, "rqT_ready")
            ret_decay(0)
            rss = stat[:, 36:44]
            for h in range(RH):
                for j in range(4):
                    if h >= 2 and j == 0:
                        act.wait_ge(S("ret_out"), 2 * (h - 1))
                    evac(rv[h % 2][:, j, :], ("rv", h, j), lambda ps: ps[:, :], "rv_ready")
                for t in range(TC):
                    evac(ret[:, t, h * RV:(h + 1) * RV], ("rg", h, t), lambda ps: ps[:, :], "ret_gate", func=ACT.Silu)
                for t in range(TC):
                    ps = tile(act, ("ro", h, t))
                    af(junk[:, :], ps[:, :], ACT.Square, accum_out=rss[:, 2 * h + t:2 * h + t + 1]).then_inc(S("ret_ss"), 1)
                    act.wait_ge(S("ret_ss"), 2 * h + t + 1)
                if h + 1 < RH:
                    ret_decay(h + 1)
            for u in range(2):
                for t in range(TC):
                    evac(sig_gr[:, t, u * 512:(u + 1) * 512], ("gr", u, t), lambda ps: ps[:, :], "sig_gr_ready", func=ACT.Sigmoid)

            mss = stat[:, 44:50]
            for t in range(TC):
                ps = tile(act, ("cq", t))
                af(junk[:, 0:QR], ps[:, 0:QR], ACT.Square, accum_out=mss[:, t:t + 1]).then_inc(S("mla_ss"), 1)
                act.wait_ge(S("mla_ss"), t + 1)
            for j in range(4):
                ps = tile(act, ("ck", j))
                af(junk[:, 0:KVR], ps[:, 0:KVR], ACT.Square, accum_out=mss[:, 2 + j:3 + j]).then_inc(S("mla_ss"), 1)
                act.wait_ge(S("mla_ss"), TC + j + 1)
            tile(act, ("gm", 1, 1))
            for u in range(2):
                for t in range(TC):
                    evac(sig_gm[:, t, u * 512:(u + 1) * 512], ("gm", u, t), lambda ps: ps[:, :], "sig_gm_ready", func=ACT.Sigmoid)
            for cp in range(8):
                evac(pairs(retT, cp), ("retT", cp), two, "retT_ready")
            for hp in range(4):
                evac(pairs(qnT, hp), ("qn", hp), two, "qnT_ready")
            for h in range(MH):
                evac(knT[:, h, :], ("kn", h), lambda ps: ps[:, :], "knT_ready")
            for pp in range(2):
                evac(pairs(qrT, pp), ("qrT", pp), two, "qrT_ready")

            mden, mnm = stat[:, 50:66], stat[:, 66:82]
            scale = (NOPE + ROPE) ** -0.5

            def mla_exp(j):
                ps = tile(act, ("s", j))
                act.wait_ge(S("mla_max"), j + 1)
                freed(af(mp[:, j % 2, :], ps[:, :], ACT.Exp, scale=scale, bias=mnm[:, j:j + 1],
                         accum_out=mden[:, j:j + 1]), ("s", j))
                act.wait_ge(S(f"bank_free{tiles['s', j][0]}"), tiles["s", j][1] + 1)
                act.nop().then_inc(S("mla_exp"), 1)

            def mla_turned(j):
                p, e = j // 2, j % 2
                hp, t = p // TC, p % TC
                if t == 0 and hp:
                    h = 2 * hp - 2 + e
                    evac(mT[:, h, :], ("mo", h), lambda ps: ps[:, 0:T], "mT_ready")
                evac(mpT[e][:, :, t * P:(t + 1) * P], ("mpT", j), lambda ps: ps[:, :].rearrange("p (c q) -> p c q", c=4),
                     "mpT_ready")

            for j in range(2 * MH):
                if j >= 2:
                    tile(act, ("mpT", j - 2))
                mla_exp(j)
                if j >= 2:
                    mla_turned(j - 2)
            for j in range(2 * MH - 2, 2 * MH):
                mla_turned(j)
            for h in range(MH - 2, MH):
                evac(mT[:, h, :], ("mo", h), lambda ps: ps[:, 0:T], "mT_ready")
            for j in range(4):
                evac(gate_bc[:, j // 2, (j % 2) * 512:(j % 2) * 512 + 512], ("bc", j), lambda ps: ps[:, :], "bc_ready")
            for cp in range(4):
                evac(pairs(mergedT, cp), ("mgT", cp), two, "mgT_ready")
            for t in range(TC):
                act.wait_ge(*stage(("x3_half", "x3_ready")[t]))
                i = af(B(3, 1024, 1024 * t), x_rows[:, t, :], ACT.Square, accum_out=stat[:, 82 + t:83 + t])
            i.then_inc(stage("x3_ss")[0], 1)
            gates_exp("m2")
            for t in range(TC):
                for f in range(2):
                    evac(y_acc["m2"][:, t, f * 512:(f + 1) * 512], ("m2", "bdown", t, f), lambda ps: ps[:, :], "route_out")
            moe("m2")
            for t in range(TC):
                act.wait_ge(*stage(("x4_half", "x4_ready")[t]))
                i = af(B(3, 1024, 1024 * t), y_acc["m2"][:, t, :], ACT.Square, accum_out=stat[:, 84 + t:85 + t])
            i.then_inc(stage("x4_ss")[0], 1)

        @block.vector
        def _(dve):
            v = nc.vector
            tt, ts, stt = v.tensor_tensor, v.tensor_scalar, v.scalar_tensor_tensor
            chain = [0]
            chain_root = [0]
            marks = {}

            def link(ins):
                chain[0] += 1
                ins.then_inc(S("dve_chain"), 1)
                dve.wait_ge(S("dve_chain"), chain[0])

            def mark(ins, name):
                marks[name] = marks.get(name, 0) + 1
                sem, value = stage(name) if name in DVE_STAGES else (S(name), marks[name])
                ins.then_inc(sem, 1)
                dve.wait_ge(sem, value)

            def rsqrt(x, scale, eps, meanwhile=None):
                chain_root[0] += 1
                r = root[:, 0:x.shape[1]]
                ts(r, x, scale, eps, ALU.mult, ALU.add).then_inc(S("root_asked"), 1)
                if meanwhile:
                    meanwhile()
                dve.wait_ge(S("root_given"), chain_root[0])
                link(v.tensor_copy(x, r))

            def bcast(x, n):
                return x.unsqueeze(2).to_broadcast([x.shape[0], x.shape[1], n])

            def two(ps):
                return ps[:, :].rearrange("p (c t) -> p c t", c=2)

            def sb_mask(p):
                for j in range(2):
                    h = 2 * p + j
                    ps = tile(dve, ("z", h))
                    link(tt(sb_work[:, p % 2, 0, j * 384:(j + 1) * 384], ps[:, 0:384], C("sb_mask"), ALU.add))
                    freed(dve.nop(), ("z", h))
                dve.nop().then_inc(S("sb_masked"), 1)

            for kind, dst in (("v_sb", v_sb), ("v_dl", v_dl)):
                if kind == "v_dl":
                    ps = tile(dve, "vec")
                    link(v.tensor_copy(vecT[:, :], ps[:, 0:NVEC]))
                    freed(dve.nop(), "vec")
                    dve.nop().then_inc(stage("vec_ready")[0], 1)
                    ps = tile(dve, "rel")
                    link(v.tensor_copy(bias8[0:HEADS, :], ps[0:HEADS, 0:384]))
                    freed(dve.nop(), "rel")
                    dve.nop().then_inc(stage("bias_rows_ready")[0], 1)
                    sb_mask(0)
                for t in range(TC):
                    ps = tile(dve, (kind, t))
                    link(v.tensor_copy(dst[:, t, :], ps[:, :]))
                    freed(dve.nop(), (kind, t))
                    dve.nop().then_inc(S("v_ready"), 1)

            def sb_softplus(p):
                dve.wait_ge(S("sb_log"), p + 1)
                w = sb_work[:, p % 2]
                stt(w[:, 2, :], w[:, 0, :], 0.0, w[:, 1, :], ALU.max, ALU.add).then_inc(S("sb_softplus"), 1)

            def sb_exponent(p):
                for j in range(2):
                    h = 2 * p + j
                    ps = tile(dve, ("R", h))
                    z = sb_work[:, p % 2, 0, j * 384:(j + 1) * 384]
                    link(tt(z, z, ps[:, 0:384], ALU.subtract))
                    freed(dve.nop(), ("R", h))
                dve.nop().then_inc(S("sb_exponent"), 1)

            for p in range(4):
                if p < 3:
                    if p >= 1:
                        dve.wait_ge(S("sb_weights"), p)
                    sb_mask(p + 1)
                sb_softplus(p)
                sb_exponent(p)

            nmx = stat[:, 16:32].rearrange("p (h t) -> p h t", t=2)
            den = stat[:, 0:16].rearrange("p (h t) -> p h t", t=2)

            def dl_max(h):
                ps = tile(dve, ("L", h))
                v.tensor_reduce(nmx[:, h, 0:1], ps[:, 0:256], AX_X, ALU.max, negate=True)
                v.tensor_reduce(nmx[:, h, 1:2], ps[:, 256:384], AX_X, ALU.max, negate=True).then_inc(S("dl_max"), 1)

            def dl_copy(h):
                ps = tile(dve, ("pT", h))
                if h >= 2:
                    dve.wait_ge(S("dl_values_done"), h - 1)
                link(v.tensor_copy(dl_pT[:, h % 2, :], ps[:, 0:384]))
                freed(dve.nop(), ("pT", h))
                dve.nop().then_inc(S("dl_pT_ready"), 1)

            for t in range(TC):
                ps = tile(dve, ("sb_o", t))
                link(v.tensor_copy(y_rows[:, t, 0:512], ps[:, :]))
                freed(dve.nop(), ("sb_o", t))
            heads = B(6).rearrange("p (t w h c) -> p t w h c", t=TC, w=2, c=HD)
            sq = B(7).rearrange("p (t w h c) -> p t w h c", t=TC, w=2, c=HD)
            sums = [stat[:, at:at + 2 * HEADS] for at in (50, 16)]

            def head_squares(w):
                link(tt(sq[:, :, w], heads[:, :, w], heads[:, :, w], ALU.mult))
                link(v.tensor_reduce(sums[w].rearrange("p (t h) -> p t h", t=TC), sq[:, :, w], AX_X, ALU.add))

            def head_norm(w, sem):
                for t in range(TC):
                    i = tt(heads[:, t, w], heads[:, t, w], bcast(sums[w][:, HEADS * t:HEADS * (t + 1)], HD), ALU.mult)
                    if t == 0:
                        link(i)
                mark(i, sem)

            def stick_breaking_norm():
                head_squares(0)
                rsqrt(sums[0], 1.0 / HD, RMS_EPS)
                head_norm(0, "y_sb_ready")

            dve.wait_ge(S("root_set"), 2)
            for h in range(HEADS + 1):
                if h < HEADS:
                    dl_max(h)
                if h > 0:
                    dl_copy(h - 1)
                if h == 3:
                    stick_breaking_norm()
            dve.wait_ge(S("dl_exp"), 2 * HEADS)
            link(v.reciprocal(stat[:, 0:16], stat[:, 0:16]))
            for t in range(TC):
                ps = tile(dve, ("dl_o", t))
                link(tt(y_rows[:, t, 512:1024].rearrange("p (h c) -> p h c", h=HEADS),
                        ps[:, :].rearrange("p (h c) -> p h c", h=HEADS), bcast(den[:, :, 1 - t], HD), ALU.mult))
                freed(dve.nop(), ("dl_o", t))

            def conditioning():
                b0 = VEC["ada_b"][0]
                m3 = mod[:, :].rearrange("p (c w) -> p c w", w=2)
                for q in range(3):
                    ps = tile(dve, ("adaT", q))
                    got = ps[:, :].rearrange("p (c g v) -> p g c v", c=4, g=4)
                    bias = vecT[:, b0 + 16 * q:b0 + 16 * (q + 1)].rearrange("p (g c) -> p g c", g=4)
                    for w in range(2):
                        to = m3[:, 16 * q:16 * (q + 1), w].rearrange("p (g c) -> p g c", g=4)
                        link(tt(to, got[:, :, :, w], bias, ALU.add))
                    freed(dve.nop(), ("adaT", q))
                n1, n2 = VEC["n1g"], VEC["n2g"]
                link(stt(sc1[:, :].rearrange("p (c w) -> p c w", w=2), m3[:, 8:16, :], 1.0, bcast(vecT[:, n1[0]:n1[1]], 2),
                         ALU.add, ALU.mult))
                mark(stt(sc2[:, :], m3[:, 32:40, 0], 1.0, vecT[:, n2[0]:n2[1]], ALU.add, ALU.mult), "mod_ready")

            g0 = VEC["g_sb"][0]

            def heads_in_columns(*cps):
                for cp in cps:
                    ps = tile(dve, ("yT", cp))
                    for c in range(2):
                        k = 2 * cp + c
                        mark(ts(yT[:, k, :], ps[:, c * T:(c + 1) * T], vecT[:, g0 + k:g0 + k + 1], None, ALU.mult),
                             "yT_ready")
                    freed(dve.nop(), ("yT", cp))

            def meanwhile():
                conditioning()
                heads_in_columns(0, 1)

            head_squares(1)
            rsqrt(sums[1], 1.0 / HD, RMS_EPS, meanwhile)
            m3 = mod[:, :].rearrange("p (c w) -> p c w", w=2)
            head_norm(1, "y_ready")
            heads_in_columns(2, 3)

            ss = stat[:, 32:36]
            dve.wait_ge(*stage("ctx_ss"))
            rsqrt(ss[:, 0:2], 1.0 / D, RMS_EPS)
            for t in range(TC):
                link(ts(ctx_rows[:, t, :], ctx_rows[:, t, :], ss[:, t:t + 1], None, ALU.mult))
            mark(dve.nop(), "ctxn_ready")

            def layer_norm(rows, gb, sem):
                st = stat[:, 96:108]
                mean_var = stat[:, 88:88 + 2 * TC].rearrange("p (t w) -> p t w", w=2)
                for t in range(TC):
                    for f in range(2):
                        link(v.bn_stats(st[:, 6 * f:6 * f + 6], rows[:, t, f * 512:(f + 1) * 512]))
                    link(v.bn_aggr(mean_var[:, t, :], st))
                rsqrt(mean_var[:, :, 1], 1.0, LN_EPS)
                for t in range(TC):
                    link(stt(rows[:, t, :], rows[:, t, :], mean_var[:, t, 0:1], gb[:, 0, :], ALU.subtract, ALU.mult))
                    link(stt(rows[:, t, :], rows[:, t, :], mean_var[:, t, 1:2], gb[:, 1, :], ALU.mult, ALU.add))
                mark(dve.nop(), sem)

            for t in range(TC):
                for f in range(2):
                    ps = tile(dve, ("wo1", t, f))
                    xs = x_rows[:, t, f * 512:(f + 1) * 512]
                    link(stt(xs, xs, ALPHA, ps[:, :], ALU.mult, ALU.add))
                    freed(dve.nop(), ("wo1", t, f))
            dve.wait_ge(S("ld_ln"), 64)
            layer_norm(x_rows, ln1, "x1_ready")

            def ranks(dst, vals, groups, n, cmp):
                big = cmp[:, 0:groups * n * n].rearrange("p (g i j) -> p g i j", g=groups, i=n)
                tie = cmp[:, groups * n * n:groups * n * n + n * n].rearrange("p (i j) -> p i j", i=n)
                eq = cmp[:, 1024 + n * n:1024 + n * n + groups * n * n].rearrange("p (g i j) -> p g i j", g=groups, i=n)
                row = C("iota")[:, 0:n]
                vj = vals.unsqueeze(2).to_broadcast([P, groups, n, n])
                vi = vals.unsqueeze(3).to_broadcast([P, groups, n, n])
                link(tt(tie, row.unsqueeze(1).to_broadcast([P, n, n]), bcast(row, n), ALU.is_lt))
                link(tt(eq, vj, vi, ALU.is_equal))
                link(tt(eq, eq, tie.unsqueeze(1).to_broadcast([P, groups, n, n]), ALU.mult))
                link(tt(big, vj, vi, ALU.is_gt))
                link(tt(big, big, eq, ALU.add))
                link(v.tensor_reduce(dst, big, AX_X, ALU.add))

            def largest(sel3, L3, n, scratch):
                E = L3.shape[2]
                left, hit = (scratch[:, i * TC * E:(i + 1) * TC * E].rearrange("p (t e) -> p t e", t=TC) for i in range(2))
                order = scratch[:, 2 * TC * E:2 * TC * E + E]
                top = stat[:, 0:TC]
                link(v.tensor_copy(left, L3))
                link(ts(order, C("iota")[:, 0:E], -1.0, float(E), ALU.mult, ALU.add))
                for r in range(n):
                    link(v.tensor_reduce(top, left, AX_X, ALU.max))
                    link(tt(hit, left, bcast(top, E), ALU.is_equal))
                    link(tt(hit, hit, order.unsqueeze(1).to_broadcast([P, TC, E]), ALU.mult))
                    link(v.tensor_reduce(top, hit, AX_X, ALU.max))
                    to = hit if r else sel3
                    link(tt(to, hit, bcast(top, E), ALU.is_equal))
                    if r:
                        link(tt(sel3, sel3, hit, ALU.add))
                    if r + 1 < n:
                        link(stt(left, to, -3e38, left, ALU.mult, ALU.add))

            def choose(m, bias, scratch):
                E, NB = MOE[m]
                sel, gate = route_parts(m)[:2]
                sel3, gate3 = (w.rearrange("p (t e) -> p t e", t=TC) for w in (sel, gate))
                L = rt_logits(m)
                L3 = L.rearrange("p (t e) -> p t e", t=TC)
                mx = stat[:, 86:88]
                ps = tile(dve, (m, "logits"))
                link(tt(L3, ps[:, 0:TC * E].rearrange("p (t e) -> p t e", t=TC),
                        bias.unsqueeze(1).to_broadcast([P, TC, E]), ALU.add))
                freed(dve.nop(), (m, "logits"))
                if m == "m2":
                    largest(sel3, L3, TOP2, scratch)
                link(v.tensor_reduce(mx, L3, AX_X, ALU.max))
                tt(L3, L3, bcast(mx, E), ALU.subtract).then_inc(stage(f"{m}_shifted")[0], 1)
                dve.wait_ge(*stage(f"{m}_exp"))
                if m == "m1":
                    link(v.tensor_reduce(mx, L3, AX_X, ALU.add))
                    link(v.reciprocal(mx, mx))
                    link(tt(L3, L3, bcast(mx, E), ALU.mult))
                    G = E // GRP
                    Lg = L.rearrange("p (g e) -> p g e", e=GRP)
                    sg = sel.rearrange("p (g e) -> p g e", e=GRP)
                    gs = stat[:, 0:TC * G]
                    gr = stat[:, 8:8 + TC * G]
                    ranks(sg, Lg, TC * G, GRP, scratch)
                    link(ts(sel, sel, float(TOP1), None, ALU.is_lt))
                    link(tt(gate, L, sel, ALU.mult))
                    link(v.tensor_reduce(gs, gate.rearrange("p (g e) -> p g e", e=GRP), AX_X, ALU.add))
                    ranks(gr.rearrange("p (t g) -> p t g", t=TC), gs.rearrange("p (t g) -> p t g", t=TC), TC, G, scratch)
                    link(ts(gr, gr, 1.0, None, ALU.is_lt))
                    link(tt(sg, sg, bcast(gr, GRP), ALU.mult))
                link(tt(gate, L, sel, ALU.mult))
                link(v.tensor_reduce(mx, gate3, AX_X, ALU.add))
                link(v.reciprocal(mx, mx))
                mark(tt(gate3, gate3, bcast(mx, E), ALU.mult), f"{m}_chosen")

            def block_table(m):
                E, NB = MOE[m]
                sel, gate, posm, nb, selT, gateT, bsel, rnd = route_parts(m)
                ps = tile(dve, (m, "pos"))
                link(stt(posm, sel, 1e6, ps[:, 0:2 * E], ALU.mult, ALU.add))
                freed(dve.nop(), (m, "pos"))
                link(ts(posm, posm, -1e6, None, ALU.add))
                ps = tile(dve, (m, "count"))
                cnt, first, last = (stat[0:E, 90 + i:91 + i] for i in range(3))
                link(v.tensor_copy(cnt, ps[0:E, 0:1]))
                freed(dve.nop(), (m, "count"))
                link(ts(nb, C("pidx", E), 0.0, None, ALU.is_equal))
                link(stt(nb, cnt, 0.0, nb, ALU.is_gt, ALU.max))
                for r in range(1, T // CAP):
                    link(stt(nb, cnt, float(CAP * r), nb, ALU.is_gt, ALU.add))
                mark(dve.nop(), f"{m}_placed")
                ps = tile(dve, (m, "turned"))
                link(v.tensor_copy(selT, ps[0:E, 0:T]))
                link(v.tensor_copy(gateT, ps[0:E, T:2 * T]))
                freed(dve.nop(), (m, "turned"))
                ps = tile(dve, (m, "start"))
                link(v.tensor_copy(first, ps[0:E, 0:1]))
                freed(dve.nop(), (m, "start"))
                link(tt(last, first, nb, ALU.add))
                row = C("iota", E)[:, 0:NB]
                link(ts(rnd, row, first, None, ALU.is_ge))
                link(stt(bsel, row, last, rnd, ALU.is_lt, ALU.mult))
                link(ts(rnd, row, first, -float(CAP), ALU.subtract, ALU.mult))
                mark(tt(rnd, rnd, bsel, ALU.mult), f"{m}_laid")
                for name, dst in (("posb", posb), ("gateb", gateb)):
                    ps = tile(dve, (m, name))
                    link(v.tensor_copy(dst[:, 0:TC * NB], ps[:, 0:TC * NB]))
                    freed(dve.nop(), (m, name))
                ps = tile(dve, (m, "blocks"))
                link(v.tensor_copy(table[0:1, NB2:NB2 + 1], ps[0:1, 0:1]))
                freed(dve.nop(), (m, "blocks"))
                ps = tile(dve, (m, "experts"))
                link(v.tensor_copy(table[0:1, 0:NB], ps[0:1, 0:NB]))
                freed(dve.nop(), (m, "experts"))
                mark(dve.nop(), f"{m}_table")

            def moe(m):
                E, NB = MOE[m]
                XG, G, U, _, Y0, Y1, PT, HT = banks
                n = dve.value_load(table[0:1, NB2:NB2 + 1], min_val=1, max_val=NB - 1)
                pos3 = posb[:, 0:TC * NB].rearrange("p (t b) -> p t b", t=TC)
                gat3 = gateb[:, 0:TC * NB].rearrange("p (t b) -> p t b", t=TC)
                row = C("iota")[:, 0:CAP]

                def picks(i):
                    for t in range(TC):
                        ins = ts(pick[:, t, :], row, pos3[:, t, bass.ds(i, 1)], None, ALU.is_equal)
                    ins.then_inc(S(f"{m}_pick"), 1)

                def gathered():
                    xg = XG[:, :].rearrange("p (k s) -> p k s", k=KC)
                    if m == "m1":
                        v.tensor_copy(xgT, xg).then_inc(S(f"{m}_xgT"), 1)
                    else:
                        tt(xgT, xg, bcast(sc2[:, :], CAP), ALU.mult).then_inc(S("m2_scaled"), 1)

                def shifted():
                    if m == "m2":
                        tt(xgT, xgT, bcast(m3[:, 24:32, 0], CAP), ALU.add).then_inc(S(f"{m}_xgT"), 1)

                def expert(i):
                    bsel = route_parts(m)[6]
                    v.tensor_copy(this_expert, bsel[:, bass.ds(i, 1)].to_broadcast([E2, CAP])).then_inc(S("m2_expert"), 1)

                def add(before_, q):
                    dve.wait_ge(S(f"{m}_scattered"), before_ + q + 1)
                    t, f = q // 2, q % 2
                    ys = y_acc[m][:, t, f * 512:(f + 1) * 512]
                    tt(ys, ys, (Y0, Y1)[f][:, :], ALU.add).then_inc(S(f"{m}_added"), 1)

                v.memset(put, 0.0).then_inc(S(f"{m}_put"), 1)
                v.memset(y_slot, 0.0).then_inc(S(f"{m}_y_slot"), 1)
                dve.nop().then_inc(S(f"{m}_added"), 1)
                dve.nop().then_inc(S(f"{m}_added"), 1)
                dve.nop().then_inc(S(f"{m}_hid"), 1)
                picks(0)
                if m == "m2":
                    expert(0)
                dve.wait_ge(S(f"{m}_gathered"), 1)
                gathered()
                if m == "m2":
                    dve.wait_ge(S("m2_scaled"), 1)
                    shifted()
                    dve.wait_ge(S("route_out"), 2 + 2 * TC)
                with dve.Fori(0, n) as i:
                    dve.wait_ge(S(f"{m}_gathered"), i + 1)
                    picks(i + 1)
                    dve.wait_ge(S(f"{m}_put_ps"), i + 1)
                    for t in range(TC):
                        ins = ts(pick_g[:, t, :, :], row.unsqueeze(1).to_broadcast([P, 2, CAP]), pos3[:, t, bass.ds(i, 1)],
                                 gat3[:, t, bass.ds(i, 1)], ALU.is_equal, ALU.mult)
                    ins.then_inc(S(f"{m}_pick_g"), 1)
                    if m == "m2":
                        dve.wait_ge(S("m2_biased"), i + 1)
                        expert(i + 1)
                    for q in range(4):
                        add(4 * i, q)
                    if m == "m1":
                        dve.wait_ge(S(f"{m}_act"), i + 1)
                        dve.wait_ge(S(f"{m}_free3"), i + 2)
                        tt(hid, act_g, U[:, :], ALU.mult).then_inc(S(f"{m}_hid"), 1)
                    else:
                        dve.wait_ge(S(f"{m}_free1"), i + 2)
                        ts(gate_1, G[:, :], LIMIT, None, ALU.min).then_inc(S(f"{m}_gate"), 1)
                        dve.wait_ge(S(f"{m}_act"), i + 1)
                        tt(gate_1, gate_1, act_g, ALU.mult).then_inc(S("m2_halves"), 1)
                        dve.wait_ge(S(f"{m}_free3"), i + 2)
                        ts(up_1, U[:, :], LIMIT, -LIMIT, ALU.min, ALU.max).then_inc(S("m2_halves"), 1)
                        dve.wait_ge(S("m2_halves"), 2 * i + 2)
                        stt(hid, up_1, 1.0, gate_1, ALU.add, ALU.mult).then_inc(S(f"{m}_hid"), 1)
                    dve.wait_ge(S(f"{m}_gathered"), i + 2)
                    gathered()
                    dve.wait_ge(S(f"{m}_turned"), i + 1)
                    v.tensor_copy(hidT, HT[:, :]).then_inc(S(f"{m}_hidT"), 1)
                    if m == "m2":
                        dve.wait_ge(S("m2_scaled"), i + 2)
                        shifted()
                    dve.wait_ge(S(f"{m}_put_ps"), i + 2)
                    v.tensor_copy(put, PT[:, 0:T]).then_inc(S(f"{m}_put"), 1)
                for q in range(4):
                    add(4 * n, q)
                dve.wait_ge(S(f"{m}_added"), 4 * n + 6)
                mark(dve.nop(), f"{m}_sum")

            choose("m1", rb1[:, :], pool[:, 7 * BUF:9 * BUF])
            block_table("m1")
            link(ts(y_sum["m1"], B(0), ALPHA, None, ALU.mult))
            moe("m1")

            link(v.tensor_copy(B(0), y_sum["m1"]))
            layer_norm(x_rows, ln2, "x2_ready")
            dve.wait_ge(*stage("x2_ss"))
            rsqrt(ss[:, 2:4], 1.0 / D, RMS_EPS)
            for t in range(TC):
                link(ts(xn_rows[:, t, :], x_rows[:, t, :], ss[:, 2 + t:3 + t], None, ALU.mult))
            mark(dve.nop(), "xn_ready")
            for cp in range(4):
                ps = tile(dve, ("lT", cp))
                for c in range(2):
                    k = 2 * cp + c
                    mark(ts(latT[:, k, :], ps[:, c * T:(c + 1) * T], sc1[:, 2 * k:2 * k + 1], mod[:, 2 * k:2 * k + 1],
                            ALU.mult, ALU.add), "latT_ready")
                freed(dve.nop(), ("lT", cp))

            dve.wait_ge(*stage("decay_log"))
            link(stt(lg[:, 0:8], decay[:, :], 0.0, lg[:, 8:16], ALU.min, ALU.subtract))
            link(ts(lg[:, 16:24], lg[:, 0:8], float(T), None, ALU.mult))
            link(ts(lg[:, 24:32], lg[:, 0:8], -1.0, None, ALU.mult))
            link(ts(lagf[:, :], C("lag"), 0.0, None, ALU.max))
            link(ts(lagb[:, :], C("lag"), -1.0, 0.0, ALU.mult, ALU.max))
            mark(dve.nop(), "lag_ready")

            def rope(dst, z, heads, f, cos, sin, tmp):
                w = 4 * f
                d4, z4, t4 = (x.rearrange("p (a t f) -> p a t f", t=2, f=f) for x in (dst, z, tmp))
                link(tt(dst.rearrange("p (h w) -> p h w", w=w), z.rearrange("p (h w) -> p h w", w=w),
                        cos.unsqueeze(1).to_broadcast([P, heads, w]), ALU.mult))
                for h in range(heads):
                    link(tt(t4[:, 2 * h:2 * h + 2, 0, :], z4[:, 2 * h:2 * h + 2, 1, :], sin, ALU.mult))
                    link(tt(t4[:, 2 * h:2 * h + 2, 1, :], z4[:, 2 * h:2 * h + 2, 0, :], sin, ALU.mult))
                link(tt(d4[:, :, 0, :], d4[:, :, 0, :], t4[:, :, 0, :], ALU.subtract))
                link(tt(d4[:, :, 1, :], d4[:, :, 1, :], t4[:, :, 1, :], ALU.add))

            rcos = C("rcos").rearrange("p (t w) -> p t w", t=TC)
            rsin = C("rsin").rearrange("p (t h f) -> p t h f", t=TC, h=2)
            for kind, dst in (("rk", rk_rows), ("rq", rq_rows)):
                for u in range(2):
                    for t in range(TC):
                        ps = tile(dve, (kind, u, t))
                        rope(dst[:, t, u * 512:(u + 1) * 512], ps[:, :], 2, 64, rcos[:, t, :], rsin[:, t], rope_tmp)
                        freed(dve.nop(), (kind, u, t))
                        mark(dve.nop(), "rotated")

            rss = stat[:, 36:44]
            for h in range(RH):
                dve.wait_ge(S("ret_decays"), h + 1)
                link(tt(dec[:, 0:2, :], dec[:, 0:2, :], dec2[:, 0:2, :], ALU.add))
                link(tt(dec[:, 2:4, :], dec[:, 2:4, :], dec2[:, 2:4, :], ALU.mult))
                for jp in range(2):
                    ps = tile(dve, ("S", h, jp))
                    mark(tt(dec2[:, 2 * jp:2 * jp + 2, :], two(ps), dec[:, 2 * jp:2 * jp + 2, :], ALU.mult), "ret_weights")
                    freed(dve.nop(), ("S", h, jp))
                dve.wait_ge(S("ret_ss"), 2 * h + 2)
                rsqrt(rss[:, 2 * h:2 * h + 2], 1.0 / RV, RMS_EPS)
                dve.wait_ge(S("ret_gate"), 2 * h + 2)
                for t in range(TC):
                    ps = tile(dve, ("ro", h, t))
                    r = ret[:, t, h * RV:(h + 1) * RV]
                    mark(stt(r, ps[:, :], rss[:, 2 * h + t:2 * h + t + 1], r, ALU.mult, ALU.mult), "ret_out")
                    freed(dve.nop(), ("ro", h, t))
                mark(dve.nop(), "ret_ready")

            mss = stat[:, 44:50]
            mcos = C("mcos").rearrange("p (t w) -> p t w", t=TC)
            msin = C("msin").rearrange("p (t h f) -> p t h f", t=TC, h=2)
            dve.wait_ge(S("mla_ss"), 6)
            rsqrt(mss[:, 0:2], 1.0 / QR, RMS_EPS)
            rsqrt(mss[:, 2:6], 1.0 / KVR, RMS_EPS)
            for t in range(TC):
                ps = tile(dve, ("cq", t))
                mark(ts(cqn[:, t, :], ps[:, 0:QR], mss[:, t:t + 1], None, ALU.mult), "cqn_ready")
                freed(dve.nop(), ("cq", t))
            for j in range(4):
                ps = tile(dve, ("ck", j))
                mark(ts(ckn[:, j, :], ps[:, 0:KVR], mss[:, 2 + j:3 + j], None, ALU.mult), "ckn_ready")
                if j < TC:
                    link(v.tensor_copy(kr2[:, j, 0:ROPE], ps[:, KVR:CKR]))
                else:
                    rope(kr2[:, j, 0:ROPE], ps[:, KVR:CKR], 1, 16, mcos[:, j - TC, :], msin[:, j - TC], mrope_tmp[:, 0:ROPE])
                freed(dve.nop(), ("ck", j))
                mark(v.tensor_copy(kr2[:, j, ROPE:2 * ROPE], kr2[:, j, 0:ROPE]), "kr_ready")

            q0, k0 = VEC["qng"][0], VEC["kvg"][0]
            for c in range(3):
                name = ("cqT", c // 2)
                ps = tile(dve, name)
                mark(ts(cqnT[:, c, :], ps[:, (c % 2) * T:(c % 2 + 1) * T], vecT[:, q0 + c:q0 + c + 1], None, ALU.mult),
                     "cqnT_ready")
                if c:
                    freed(dve.nop(), name)
            for c in range(2):
                ps = tile(dve, ("ckT", c))
                mark(ts(cknT[:, c, :], ps[:, :], vecT[:, k0 + c:k0 + c + 1], None, ALU.mult), "cknT_ready")
                freed(dve.nop(), ("ckT", c))
            ps = tile(dve, "krT")
            mark(v.tensor_copy(krT[:, :], ps[:, :]), "krT_ready")
            freed(dve.nop(), "krT")
            dve.wait_ge(S("sig_gr_ready"), 4)
            for t in range(TC):
                for f in range(2):
                    ps = tile(dve, ("br", t, f))
                    c = slice(f * 512, (f + 1) * 512)
                    link(tt(merged[:, t, c], ps[:, :], sig_gr[:, t, c], ALU.mult))
                    freed(dve.nop(), ("br", t, f))

            for u in range(2):
                for t in range(TC):
                    ps = tile(dve, ("qr", u, t))
                    rope(qr_rows[:, t, u * 256:(u + 1) * 256], ps[:, 0:256], 4, 16, mcos[:, t, :], msin[:, t], mrope_tmp)
                    freed(dve.nop(), ("qr", u, t))
                    mark(dve.nop(), "qr_ready")
            for j in range(4):
                for g in range(2):
                    ps = tile(dve, ("mv", j, g))
                    mark(v.tensor_copy(mv[j // 2][:, j % 2, g * 512:(g + 1) * 512], ps[:, :]), "mv_ready")
                    freed(dve.nop(), ("mv", j, g))

            mden, mnm = stat[:, 50:66], stat[:, 66:82]
            scale = (NOPE + ROPE) ** -0.5

            def mla_max(j):
                ps = tile(dve, ("s", j))
                link(v.tensor_reduce(mnm[:, j:j + 1], ps[:, :], AX_X, ALU.max))
                mark(ts(mnm[:, j:j + 1], mnm[:, j:j + 1], -scale, None, ALU.mult), "mla_max")

            mla_max(0)
            mla_max(1)
            for p in range(MH // 2 * TC):
                for j in (2 * p, 2 * p + 1):
                    dve.wait_ge(S("mla_exp"), j + 1)
                    link(v.reciprocal(mden[:, j:j + 1], mden[:, j:j + 1]))
                    mark(ts(mp[:, j % 2, :], mp[:, j % 2, :], mden[:, j:j + 1], None, ALU.mult), "mla_probs")
                if p + 1 < MH // 2 * TC:
                    mla_max(2 * p + 2)
                    mla_max(2 * p + 3)

            tile(dve, ("mo", MH - 1))
            for w, c0 in enumerate((16, 40)):
                i = tt(diag[:, 8 * w:8 * w + 8, :], ident.unsqueeze(1).to_broadcast([P, 8, P]), bcast(m3[:, c0:c0 + 8, 0], P),
                       ALU.mult)
                link(i)
            mark(dve.nop(), "diag_ready")

            dve.wait_ge(S("sig_gm_ready"), 4)
            for t in range(TC):
                for f in range(2):
                    ps = tile(dve, ("bm", t, f))
                    c = slice(f * 512, (f + 1) * 512)
                    link(tt(sig_gm[:, t, c], ps[:, :], sig_gm[:, t, c], ALU.mult))
                    freed(dve.nop(), ("bm", t, f))
                    mark(tt(merged[:, t, c], merged[:, t, c], sig_gm[:, t, c], ALU.add), "merged_ready")

            dve.wait_ge(S("bc_ready"), 4)
            for t in range(TC):
                for f in range(2):
                    ps = tile(dve, ("yo", t, f))
                    c = slice(f * 512, (f + 1) * 512)
                    link(tt(merged[:, t, c], ps[:, :], gate_bc[:, 0, c], ALU.mult))
                    freed(dve.nop(), ("yo", t, f))
                    link(tt(x_rows[:, t, c], x_rows[:, t, c], merged[:, t, c], ALU.add))
                mark(dve.nop(), ("x3_half", "x3_ready")[t])
            dve.wait_ge(*stage("x3_ss"))
            rsqrt(stat[:, 82:84], 1.0 / D, RMS_EPS)
            for t in range(TC):
                link(ts(n2_rows[:, t, :], x_rows[:, t, :], stat[:, 82 + t:83 + t], None, ALU.mult))
            mark(dve.nop(), "n2_ready")
            for cp in range(4):
                ps = tile(dve, ("nT", cp))
                for c in range(2):
                    k = 2 * cp + c
                    mark(ts(h2T[:, k, :], ps[:, c * T:(c + 1) * T], sc2[:, k:k + 1], mod[:, 48 + 2 * k:49 + 2 * k],
                            ALU.mult, ALU.add), "h2T_ready")
                freed(dve.nop(), ("nT", cp))
            choose("m2", rb2[:, :], pool[:, 2 * BUF:5 * BUF])
            block_table("m2")
            moe("m2")

            for t in range(TC):
                y = y_acc["m2"][:, t, :]
                link(tt(y, y, gate_bc[:, 1, :], ALU.mult))
                mark(tt(y, y, x_rows[:, t, :], ALU.add), ("x4_half", "x4_ready")[t])
            dve.wait_ge(*stage("x4_ss"))
            rsqrt(stat[:, 84:86], 1.0 / D, RMS_EPS)
            dve.wait_ge(S("ld_fng"), 16)
            for t in range(TC):
                y = y_acc["m2"][:, t, :]
                mark(stt(y, y, stat[:, 84 + t:85 + t], fng, ALU.mult, ALU.mult), ("out_half", "out_ready")[t])


_NAMES = ("x w_in g_sb g_dil w_out ln1_g ln1_b ln2_g ln2_b rel_bias w_router b_router w_gate w_up w_down c_2 ctx_2 c_ctx_2 "
          "norm1_g_2 norm2_g_2 ada_w_2 ada_b_2 w_in_2 ret_decay_fwd_2 ret_decay_bwd_2 mla_q_norm_g_2 mla_w_uq_2 "
          "mla_kv_norm_g_2 mla_w_ukv_2 w_branch_ret_2 w_branch_mla_2 w_out_2 router_w_2 router_b_2 exp_w_gu_2 exp_b_gu_2 "
          "exp_w_down_2 exp_b_down_2 final_norm_g_2").split()


def kernel(**inputs):
    import concourse.bacc as bacc
    from concourse.bass_utils import run_bass_kernel_spmd

    nc = bacc.Bacc("TRN2", target_bir_lowering=False, num_devices=1)
    arrays, aps = {}, {}
    for name in _NAMES:
        arrays["in_" + name] = v = np.ascontiguousarray(inputs[name])
        aps[name] = nc.dram_tensor("in_" + name, v.shape, F32, kind="ExternalInput").ap()
    arrays["shape_constants"] = CONSTS
    consts = nc.dram_tensor("shape_constants", CONSTS.shape, F32, kind="ExternalInput").ap()
    bias_rows = nc.dram_tensor("bias_rows", [HEADS, 384], F32, kind="Internal").ap()
    out = nc.dram_tensor("out", [1, T, D], F32, kind="ExternalOutput").ap()
    two_block_kernel(nc, aps, consts, bias_rows, out)
    got = run_bass_kernel_spmd(nc, [arrays], core_ids=[0])
    return got.results[0]["out"]
```
